# Optimizing a Trainium2 kernel written in Bass

```python
import jax, jax.numpy as jnp
from jax import lax
import numpy as np

D_MODEL = 1024
BATCH = 1
SEQ = 512
DEPTH = 2

RG_WIDTH = 1024
RG_BLOCKS = 16
RG_BLOCK_DIM = RG_WIDTH // RG_BLOCKS
CONV_WIDTH = 4
RG_C = 8.0
SB_HEADS = 8
SB_HEAD_DIM = 64
SB_WIDTH = SB_HEADS * SB_HEAD_DIM
FOX_HEADS = 8
FOX_HEAD_DIM = 64
FOX_WIDTH = FOX_HEADS * FOX_HEAD_DIM
N_BRANCHES = 3
D_FF = 2816
Q_BLOCK = 128
N_SUBLAYERS = 3
EPS = 1e-6
IN_SIZES = (RG_WIDTH, RG_WIDTH, 3 * SB_WIDTH, 3 * FOX_WIDTH, FOX_HEADS, N_BRANCHES * D_MODEL)
N_IN = sum(IN_SIZES)

kernel_name = "hybrid_rglru_stickbreak_fox_macaron_adaln"

def _rmsnorm(x, gain):
    x32 = x.astype(jnp.float32)
    y = x32 * lax.rsqrt(jnp.mean(x32 * x32, axis=-1, keepdims=True) + EPS)
    return y.astype(x.dtype) * gain

def _modulate(h, shift, scale):
    return h * (1.0 + scale[:, None, :]) + shift[:, None, :]

def _swiglu(h, w1, w3, w2):
    return (jax.nn.silu(h @ w1) * (h @ w3)) @ w2

def _causal_depthwise_conv(x, w, b):
    y = lax.conv_general_dilated(
        x, w[:, None, :].astype(x.dtype), window_strides=(1,), padding=[(CONV_WIDTH - 1, 0)],
        dimension_numbers=('NWC', 'WIO', 'NWC'), feature_group_count=x.shape[-1])
    return y + b

def _block_diag(x, w, b):
    bsz, slen, _ = x.shape
    xb = x.reshape(bsz, slen, RG_BLOCKS, RG_BLOCK_DIM)
    return jnp.einsum('bsnd,nde->bsne', xb, w).reshape(bsz, slen, RG_WIDTH) + b

def _rg_lru(x, w_a, b_a, w_x, b_x, lam):
    x32 = x.astype(jnp.float32)
    r = jax.nn.sigmoid(_block_diag(x, w_a, b_a).astype(jnp.float32))
    i = jax.nn.sigmoid(_block_diag(x, w_x, b_x).astype(jnp.float32))
    log_a = -RG_C * r * jax.nn.softplus(-lam.astype(jnp.float32))
    a = jnp.exp(log_a)
    u = jnp.sqrt(-jnp.expm1(2.0 * log_a)) * (i * x32)

    def combine(left, right):
        a_l, b_l = left
        a_r, b_r = right
        return a_l * a_r, a_r * b_l + b_r

    _, h = lax.associative_scan(combine, (a, u), axis=1)
    return h.astype(x.dtype)

def _split_qkv(t, n_heads, head_dim):
    bsz, slen, _ = t.shape
    t = t.reshape(bsz, slen, 3, n_heads, head_dim).transpose(2, 0, 3, 1, 4)
    return t[0], t[1], t[2]

def _merge_heads(o):
    bsz, nh, slen, hd = o.shape
    return o.transpose(0, 2, 1, 3).reshape(bsz, slen, nh * hd)

def _stick_breaking_attention(q, k, v):
    slen, hd = q.shape[2], q.shape[3]
    scale = hd ** -0.5
    outs = []
    for blk in range(slen // Q_BLOCK):
        q0, q1 = blk * Q_BLOCK, (blk + 1) * Q_BLOCK
        z = jnp.einsum('bhqd,bhkd->bhqk', q[:, :, q0:q1], k[:, :, :q1],
                       preferred_element_type=jnp.float32) * scale
        t_idx = q0 + jnp.arange(Q_BLOCK)[:, None]
        s_idx = jnp.arange(q1)[None, :]
        strict = s_idx < t_idx
        log_keep = jnp.where(strict, jax.nn.log_sigmoid(-z), 0.0)
        suffix = lax.cumsum(log_keep, axis=3, reverse=True) - log_keep
        w = jnp.where(strict, jnp.exp(jax.nn.log_sigmoid(z) + suffix), 0.0)
        outs.append(jnp.einsum('bhqk,bhkd->bhqd', w.astype(v.dtype), v[:, :, :q1]))
    return jnp.concatenate(outs, axis=2)

def _forgetting_attention(q, k, v, log_f):
    slen, hd = q.shape[2], q.shape[3]
    scale = hd ** -0.5
    cum = lax.cumsum(log_f, axis=2)
    outs = []
    for blk in range(slen // Q_BLOCK):
        q0, q1 = blk * Q_BLOCK, (blk + 1) * Q_BLOCK
        z = jnp.einsum('bhqd,bhkd->bhqk', q[:, :, q0:q1], k[:, :, :q1],
                       preferred_element_type=jnp.float32) * scale
        z = z + cum[:, :, q0:q1, None] - cum[:, :, None, :q1]
        causal = jnp.arange(q1)[None, :] <= (q0 + jnp.arange(Q_BLOCK)[:, None])
        p = jax.nn.softmax(jnp.where(causal, z, -jnp.inf), axis=-1)
        outs.append(jnp.einsum('bhqk,bhkd->bhqd', p.astype(v.dtype), v[:, :, :q1]))
    return jnp.concatenate(outs, axis=2)

def _hybrid_mixer(h, w_in, conv_w, conv_b, rg_wa, rg_ba, rg_wx, rg_bx, rg_lam, fox_bf, merge_b,
                  w_rg, w_sb, w_fox, w_o):
    bsz, slen, _ = h.shape
    proj = h @ w_in
    cuts = np.cumsum(IN_SIZES)[:-1].tolist()
    rg_x, rg_gate, sb_qkv, fox_qkv, fox_f, merge = jnp.split(proj, cuts, axis=-1)
    xa = _causal_depthwise_conv(rg_x, conv_w, conv_b)
    ya = jax.nn.gelu(rg_gate) * _rg_lru(xa, rg_wa, rg_ba, rg_wx, rg_bx, rg_lam)
    q_b, k_b, v_b = _split_qkv(sb_qkv, SB_HEADS, SB_HEAD_DIM)
    yb = _merge_heads(_stick_breaking_attention(q_b, k_b, v_b))
    q_c, k_c, v_c = _split_qkv(fox_qkv, FOX_HEADS, FOX_HEAD_DIM)
    log_f = jax.nn.log_sigmoid((fox_f + fox_bf).astype(jnp.float32)).transpose(0, 2, 1)
    yc = _merge_heads(_forgetting_attention(q_c, k_c, v_c, log_f))
    g = jax.nn.sigmoid(merge + merge_b).reshape(bsz, slen, N_BRANCHES, D_MODEL)
    mixed = g[:, :, 0] * (ya @ w_rg) + g[:, :, 1] * (yb @ w_sb) + g[:, :, 2] * (yc @ w_fox)
    return mixed @ w_o

def setup_inputs(seed: int = 0) -> dict:
    key = jax.random.key(seed)
    ks = jax.random.split(key, 32)
    f32 = jnp.float32
    L, D = DEPTH, D_MODEL

    def nrm(k, shape, fan_in, mult=1.0):
        return jax.random.normal(k, shape, f32) * (mult * fan_in ** -0.5)

    def gain(k, shape):
        return 1.0 + 0.01 * jax.random.normal(k, shape, f32)

    def small(k, shape):
        return 0.01 * jax.random.normal(k, shape, f32)

    a_c = jax.random.uniform(ks[12], (L, RG_WIDTH), f32, 0.9, 0.999)
    a = a_c ** (1.0 / RG_C)
    rg_lam = jnp.log(a) - jnp.log1p(-a)
    return {
        "x": jax.random.normal(ks[0], (BATCH, SEQ, D), f32),
        "c": jax.random.normal(ks[1], (BATCH, D), f32),
        "ffn1_norm": gain(ks[2], (L, D)),
        "ffn1_w1": nrm(ks[3], (L, D, D_FF), D),
        "ffn1_w3": nrm(ks[4], (L, D, D_FF), D),
        "ffn1_w2": nrm(ks[5], (L, D_FF, D), D_FF),
        "mix_norm": gain(ks[6], (L, D)),
        "w_in": nrm(ks[7], (L, D, N_IN), D),
        "conv_w": nrm(ks[8], (L, CONV_WIDTH, RG_WIDTH), CONV_WIDTH),
        "conv_b": small(ks[9], (L, RG_WIDTH)),
        "rg_wa": nrm(ks[10], (L, RG_BLOCKS, RG_BLOCK_DIM, RG_BLOCK_DIM), RG_BLOCK_DIM),
        "rg_ba": small(ks[11], (L, RG_WIDTH)),
        "rg_wx": nrm(ks[13], (L, RG_BLOCKS, RG_BLOCK_DIM, RG_BLOCK_DIM), RG_BLOCK_DIM),
        "rg_bx": small(ks[14], (L, RG_WIDTH)),
        "rg_lam": rg_lam,
        "fox_bf": jax.random.uniform(ks[15], (L, FOX_HEADS), f32, 2.0, 5.0),
        "merge_b": small(ks[16], (L, N_BRANCHES * D)),
        "w_rg": nrm(ks[17], (L, RG_WIDTH, D), RG_WIDTH),
        "w_sb": nrm(ks[18], (L, SB_WIDTH, D), SB_WIDTH),
        "w_fox": nrm(ks[19], (L, FOX_WIDTH, D), FOX_WIDTH),
        "w_o": nrm(ks[20], (L, D, D), D),
        "ffn2_norm": gain(ks[21], (L, D)),
        "ffn2_w1": nrm(ks[22], (L, D, D_FF), D),
        "ffn2_w3": nrm(ks[23], (L, D, D_FF), D),
        "ffn2_w2": nrm(ks[24], (L, D_FF, D), D_FF),
        "ada_w": nrm(ks[25], (L, D, N_SUBLAYERS * 3 * D), D, 0.1),
        "ada_b": small(ks[26], (L, N_SUBLAYERS * 3 * D)),
        "final_norm": gain(ks[27], (D,)),
        "final_ada_w": nrm(ks[28], (D, 2 * D), D, 0.1),
        "final_ada_b": small(ks[29], (2 * D,)),
    }

def reference(x, c, ffn1_norm, ffn1_w1, ffn1_w3, ffn1_w2, mix_norm, w_in, conv_w, conv_b,
              rg_wa, rg_ba, rg_wx, rg_bx, rg_lam, fox_bf, merge_b, w_rg, w_sb, w_fox, w_o,
              ffn2_norm, ffn2_w1, ffn2_w3, ffn2_w2, ada_w, ada_b, final_norm, final_ada_w,
              final_ada_b):
    bsz = x.shape[0]
    c_act = jax.nn.silu(c)
    for l in range(DEPTH):
        mod = (c_act @ ada_w[l] + ada_b[l]).reshape(bsz, N_SUBLAYERS, 3, D_MODEL)
        h = _modulate(_rmsnorm(x, ffn1_norm[l]), mod[:, 0, 0], mod[:, 0, 1])
        x = x + 0.5 * (1.0 + mod[:, 0, 2])[:, None, :] * _swiglu(h, ffn1_w1[l], ffn1_w3[l], ffn1_w2[l])
        h = _modulate(_rmsnorm(x, mix_norm[l]), mod[:, 1, 0], mod[:, 1, 1])
        y = _hybrid_mixer(h, w_in[l], conv_w[l], conv_b[l], rg_wa[l], rg_ba[l], rg_wx[l], rg_bx[l],
                          rg_lam[l], fox_bf[l], merge_b[l], w_rg[l], w_sb[l], w_fox[l], w_o[l])
        x = x + (1.0 + mod[:, 1, 2])[:, None, :] * y
        h = _modulate(_rmsnorm(x, ffn2_norm[l]), mod[:, 2, 0], mod[:, 2, 1])
        x = x + 0.5 * (1.0 + mod[:, 2, 2])[:, None, :] * _swiglu(h, ffn2_w1[l], ffn2_w3[l], ffn2_w2[l])
    fm = (c_act @ final_ada_w + final_ada_b).reshape(bsz, 2, D_MODEL)
    return _modulate(_rmsnorm(x, final_norm), fm[:, 0], fm[:, 1])


_drawn_inputs = setup_inputs


def setup_inputs(seed=0):
    import zlib

    import numpy as np

    out = dict(_drawn_inputs(seed))
    spreads = {}
    factors = {'ffn1_norm': 8.0,
     'mix_norm': 7.141,
     'rg_ba': 40.046,
     'rg_bx': 32.16,
     'merge_b': 25.251,
     'ffn2_norm': 27.759,
     'final_norm': 39.027,
     'final_ada_b': 4.052,
     'conv_b': 5.665}
    for name, (base, spread) in spreads.items():
        noise = np.random.default_rng([zlib.crc32(name.encode()), seed]).standard_normal(out[name].shape)
        drawn = base * np.exp(spread * noise) if base else spread * noise
        out[name] = __import__('jax').numpy.asarray(drawn.astype(out[name].dtype))
    for name, factor in factors.items():
        out[name] = (out[name] * factor).astype(out[name].dtype)
    return out
```

```python
from contextlib import ExitStack

import concourse.bass as bass
from concourse import mybir

F32 = mybir.dt.float32
F32R = mybir.dt.float32r
ALU = mybir.AluOpType
ACT = mybir.ActivationFunctionType
AX = mybir.AxisListType

P = 128
D = 1024
T = 512
DEPTH = 2
DFF = 2816
KD = D // P
KF = DFF // P
UB = 8
HEADS = 8
PAIRS = HEADS
HD = 64
TT = T // P
EPS = 1e-6
NEG = -(2.0 ** 100)

FFN_UNITS = 2 * KF + KF * KD // UB
U_FFN = (0, FFN_UNITS + 88)
U_RG = FFN_UNITS
U_QKV = U_RG + 2 * KD
U_MERGE = U_QKV + 3 * PAIRS
U_WO = U_MERGE + 5 * KD
UNITS = 2 * FFN_UNITS + 88
AHEAD = 3
RAW, RING = 2, 4
assert UNITS % RING == 0 and U_WO + KD == U_FFN[1]

V_NORM1, V_NORM2, V_NORM3 = 0, 8, 16
V_ADAB = 24
V_CONVW = 96
V_CONVB, V_BA, V_BX, V_LAM = 128, 136, 144, 152
V_MERGEB = 160
V_FOXB = 184
NV = 185

SB_AT = [(0, 0), (1, 0), (2, 0), (1, 384)]
FX_AT = [(1, 384), (2, 0), (1, 0), (0, 0)]
CHUNK = [(0, 512), (512, 512), (1024, 256)]
NS = 1280


INSIDE = [n for n in range(KD) if (n + 1) * KF % UB]
TILE_ENDS = len(INSIDE)


class Signal:

    def __init__(self, sem, per_layer, before=0):
        self.sem, self.per_layer, self.before = sem, per_layer, before

    def at(self, l, k):
        assert k + self.before > 0
        return l * self.per_layer + k + self.before


def trunk(nc, w_units, ada_w, vecs, wf, wab, c_rows, x_in, out):
    with ExitStack() as ctx:
        def sb(name, shape, dt=F32):
            return ctx.enter_context(nc.sbuf_tensor(name, shape, dt))

        def sig(name, per_layer=0, before=0):
            return Signal(ctx.enter_context(nc.semaphore(name)), per_layer, before)

        x = sb("x", [P, KD, T])
        h_hi = sb("h_hi", [P, KD, T], F32R)
        h_lo = sb("h_lo", [P, KD, T], F32R)
        raw = [sb(f"raw{i}", [P, UB, P]) for i in range(RAW)]
        w_hi = [sb(f"w_hi{i}", [P, UB, P], F32R) for i in range(RING)]
        w_lo = [sb(f"w_lo{i}", [P, UB, P], F32R) for i in range(RING)]
        c_act = sb("c_act", [P, D])
        vec = sb("vec", [P, NV])
        mod = sb("mod", [P, 72])
        nscale = sb("nscale", [P, 3, KD])
        gatec = sb("gatec", [P, KD])
        spc = sb("spc", [P, 6, KD])
        neg_sp = sb("neg_sp", [P, KD])
        pos_sp = sb("pos_sp", [P, KD])
        negmax = sb("negmax", [P, 2, TT])
        psums = sb("psums", [P, 2, TT])
        rsums = sb("rsums", [P, 2, TT])
        eps_col = sb("eps_col", [P, 1])
        one_col = sb("one_col", [P, 1])
        ident = sb("ident", [P, P])
        ident_r = sb("ident_r", [P, P], F32R)
        ones_r = sb("ones_r", [P, P], F32R)
        nones_r = sb("nones_r", [P, P], F32R)
        ntri_r = sb("ntri_r", [P, P], F32R)
        mask_sb = sb("mask_sb", [P, P], F32R)
        mask_fx = sb("mask_fx", [P, P], F32R)
        wf_raw = sb("wf_raw", [P, KD, HEADS])
        wf_hi = sb("wf_hi", [P, KD, HEADS], F32R)
        wf_lo = sb("wf_lo", [P, KD, HEADS], F32R)

        base = (nc.sbuf_base + 31) // 32 * 32
        ARENA = 110720
        sb("arena", [P, ARENA // 4])

        def at(name, offset, shape, dt=F32):
            size = 4
            for s in shape[1:]:
                size *= s
            assert offset + size <= ARENA, (name, offset + size)
            return nc.alloc_sbuf_tensor_at(name, shape, dt, offset=base + offset)

        g_hi = at("g_hi", 0, [P, KF, T], F32R)
        g_lo = at("g_lo", 45056, [P, KF, T], F32R)
        ada = [at(f"ada{i}", 90112 + 4096 * i, [P, D]) for i in range(2)]
        tmp = [at(f"tmp{i}", 98304 + 2048 * i, [P, T]) for i in range(4)]
        sq_hi = [at(f"sq_hi{i}", 102400 + 2048 * i, [P, T], F32R) for i in range(2)]
        sq_lo = [at(f"sq_lo{i}", 98304 + 2048 * i, [P, T], F32R) for i in range(2)]
        rstd = at("rstd", 106496, [P, T])
        ya_hi = at("ya_hi", 0, [P, KD, T], F32R)
        ya_lo = at("ya_lo", 16384, [P, KD, T], F32R)
        yb_hi = at("yb_hi", 32768, [P, KD, T], F32R)
        yb_lo = at("yb_lo", 49152, [P, KD, T], F32R)
        xa = [at(f"xa{i}", 32768 + 2048 * i, [P, T]) for i in range(2)]
        gel = [at(f"gel{i}", 36864 + 2048 * i, [P, T]) for i in range(2)]
        xa_hi = at("xa_hi", 40960, [P, T], F32R)
        xa_lo = at("xa_lo", 43008, [P, T], F32R)
        gr = at("gr", 45056, [P, T])
        gi = at("gi", 47104, [P, T])
        gt = at("gt", 49152, [P, T])
        wab_raw = at("wab_raw", 51200, [P, KD, 2, P])
        wab_hi = [at(f"wab_hi{i}", 59392 + 1024 * i, [P, 2, P], F32R) for i in range(2)]
        wab_lo = [at(f"wab_lo{i}", 61440 + 1024 * i, [P, 2, P], F32R) for i in range(2)]
        asq = at("asq", 63488, [P, T])
        xs = at("xs", 108544, [P, T + 4])
        q_hi = at("q_hi", 65536, [P, T], F32R)
        q_lo = at("q_lo", 67584, [P, T], F32R)
        k_hi = at("k_hi", 69632, [P, T], F32R)
        k_lo = at("k_lo", 71680, [P, T], F32R)
        v_hi = at("v_hi", 73728, [P, TT, 2 * P], F32R)
        v_lo = at("v_lo", 77824, [P, TT, 2 * P], F32R)
        e_f = [at(f"e_f{i}", 81920 + 10240 * i, [P, NS]) for i in range(2)]
        e_lo = [at(f"e_lo{i}", 81920 + 10240 * i, [P, NS], F32R) for i in range(2)]
        e_hi = [at(f"e_hi{i}", 87040 + 10240 * i, [P, NS], F32R) for i in range(2)]
        nc_hi = at("nc_hi", 102400, [HEADS, T], F32R)
        nc_lo = at("nc_lo", 104448, [HEADS, T], F32R)
        fx_a = at("fx_a", 98304, [HEADS, T])
        fx_b = at("fx_b", 100352, [HEADS, T])
        fx_c = at("fx_c", 106496, [HEADS, T])
        vt = at("vt", 108544, [P, T])
        mx_hi = at("mx_hi", 65536, [P, KD, T], F32R)
        mx_lo = at("mx_lo", 81920, [P, KD, T], F32R)
        sg = tmp[0:3]
        mx = tmp[3]

        bank = [ctx.enter_context(nc.psum_tensor(f"bank{i}", [P, T], F32)) for i in range(8)]
        BS = 6

        x_loaded = sig("x_loaded")
        c_loaded = sig("c_loaded")
        vec_loaded = sig("vec_loaded", 16, 16)
        wf_loaded = sig("wf_loaded", 16)
        wab_loaded = sig("wab_loaded", 16)
        raw_loaded = [sig(f"raw_loaded{i}", 16 * UNITS // RAW) for i in range(RAW)]
        ada_loaded = [sig(f"ada_loaded{i}", 16 * 36, 16 * 8) for i in range(2)]
        out_stored = [sig(f"out_stored{i}") for i in range(2)]
        consts = sig("consts")
        consts_v = sig("consts_v")
        silu_c = sig("silu_c")
        unit_hi = sig("unit_hi", UNITS)
        unit_lo = sig("unit_lo", UNITS)
        unit_done = sig("unit_done", UNITS)
        ada_done = sig("ada_done", 72, 16)
        mod_set = sig("mod_set", 3, 1)
        nscale_set = sig("nscale_set", 3, 1)
        gate_set = sig("gate_set", 3)
        x_ready = sig("x_ready", 24, 0)
        sq_ready = sig("sq_ready", 24, 8)
        sqh_ready = sig("sqh_ready", 24, 8)
        sql_ready = sig("sql_ready", 24, 8)
        sumsq = sig("sumsq", 24, 8)
        ln_ready = sig("ln_ready", 3, 1)
        rstd_ready = sig("rstd_ready", 3, 1)
        xr_ready = sig("xr_ready", 24, 0)
        hf_ready = sig("hf_ready", 24, 0)
        hh_ready = sig("hh_ready", 24, 0)
        hl_ready = sig("hl_ready", 24, 0)
        silu_ready = sig("silu_ready", 2 * KF)
        g_ready = sig("g_ready", 2 * KF)
        gh_ready = sig("gh_ready", 2 * KF)
        gl_ready = sig("gl_ready", 2 * KF)
        down_done = sig("down_done", 2 * TILE_ENDS)
        wfh = sig("wfh", 1)
        wfl = sig("wfl", 1)
        sp_step = sig("sp_step", 14)
        sp_exp = sig("sp_exp", 2)
        sp_set = sig("sp_set", 2)
        xs_zero = sig("xs_zero", 1)
        xs_ready = sig("xs_ready", KD)
        xa0_ready = sig("xa0_ready", KD)
        conv = sig("conv", 3 * KD)
        xah = sig("xah", KD)
        xal = sig("xal", KD)
        gelu_ready = sig("gelu_ready", KD)
        wabh = sig("wabh", KD)
        wabl = sig("wabl", KD)
        gates_done = sig("gates_done", KD)
        r_ready = sig("r_ready", KD)
        i_ready = sig("i_ready", KD)
        t_ready = sig("t_ready", KD)
        a_ready = sig("a_ready", KD)
        ix_ready = sig("ix_ready", KD)
        asq_ready = sig("asq_ready", KD)
        s_ready = sig("s_ready", KD)
        sqrt_ready = sig("sqrt_ready", KD)
        u_ready = sig("u_ready", KD)
        scan_ready = sig("scan_ready", KD)
        ya_ready = sig("ya_ready", KD)
        yah = sig("yah", KD)
        yal = sig("yal", KD)
        foxf_done = sig("foxf_done", 1)
        fx_step = sig("fx_step", 3)
        fx_act = sig("fx_act", 3)
        nch = sig("nch", 1)
        ncl = sig("ncl", 1)
        qh = sig("qh", PAIRS)
        ql = sig("ql", PAIRS)
        kh = sig("kh", PAIRS)
        kl = sig("kl", PAIRS)
        vt_ready = sig("vt_ready", PAIRS)
        vt_done = sig("vt_done", PAIRS)
        vh = sig("vh", PAIRS)
        vl = sig("vl", PAIRS)
        v_zero = sig("v_zero", 2)
        z_done = sig("z_done", 3 * 2 * PAIRS)
        abs_ready = sig("abs_ready", 3 * HEADS)
        exp_ready = sig("exp_ready", HEADS)
        lnp_ready = sig("lnp_ready", HEADS)
        sp_ready = sig("sp_ready", 3 * HEADS)
        sph = sig("sph", HEADS)
        spl = sig("spl", HEADS)
        suf_done = sig("suf_done", 3 * 2 * PAIRS)
        w_ready = sig("w_ready", 3 * HEADS)
        eh = sig("eh", HEADS)
        el = sig("el", HEADS)
        max_ready = sig("max_ready", TT * HEADS)
        p_ready = sig("p_ready", TT * HEADS)
        rs_ready = sig("rs_ready", HEADS)
        pn_ready = sig("pn_ready", TT * HEADS)
        ph = sig("ph", 3 * HEADS)
        pl = sig("pl", 3 * HEADS)
        pv_head = sig("pv_head", 2 * PAIRS)
        ybh = sig("ybh", PAIRS)
        ybl = sig("ybl", PAIRS)
        sg_ready = sig("sg_ready", 3 * KD)
        mx_step = sig("mx_step", 5 * KD)
        mxh = sig("mxh", KD)
        mxl = sig("mxl", KD)

        block = ctx.enter_context(nc.Block())

        @block.sync
        def _(sp):
            def load_unit(l, u, idx=None):
                sp.wait_ge(unit_lo.sem, unit_lo.at(l, u - RAW + 1))
                idx = l * UNITS + u if idx is None else idx
                sp.dma_start(raw[u % RAW][:, :, :], w_units[idx]).then_inc(raw_loaded[u % RAW].sem, 16)

            def load_ada(l, a):
                if a >= -14:
                    sp.wait_ge(ada_done.sem, ada_done.at(l, a - 1))
                sp.dma_start(ada[a % 2][:, :], ada_w[l * 72 + a + 16]).then_inc(ada_loaded[a % 2].sem, 16)

            sp.dma_start(c_act[:, :], c_rows).then_inc(c_loaded.sem, 16)
            sp.dma_start(vec[:, :], vecs[0]).then_inc(vec_loaded.sem, 16)
            for n in range(KD):
                sp.dma_start(x[:, n, :], x_in[n]).then_inc(x_loaded.sem, 16)
            for a in range(-16, 0):
                load_ada(0, a)
                if -16 + RAW > a:
                    sp.dma_start(raw[a + 16][:, :, :], w_units[a + 16]).then_inc(raw_loaded[a + 16].sem, 16)
            with sp.Fori(0, DEPTH) as l:
                for u in range(RAW, UNITS + RAW):
                    load_unit(l, u)
                    if u == 4:
                        sp.dma_start(wf_raw[:, :, :], wf[l]).then_inc(wf_loaded.sem, 16)
                    if 4 <= u < 48:
                        load_ada(l, u - 4)
                    for m in range(12):
                        if u == 49 + m * 4 // 3:
                            load_ada(l, 44 + m)
                    if u == U_RG + 4:
                        sp.wait_ge(unit_done.sem, unit_done.at(l, U_RG))
                        sp.dma_start(wab_raw[:, :, :, :], wab[l]).then_inc(wab_loaded.sem, 16)
                    if u == U_FFN[1] + 1:
                        sp.wait_ge(sg_ready.sem, sg_ready.at(l, 3 * KD))
                        sp.dma_start(vec[:, :], vecs[l + 1]).then_inc(vec_loaded.sem, 16)
                    if u == U_FFN[1] + 5:
                        sp.wait_ge(unit_done.sem, unit_done.at(l, U_WO + KD))
                    if U_FFN[1] + 6 <= u < U_FFN[1] + 22:
                        load_ada(l, 56 + u - U_FFN[1] - 6)
            for u in range(RAW, AHEAD):
                load_unit(DEPTH, u, u)
            for n in range(KD):
                sp.wait_ge(hf_ready.sem, 24 * DEPTH + n + 1)
                sp.dma_start(out[n], tmp[2 + n % 2][:, :]).then_inc(out_stored[n % 2].sem, 16)
            for s in out_stored:
                sp.wait_ge(s.sem, 16 * KD // 2)

        @block.gpsimd
        def _(gp):
            def const(i, fn):
                if i:
                    gp.wait_ge(consts.sem, i)
                fn().then_inc(consts.sem, 1)
            f = tmp
            sel = lambda dst, src, op, fill, b, cm, st: nc.gpsimd.affine_select(
                out=dst, in_=src, compare_op=op, fill=fill, base=b, pattern=[[st, P]], channel_multiplier=cm)
            const(0, lambda: nc.gpsimd.memset(ident[:, :], 0.0))
            const(1, lambda: sel(ident[:, :], ident[:, :], ALU.not_equal, 1.0, 0, 1, -1))
            const(2, lambda: nc.gpsimd.memset(f[0][:, 0:128], -1.0))
            const(3, lambda: sel(f[0][:, 128:256], f[0][:, 0:128], ALU.is_ge, 0.0, 0, 1, -1))
            const(4, lambda: nc.gpsimd.memset(f[1][:, 0:128], 0.0))
            const(5, lambda: sel(f[1][:, 128:256], f[1][:, 0:128], ALU.is_gt, NEG, 0, -1, 1))
            const(6, lambda: sel(f[1][:, 256:384], f[1][:, 0:128], ALU.is_ge, NEG, 0, 1, -1))
            const(7, lambda: nc.gpsimd.memset(f[0][:, 256:384], 1.0))

            def lo(l, u):
                gp.wait_ge(unit_hi.sem, unit_hi.at(l, u + 1))
                s = u % RING
                nc.gpsimd.tensor_tensor(w_lo[s][:, :, :], raw[u % RAW][:, :, :], w_hi[s][:, :, :].bitcast(F32),
                                        ALU.subtract).then_inc(unit_lo.sem, 1)

            def wab_lo_part(l, c):
                gp.wait_ge(wabh.sem, wabh.at(l, c + 1))
                nc.gpsimd.tensor_tensor(wab_lo[c % 2][:, :, :], wab_raw[:, c, :, :],
                                        wab_hi[c % 2][:, :, :].bitcast(F32), ALU.subtract).then_inc(wabl.sem, 1)

            with gp.Fori(0, DEPTH) as l:
                for u in range(UNITS):
                    lo(l, u)
                    if U_RG + 4 <= u < U_RG + 4 + 2 * KD and (u - U_RG) % 2 == 0:
                        wab_lo_part(l, (u - U_RG - 4) // 2)
            for u in range(AHEAD):
                lo(DEPTH, u)

        @block.scalar
        def _(act):
            A = nc.scalar.activation

            def tick(l, u):
                n = u + AHEAD
                slot = n % RAW
                act.wait_ge(raw_loaded[slot].sem, raw_loaded[slot].at(l, 16 * (n // RAW + 1)))
                if n >= RING:
                    act.wait_ge(unit_done.sem, unit_done.at(l, n - RING + 1))
                A(w_hi[n % RING][:, :, :], raw[slot][:, :, :], ACT.Copy).then_inc(unit_hi.sem, 1)

            def square(l, m, n):
                j = 8 * m + n
                if m >= 0 or n >= 2:
                    act.wait_ge(sumsq.sem, sumsq.at(l, j - 1))
                A(tmp[n % 2][:, :], x[:, n, :], ACT.Square).then_inc(sq_ready.sem, 1)
                act.wait_ge(sq_ready.sem, sq_ready.at(l, j + 1))
                A(sq_hi[n % 2][:, :], tmp[n % 2][:, :], ACT.Copy).then_inc(sqh_ready.sem, 1)

            def norm(l, m, final=False):
                nc.scalar.preload_act_table_set("natural_log_exp_and_others")
                act.wait_ge(sumsq.sem, sumsq.at(l, 8 * m + 8))
                A(rstd[:, :], bank[BS][:, :], ACT.Ln, bias=eps_col[:, 0:1], scale=1.0 / D).then_inc(ln_ready.sem, 1)
                act.wait_ge(ln_ready.sem, ln_ready.at(l, m + 1))
                A(rstd[:, :], rstd[:, :], ACT.Exp, scale=-0.5).then_inc(rstd_ready.sem, 1)

            def h_round(l, m, group):
                act.wait_ge(nscale_set.sem, nscale_set.at(l, m + 1))
                for k in range(KD):
                    j = 8 * (m + 1) + k
                    act.wait_ge(xr_ready.sem, xr_ready.at(l, j + 1))
                    A(h_hi[:, k, :], tmp[k % 2][:, :], ACT.Identity, bias=mod[:, 24 * group + k:24 * group + k + 1],
                      scale=nscale[:, group, k:k + 1]).then_inc(hh_ready.sem, 1)

            def ffn(l, s):
                u0 = U_FFN[s]
                for f in range(KF):
                    tick(l, u0 + 2 * f)
                    tick(l, u0 + 2 * f + 1)
                    if f:
                        g_round(l, s, f - 1)
                    act.wait_ge(unit_done.sem, unit_done.at(l, u0 + 2 * f + 2))
                    if f >= 2:
                        act.wait_ge(g_ready.sem, g_ready.at(l, s * KF + f - 1))
                    A(tmp[f % 2][:, :], bank[2 * (f % 2)][:, :], ACT.Silu).then_inc(silu_ready.sem, 1)
                tick(l, u0 + 2 * KF)
                g_round(l, s, KF - 1)
                u = 2 * KF + 1
                for n in range(KD):
                    while u < 2 * KF + ((n + 1) * KF + UB - 1) // UB:
                        tick(l, u0 + u)
                        u += 1
                    act.wait_ge(x_ready.sem, x_ready.at(l, 16 * s + n + 1))
                    square(l, 2 * s, n)

            def g_round(l, s, f):
                act.wait_ge(g_ready.sem, g_ready.at(l, s * KF + f + 1))
                A(g_hi[:, f, :], tmp[2 + f % 2][:, :], ACT.Copy).then_inc(gh_ready.sem, 1)

            def rg_1(l, c):
                u = U_RG + 2 * c
                tick(l, u)
                act.wait_ge(unit_done.sem, unit_done.at(l, u + 1))
                if c:
                    act.wait_ge(conv.sem, conv.at(l, 3 * c))
                if c == 0:
                    act.wait_ge(xs_zero.sem, xs_zero.at(l, 1))
                A(xs[:, 3:T + 3], bank[2 * (c % 2)][:, :], ACT.Copy).then_inc(xs_ready.sem, 1)
                if c >= 2:
                    act.wait_ge(ix_ready.sem, ix_ready.at(l, c - 1))
                A(xa[c % 2][:, :], bank[2 * (c % 2)][:, :], ACT.Identity, bias=vec[:, V_CONVB + c:V_CONVB + c + 1],
                  scale=vec[:, V_CONVW + 24 + c:V_CONVW + 25 + c]).then_inc(xa0_ready.sem, 1)
                tick(l, u + 1)
                act.wait_ge(unit_done.sem, unit_done.at(l, u + 2))
                if c >= 2:
                    act.wait_ge(yal.sem, yal.at(l, c - 1))
                A(gel[c % 2][:, :], bank[2 * (c % 2) + 1][:, :], ACT.Gelu_apprx_tanh).then_inc(gelu_ready.sem, 1)

                if c == 0:
                    act.wait_ge(wab_loaded.sem, wab_loaded.at(l, 16))
                if c >= 2:
                    act.wait_ge(gates_done.sem, gates_done.at(l, c - 1))
                A(wab_hi[c % 2][:, :, :], wab_raw[:, c, :, :], ACT.Copy).then_inc(wabh.sem, 1)

            def rg_2(l, c):
                nc.scalar.preload_act_table_set("sigmoid_and_others")
                act.wait_ge(gates_done.sem, gates_done.at(l, c + 1))
                if c:
                    act.wait_ge(scan_ready.sem, scan_ready.at(l, c))
                A(gr[:, :], bank[4][:, :], ACT.Sigmoid, bias=vec[:, V_BA + c:V_BA + c + 1]).then_inc(r_ready.sem, 1)
                A(gi[:, :], bank[5][:, :], ACT.Sigmoid, bias=vec[:, V_BX + c:V_BX + c + 1]).then_inc(i_ready.sem, 1)
                nc.scalar.preload_act_table_set("exp_and_others")
                act.wait_ge(r_ready.sem, r_ready.at(l, c + 1))
                if c == 0:
                    act.wait_ge(sp_set.sem, sp_set.at(l, 2))
                if c:
                    act.wait_ge(ya_ready.sem, ya_ready.at(l, c))
                A(gt[:, :], gr[:, :], ACT.Tanh, scale=pos_sp[:, c:c + 1]).then_inc(t_ready.sem, 1)
                act.wait_ge(t_ready.sem, t_ready.at(l, c + 1))
                A(gr[:, :], gr[:, :], ACT.Exp, scale=neg_sp[:, c:c + 1]).then_inc(a_ready.sem, 1)
                act.wait_ge(s_ready.sem, s_ready.at(l, c + 1))
                A(gt[:, :], gt[:, :], ACT.Sqrt).then_inc(sqrt_ready.sem, 1)
                act.wait_ge(ya_ready.sem, ya_ready.at(l, c + 1))
                A(ya_hi[:, c, :], gel[c % 2][:, :], ACT.Copy).then_inc(yah.sem, 1)

            def q_round(l, p):
                u = U_QKV + 3 * p
                tick(l, u)
                act.wait_ge(unit_done.sem, unit_done.at(l, u + 1))
                if p:
                    act.wait_ge(z_done.sem, z_done.at(l, 6 * p))
                A(q_hi[:, :], bank[QKV_BANK(p, 0)][:, :], ACT.Copy, scale=HD ** -0.5).then_inc(qh.sem, 1)

            def k_round(l, p):
                u = U_QKV + 3 * p + 1
                tick(l, u)
                act.wait_ge(unit_done.sem, unit_done.at(l, u + 1))
                A(k_hi[:, :], bank[QKV_BANK(p, 1)][:, :], ACT.Copy).then_inc(kh.sem, 1)

            def v_copy(l, p):
                u = U_QKV + 3 * p + 2
                tick(l, u)
                act.wait_ge(unit_done.sem, unit_done.at(l, u + 1))
                if p:
                    act.wait_ge(vt_done.sem, vt_done.at(l, p))
                if p == 0:
                    act.wait_ge(conv.sem, conv.at(l, 3 * KD))
                A(vt[:, :], bank[QKV_BANK(p, 2)][:, :], ACT.Copy).then_inc(vt_ready.sem, 1)

            def v_round(l, p):
                act.wait_ge(vt_done.sem, vt_done.at(l, p + 1))
                if p:
                    act.wait_ge(pv_head.sem, pv_head.at(l, 2 * p))
                if p == 0:
                    act.wait_ge(v_zero.sem, v_zero.at(l, 1))
                src = bank[7][:, :].rearrange("p (j e d) -> p j e d", j=TT, e=2)
                for e in range(2):
                    i = A(v_hi[:, :, e * (P + HD):e * (P + HD) + HD], src[:, :, e, :], ACT.Copy)
                i.then_inc(vh.sem, 1)

            def sb_1(l, p, e):
                n = 2 * p + e
                if n >= 2:
                    act.wait_ge(pv_head.sem, pv_head.at(l, n - 1))
                for c, (o, w) in enumerate(CHUNK):
                    act.wait_ge(z_done.sem, z_done.at(l, 3 * n + c + 1))
                    A(e_f[e][:, o:o + w], bank[ZB[e][c]][:, 0:w], ACT.Abs).then_inc(abs_ready.sem, 1)
                act.wait_ge(abs_ready.sem, abs_ready.at(l, 3 * n + 3))
                A(e_f[e][:, :], e_f[e][:, :], ACT.Exp, scale=-1.0).then_inc(exp_ready.sem, 1)
                act.wait_ge(exp_ready.sem, exp_ready.at(l, n + 1))
                A(e_f[e][:, :], e_f[e][:, :], ACT.Ln, bias=one_col[:, 0:1]).then_inc(lnp_ready.sem, 1)

            def sb_2(l, p, e):
                n = 2 * p + e
                for c, (o, w) in enumerate(CHUNK):
                    act.wait_ge(suf_done.sem, suf_done.at(l, 3 * n + 3))
                    A(e_f[e][:, o:o + w], bank[ZB[e][c]][:, 0:w], ACT.Exp).then_inc(w_ready.sem, 1)

            def fx_1(l, p, e):
                n = 2 * (p - 4) + e
                act.wait_ge(max_ready.sem, max_ready.at(l, TT * n + TT))
                for i in range(TT):
                    b, o = FX_AT[i]
                    A(e_f[e][:, 512 * b + o:512 * b + o + P * (i + 1)], bank[ZB[e][b]][:, o:o + P * (i + 1)], ACT.Exp,
                      bias=negmax[:, e, i:i + 1], accum_out=psums[:, e, i:i + 1]).then_inc(p_ready.sem, 1)

            def fx_2(l, p, e):
                n = 2 * (p - 4) + e
                act.wait_ge(suf_done.sem, suf_done.at(l, 6 * p + 3 * e + 3))
                for c, (o, w) in enumerate(CHUNK):
                    A(e_hi[e][:, o:o + w], bank[ZB[e][c]][:, 0:w], ACT.Copy).then_inc(ph.sem, 1)

            def y_round(l, p):
                act.wait_ge(pv_head.sem, pv_head.at(l, 2 * p + 2))
                if p == 0:
                    act.wait_ge(yal.sem, yal.at(l, KD))
                A(yb_hi[:, p, :], bank[7][:, :], ACT.Copy).then_inc(ybh.sem, 1)

            def merge(l, n):
                u = U_MERGE + 5 * n
                for g in range(3):
                    tick(l, u + g)
                    act.wait_ge(unit_done.sem, unit_done.at(l, u + g + 1))
                    if n:
                        act.wait_ge(mx_step.sem, mx_step.at(l, 5 * n))
                    A(sg[g][:, :], bank[g][:, :], ACT.Sigmoid,
                      bias=vec[:, V_MERGEB + 8 * g + n:V_MERGEB + 8 * g + n + 1]).then_inc(sg_ready.sem, 1)
                tick(l, u + 3)
                tick(l, u + 4)
                act.wait_ge(mx_step.sem, mx_step.at(l, 5 * n + 5))
                A(mx_hi[:, n, :], mx[:, :], ACT.Copy).then_inc(mxh.sem, 1)

            act.wait_ge(c_loaded.sem, 16)
            A(c_act[:, :], c_act[:, :], ACT.Silu).then_inc(silu_c.sem, 1)
            act.wait_ge(consts.sem, 8)
            for dst, src in ((ident_r, ident[:, :]), (ntri_r, tmp[0][:, 128:256]), (nones_r, tmp[0][:, 0:128]),
                             (ones_r, tmp[0][:, 256:384]), (mask_sb, tmp[1][:, 128:256]),
                             (mask_fx, tmp[1][:, 256:384])):
                A(dst[:, :], src, ACT.Copy).then_inc(consts_v.sem, 1)
            act.wait_ge(consts_v.sem, 8)
            for n in range(KD):
                act.wait_ge(x_loaded.sem, 16 * KD)
                square(0, -1, n)
            for u in range(-AHEAD, 0):
                tick(0, u)
            norm(0, -1)
            with act.Fori(0, DEPTH) as l:
                h_round(l, -1, 0)
                nc.scalar.preload_act_table_set("silu_and_others")
                ffn(l, 0)
                norm(l, 0)
                h_round(l, 0, 1)
                act.wait_ge(wf_loaded.sem, wf_loaded.at(l, 16))
                A(wf_hi[:, :, :], wf_raw[:, :, :], ACT.Copy).then_inc(wfh.sem, 1)
                act.wait_ge(sp_step.sem, sp_step.at(l, 1))
                A(spc[:, 1, :], spc[:, 0, :], ACT.Exp).then_inc(sp_exp.sem, 1)
                rg_1(l, 0)
                rg_1(l, 1)
                nc.scalar.preload_act_table_set("natural_log_exp_and_others")
                act.wait_ge(fx_step.sem, fx_step.at(l, 1))
                A(fx_b[:, :], fx_a[:, :], ACT.Abs).then_inc(fx_act.sem, 1)
                act.wait_ge(fx_act.sem, fx_act.at(l, 1))
                A(fx_b[:, :], fx_b[:, :], ACT.Exp, scale=-1.0).then_inc(fx_act.sem, 1)
                act.wait_ge(fx_act.sem, fx_act.at(l, 2))
                A(fx_b[:, :], fx_b[:, :], ACT.Ln, bias=one_col[0:HEADS, 0:1]).then_inc(fx_act.sem, 1)
                rg_2(l, 0)
                for c in range(2, KD):
                    rg_1(l, c)
                    rg_2(l, c - 1)
                q_round(l, 0)
                rg_2(l, KD - 1)
                k_round(l, 0)
                v_copy(l, 0)
                nc.scalar.preload_act_table_set("natural_log_exp_and_others")
                for p in range(PAIRS):
                    first, second = (sb_1, sb_2) if p < 4 else (fx_1, fx_2)
                    first(l, p, 0)
                    v_round(l, p)
                    if p + 1 < PAIRS:
                        first(l, p, 1)
                        q_round(l, p + 1)
                        second(l, p, 0)
                        second(l, p, 1)
                        k_round(l, p + 1)
                        y_round(l, p)
                        v_copy(l, p + 1)
                    else:
                        first(l, p, 1)
                        second(l, p, 0)
                        second(l, p, 1)
                        y_round(l, p)
                nc.scalar.preload_act_table_set("sigmoid_and_others")
                for n in range(KD):
                    merge(l, n)
                for n in range(KD):
                    tick(l, U_WO + n)
                    if n % 2 == 1:
                        for i in (n - 1, n):
                            act.wait_ge(x_ready.sem, x_ready.at(l, 8 + i + 1))
                            square(l, 1, i)
                norm(l, 1)
                h_round(l, 1, 2)
                nc.scalar.preload_act_table_set("silu_and_others")
                ffn(l, 1)
                norm(l, 2)

        @block.vector
        def _(dve):
            V = nc.vector

            def ada_tile(l, a):
                col = (a + 16) % 72
                dve.wait_ge(ada_loaded[a % 2].sem, ada_loaded[a % 2].at(l, 16 * (a // 2 + 1)))
                V.tensor_tensor_reduce(ada[a % 2][:, :], ada[a % 2][:, :], c_act[:, :], 1.0, 0.0, ALU.mult, ALU.add,
                                       mod[:, col:col + 1]).then_inc(ada_done.sem, 1)

            def mod_bias(l, a1, c0, c1):
                dve.wait_ge(ada_done.sem, ada_done.at(l, a1))
                V.tensor_tensor(mod[:, c0:c1], mod[:, c0:c1], vec[:, V_ADAB + c0:V_ADAB + c1],
                                ALU.add).then_inc(mod_set.sem, 1)

            def scale_col(l, k, vnorm, group):
                dve.wait_ge(mod_set.sem, mod_set.at(l, k))
                V.scalar_tensor_tensor(out=nscale[:, group, :], in0=mod[:, 24 * group + 8:24 * group + 16], scalar=1.0,
                                       in1=vec[:, vnorm:vnorm + 8], op0=ALU.add,
                                       op1=ALU.mult).then_inc(nscale_set.sem, 1)

            def gate_col(l, s, group, half):
                V.tensor_scalar(gatec[:, :], mod[:, 24 * group + 16:24 * group + 24], 1.0, half, ALU.add,
                                ALU.mult).then_inc(gate_set.sem, 1)
                dve.wait_ge(gate_set.sem, gate_set.at(l, s + 1))

            def square_lo(l, m, n):
                j = 8 * m + n
                dve.wait_ge(sqh_ready.sem, sqh_ready.at(l, j + 1))
                V.tensor_tensor(sq_lo[n % 2][:, :], tmp[n % 2][:, :], sq_hi[n % 2][:, :].bitcast(F32),
                                ALU.subtract).then_inc(sql_ready.sem, 1)

            def h_tiles(l, m, group, final=False):
                dve.wait_ge(rstd_ready.sem, rstd_ready.at(l, m + 1))
                dve.wait_ge(nscale_set.sem, nscale_set.at(l, m + 1))

                def rest(k):
                    j = 8 * (m + 1) + k
                    dve.wait_ge(hh_ready.sem, hh_ready.at(l, j + 1))
                    dve.wait_ge(hf_ready.sem, hf_ready.at(l, j + 1))
                    V.tensor_tensor(h_lo[:, k, :], tmp[2 + k % 2][:, :], h_hi[:, k, :].bitcast(F32),
                                    ALU.subtract).then_inc(hl_ready.sem, 1)

                for k in range(KD):
                    j = 8 * (m + 1) + k
                    if k >= 2:
                        dve.wait_ge(hf_ready.sem, hf_ready.at(l, j - 1))
                        if not final:
                            dve.wait_ge(hh_ready.sem, hh_ready.at(l, j - 1))
                    V.tensor_tensor(tmp[k % 2][:, :], x[:, k, :], rstd[:, :], ALU.mult).then_inc(xr_ready.sem, 1)
                    dve.wait_ge(xr_ready.sem, xr_ready.at(l, j + 1))
                    if k >= 2:
                        if final:
                            dve.wait_ge(out_stored[k % 2].sem, 16 * (k // 2))
                        else:
                            dve.wait_ge(hl_ready.sem, hl_ready.at(l, j - 1))
                    V.tensor_scalar(tmp[2 + k % 2][:, :], tmp[k % 2][:, :], nscale[:, group, k:k + 1],
                                    mod[:, 24 * group + k:24 * group + k + 1], ALU.mult,
                                    ALU.add).then_inc(hf_ready.sem, 1)
                    if not final and k:
                        rest(k - 1)
                if not final:
                    rest(KD - 1)

            def x_add(l, j, bnk, n):
                V.scalar_tensor_tensor(out=x[:, n, :], in0=bnk, scalar=gatec[:, n:n + 1], in1=x[:, n, :],
                                       op0=ALU.mult, op1=ALU.add).then_inc(x_ready.sem, 1)

            def ffn(l, s):
                u0 = U_FFN[s]
                tiles = (lambda u: [u] if u < 56 else []) if s == 0 else (
                    lambda u: [56 + u - 6] if 6 <= u < 22 else [])

                def gl(f):
                    dve.wait_ge(gh_ready.sem, gh_ready.at(l, s * KF + f + 1))
                    V.tensor_tensor(g_lo[:, f, :], tmp[2 + f % 2][:, :], g_hi[:, f, :].bitcast(F32),
                                    ALU.subtract).then_inc(gl_ready.sem, 1)

                for f in range(KF):
                    for u in (2 * f, 2 * f + 1):
                        for a in tiles(u):
                            ada_tile(l, a)
                    dve.wait_ge(silu_ready.sem, silu_ready.at(l, s * KF + f + 1))
                    if f >= 2:
                        dve.wait_ge(gl_ready.sem, gl_ready.at(l, s * KF + f - 1))
                    V.tensor_tensor(tmp[2 + f % 2][:, :], tmp[f % 2][:, :], bank[2 * (f % 2) + 1][:, :],
                                    ALU.mult).then_inc(g_ready.sem, 1)
                    if f:
                        gl(f - 1)
                gl(KF - 1)
                if s == 0:
                    ada_tiles = list(range(44, 56))
                    mod_bias(l, 8, 16, 24)
                    dve.wait_ge(mod_set.sem, mod_set.at(l, 1))
                    gate_col(l, 0, 0, 0.5)
                else:
                    gate_col(l, 2, 2, 0.5)
                    dve.wait_ge(vec_loaded.sem, vec_loaded.at(l, 16))
                    mod_bias(l, 72, 0, 16)
                    scale_col(l, 3, V_NORM1, 0)
                for n in range(KD):
                    if n in INSIDE:
                        dve.wait_ge(down_done.sem, down_done.at(l, s * TILE_ENDS + INSIDE.index(n) + 1))
                    else:
                        dve.wait_ge(unit_done.sem, unit_done.at(l, u0 + 2 * KF + (n + 1) * KF // UB))
                    x_add(l, 16 * s + n, bank[4 + n % 2][:, :], n)
                    square_lo(l, 2 * s, n)
                    if s == 0:
                        for a in ada_tiles[2 * n:2 * n + 2]:
                            ada_tile(l, a)
                if s == 0:
                    mod_bias(l, 56, 24, 72)
                    scale_col(l, 2, V_NORM2, 1)
                    scale_col(l, 2, V_NORM3, 2)

            def rg_1(l, c):
                s = c % 2
                dve.wait_ge(xa0_ready.sem, xa0_ready.at(l, c + 1))
                for j in range(3):
                    if j:
                        dve.wait_ge(conv.sem, conv.at(l, 3 * c + j))
                    V.scalar_tensor_tensor(out=xa[s][:, :], in0=xs[:, j:j + T],
                                           scalar=vec[:, V_CONVW + 8 * j + c:V_CONVW + 8 * j + c + 1],
                                           in1=xa[s][:, :], op0=ALU.mult, op1=ALU.add).then_inc(conv.sem, 1)
                dve.wait_ge(conv.sem, conv.at(l, 3 * c + 3))
                if c:
                    dve.wait_ge(gates_done.sem, gates_done.at(l, c))
                V.tensor_copy(xa_hi[:, :], xa[s][:, :]).then_inc(xah.sem, 1)
                dve.wait_ge(xah.sem, xah.at(l, c + 1))
                V.tensor_tensor(xa_lo[:, :], xa[s][:, :], xa_hi[:, :].bitcast(F32), ALU.subtract).then_inc(xal.sem, 1)

            def rg_2(l, c):
                s = c % 2
                dve.wait_ge(i_ready.sem, i_ready.at(l, c + 1))
                V.tensor_tensor(gi[:, :], gi[:, :], xa[s][:, :], ALU.mult).then_inc(ix_ready.sem, 1)
                dve.wait_ge(a_ready.sem, a_ready.at(l, c + 1))
                V.tensor_tensor(asq[:, :], gr[:, :], gr[:, :], ALU.mult).then_inc(asq_ready.sem, 1)
                dve.wait_ge(asq_ready.sem, asq_ready.at(l, c + 1))
                V.scalar_tensor_tensor(out=gt[:, :], in0=asq[:, :], scalar=1.0, in1=gt[:, :], op0=ALU.add,
                                       op1=ALU.mult).then_inc(s_ready.sem, 1)
                dve.wait_ge(ix_ready.sem, ix_ready.at(l, c + 1))
                dve.wait_ge(sqrt_ready.sem, sqrt_ready.at(l, c + 1))
                V.tensor_tensor(gi[:, :], gt[:, :], gi[:, :], ALU.mult).then_inc(u_ready.sem, 1)
                dve.wait_ge(u_ready.sem, u_ready.at(l, c + 1))
                V.tensor_tensor_scan(gt[:, :], gr[:, :], gi[:, :], 0.0, ALU.mult, ALU.add).then_inc(scan_ready.sem, 1)
                dve.wait_ge(scan_ready.sem, scan_ready.at(l, c + 1))
                dve.wait_ge(gelu_ready.sem, gelu_ready.at(l, c + 1))
                V.tensor_tensor(gel[s][:, :], gel[s][:, :], gt[:, :], ALU.mult).then_inc(ya_ready.sem, 1)
                dve.wait_ge(yah.sem, yah.at(l, c + 1))
                V.tensor_tensor(ya_lo[:, c, :], gel[s][:, :], ya_hi[:, c, :].bitcast(F32),
                                ALU.subtract).then_inc(yal.sem, 1)

            def softplus_lambda(l):
                n = [0]

                def step(i):
                    i.then_inc(sp_step.sem, 1)
                    n[0] += 1
                    dve.wait_ge(sp_step.sem, sp_step.at(l, n[0]))
                lam = vec[:, V_LAM:V_LAM + 8]
                step(V.scalar_tensor_tensor(out=spc[:, 0, :], in0=lam, scalar=-1.0, in1=lam, op0=ALU.mult,
                                            op1=ALU.min))
                dve.wait_ge(sp_exp.sem, sp_exp.at(l, 1))
                e = spc[:, 1, :]
                step(V.tensor_scalar(spc[:, 2, :], e, 2.0, None, ALU.add))
                step(V.reciprocal(spc[:, 2, :], spc[:, 2, :]))
                step(V.tensor_tensor(spc[:, 2, :], spc[:, 2, :], e, ALU.mult))
                step(V.tensor_tensor(spc[:, 3, :], spc[:, 2, :], spc[:, 2, :], ALU.mult))
                step(V.tensor_scalar(spc[:, 4, :], spc[:, 3, :], 1.0 / 15, None, ALU.mult))
                for d in (13, 11, 9, 7, 5, 3):
                    step(V.scalar_tensor_tensor(out=spc[:, 4, :], in0=spc[:, 4, :], scalar=1.0 / d,
                                                in1=spc[:, 3, :], op0=ALU.add, op1=ALU.mult))
                step(V.scalar_tensor_tensor(out=spc[:, 4, :], in0=spc[:, 4, :], scalar=1.0, in1=spc[:, 2, :],
                                            op0=ALU.add, op1=ALU.mult))
                step(V.tensor_scalar(spc[:, 5, :], lam, -1.0, 0.0, ALU.mult, ALU.max))
                V.scalar_tensor_tensor(out=spc[:, 0, :], in0=spc[:, 4, :], scalar=2.0, in1=spc[:, 5, :],
                                       op0=ALU.mult, op1=ALU.add).then_inc(sp_exp.sem, 1)
                dve.wait_ge(sp_exp.sem, sp_exp.at(l, 2))
                V.tensor_scalar(neg_sp[:, :], spc[:, 0, :], -8.0, None, ALU.mult).then_inc(sp_set.sem, 1)
                V.tensor_scalar(pos_sp[:, :], spc[:, 0, :], 8.0, None, ALU.mult).then_inc(sp_set.sem, 1)

            def forget_1(l):
                dve.wait_ge(foxf_done.sem, foxf_done.at(l, 1))
                b = vec[0:HEADS, V_FOXB:V_FOXB + 1]
                V.tensor_scalar(fx_a[:, :], bank[7][0:HEADS, :], b, None, ALU.add).then_inc(fx_step.sem, 1)

            def forget_2(l):
                dve.wait_ge(fx_act.sem, fx_act.at(l, 1))
                V.tensor_scalar(fx_a[:, :], fx_a[:, :], -1.0, 0.0, ALU.mult, ALU.max).then_inc(fx_step.sem, 1)
                dve.wait_ge(fx_step.sem, fx_step.at(l, 2))
                dve.wait_ge(fx_act.sem, fx_act.at(l, 3))
                V.tensor_tensor_scan(fx_c[:, :], fx_a[:, :], fx_b[:, :], 0.0, ALU.add, ALU.add)\
                    .then_inc(fx_step.sem, 1)
                dve.wait_ge(fx_step.sem, fx_step.at(l, 3))
                V.tensor_copy(nc_hi[:, :], fx_c[:, :]).then_inc(nch.sem, 1)
                dve.wait_ge(nch.sem, nch.at(l, 1))
                V.tensor_tensor(nc_lo[:, :], fx_c[:, :], nc_hi[:, :].bitcast(F32), ALU.subtract).then_inc(ncl.sem, 1)

            def q_rest(l, p):
                dve.wait_ge(qh.sem, qh.at(l, p + 1))
                V.scalar_tensor_tensor(out=q_lo[:, :], in0=bank[QKV_BANK(p, 0)][:, :], scalar=HD ** -0.5,
                                       in1=q_hi[:, :].bitcast(F32), op0=ALU.mult,
                                       op1=ALU.subtract).then_inc(ql.sem, 1)

            def k_rest(l, p):
                dve.wait_ge(kh.sem, kh.at(l, p + 1))
                V.tensor_tensor(k_lo[:, :], bank[QKV_BANK(p, 1)][:, :], k_hi[:, :].bitcast(F32),
                                ALU.subtract).then_inc(kl.sem, 1)

            def v_rest(l, p):
                if p == 0:
                    dve.wait_ge(v_zero.sem, v_zero.at(l, 2))
                dve.wait_ge(vh.sem, vh.at(l, p + 1))
                src = bank[7][:, :].rearrange("p (j e d) -> p j e d", j=TT, e=2)
                for e in range(2):
                    o = e * (P + HD)
                    i = V.tensor_tensor(v_lo[:, :, o:o + HD], src[:, :, e, :], v_hi[:, :, o:o + HD].bitcast(F32),
                                        ALU.subtract)
                i.then_inc(vl.sem, 1)

            def sb_softplus(l, p, e):
                n = 2 * p + e
                dve.wait_ge(lnp_ready.sem, lnp_ready.at(l, n + 1))
                for c, (o, w) in enumerate(CHUNK):
                    V.scalar_tensor_tensor(out=e_f[e][:, o:o + w], in0=bank[ZB[e][c]][:, 0:w], scalar=0.0,
                                           in1=e_f[e][:, o:o + w], op0=ALU.max,
                                           op1=ALU.add).then_inc(sp_ready.sem, 1)
                dve.wait_ge(sp_ready.sem, sp_ready.at(l, 3 * n + 3))
                V.tensor_copy(e_hi[e][:, :], e_f[e][:, :]).then_inc(sph.sem, 1)
                dve.wait_ge(sph.sem, sph.at(l, n + 1))
                V.tensor_tensor(e_lo[e][:, :], e_f[e][:, :], e_hi[e][:, :].bitcast(F32),
                                ALU.subtract).then_inc(spl.sem, 1)

            def sb_split(l, p, e):
                n = 2 * p + e
                dve.wait_ge(w_ready.sem, w_ready.at(l, 3 * n + 3))
                V.tensor_copy(e_hi[e][:, :], e_f[e][:, :]).then_inc(eh.sem, 1)
                dve.wait_ge(eh.sem, eh.at(l, n + 1))
                V.tensor_tensor(e_lo[e][:, :], e_f[e][:, :], e_hi[e][:, :].bitcast(F32),
                                ALU.subtract).then_inc(el.sem, 1)

            def fx_max(l, p, e):
                n = 2 * (p - 4) + e
                dve.wait_ge(pv_head.sem, pv_head.at(l, 2 * p + e - 1))
                dve.wait_ge(z_done.sem, z_done.at(l, 6 * p + 3 * e + 3))
                for i in range(TT):
                    b, o = FX_AT[i]
                    V.tensor_reduce(negmax[:, e, i:i + 1], bank[ZB[e][b]][:, o:o + P * (i + 1)], AX.X, ALU.max,
                                    negate=True).then_inc(max_ready.sem, 1)

            def fx_norm(l, p, e):
                n = 2 * (p - 4) + e
                dve.wait_ge(p_ready.sem, p_ready.at(l, TT * n + TT))
                V.reciprocal(rsums[:, e, :], psums[:, e, :]).then_inc(rs_ready.sem, 1)
                dve.wait_ge(rs_ready.sem, rs_ready.at(l, n + 1))
                for i in range(TT):
                    b, o = FX_AT[i]
                    t = e_f[e][:, 512 * b + o:512 * b + o + P * (i + 1)]
                    V.tensor_scalar(t, t, rsums[:, e, i:i + 1], None, ALU.mult).then_inc(pn_ready.sem, 1)

            def fx_split(l, p, e):
                n = 2 * (p - 4) + e
                for c, (o, w) in enumerate(CHUNK):
                    dve.wait_ge(ph.sem, ph.at(l, 3 * n + c + 1))
                    V.tensor_tensor(e_lo[e][:, o:o + w], bank[ZB[e][c]][:, 0:w], e_hi[e][:, o:o + w].bitcast(F32),
                                    ALU.subtract).then_inc(pl.sem, 1)

            def y_rest(l, p):
                dve.wait_ge(ybh.sem, ybh.at(l, p + 1))
                V.tensor_tensor(yb_lo[:, p, :], bank[7][:, :], yb_hi[:, p, :].bitcast(F32),
                                ALU.subtract).then_inc(ybl.sem, 1)

            def merge(l, n):
                u = U_MERGE + 5 * n
                m0 = 5 * n
                if n:
                    dve.wait_ge(mxl.sem, mxl.at(l, n))
                dve.wait_ge(sg_ready.sem, sg_ready.at(l, 3 * n + 3))
                dve.wait_ge(unit_done.sem, unit_done.at(l, u + 4))
                V.tensor_tensor(mx[:, :], sg[0][:, :], bank[3][:, :], ALU.mult).then_inc(mx_step.sem, 1)
                dve.wait_ge(unit_done.sem, unit_done.at(l, u + 5))
                for g in (1, 2):
                    V.tensor_tensor(sg[g][:, :], sg[g][:, :], bank[3 + g][:, :], ALU.mult).then_inc(mx_step.sem, 1)
                dve.wait_ge(mx_step.sem, mx_step.at(l, m0 + 2))
                V.tensor_tensor(mx[:, :], mx[:, :], sg[1][:, :], ALU.add).then_inc(mx_step.sem, 1)
                dve.wait_ge(mx_step.sem, mx_step.at(l, m0 + 4))
                V.tensor_tensor(mx[:, :], mx[:, :], sg[2][:, :], ALU.add).then_inc(mx_step.sem, 1)
                dve.wait_ge(mxh.sem, mxh.at(l, n + 1))
                V.tensor_tensor(mx_lo[:, n, :], mx[:, :], mx_hi[:, n, :].bitcast(F32),
                                ALU.subtract).then_inc(mxl.sem, 1)

            V.memset(eps_col[:, :], EPS).then_inc(consts_v.sem, 1)
            V.memset(one_col[:, :], 1.0).then_inc(consts_v.sem, 1)
            dve.wait_ge(silu_c.sem, 1)
            dve.wait_ge(vec_loaded.sem, 16)
            for n in range(KD):
                square_lo(0, -1, n)
            for a in range(-16, 0):
                ada_tile(0, a)
            mod_bias(0, 0, 0, 16)
            scale_col(0, 0, V_NORM1, 0)
            with dve.Fori(0, DEPTH) as l:
                h_tiles(l, -1, 0)
                ffn(l, 0)
                h_tiles(l, 0, 1)
                gate_col(l, 1, 1, 1.0)
                dve.wait_ge(wfh.sem, wfh.at(l, 1))
                V.tensor_tensor(wf_lo[:, :, :], wf_raw[:, :, :], wf_hi[:, :, :].bitcast(F32),
                                ALU.subtract).then_inc(wfl.sem, 1)
                V.memset(xs[:, 0:3], 0.0).then_inc(xs_zero.sem, 1)
                softplus_lambda(l)
                rg_1(l, 0)
                rg_1(l, 1)
                forget_1(l)
                forget_2(l)
                rg_2(l, 0)
                for c in range(2, KD):
                    rg_1(l, c)
                    rg_2(l, c - 1)
                q_rest(l, 0)
                rg_2(l, KD - 1)
                k_rest(l, 0)
                V.memset(v_hi[:, :, :].bitcast(F32), 0.0).then_inc(v_zero.sem, 1)
                V.memset(v_lo[:, :, :].bitcast(F32), 0.0).then_inc(v_zero.sem, 1)
                for p in range(PAIRS):
                    if p < 4:
                        v_rest(l, p)
                        sb_softplus(l, p, 0)
                        sb_softplus(l, p, 1)
                    else:
                        fx_max(l, p, 0)
                        fx_max(l, p, 1)
                        v_rest(l, p)
                        fx_norm(l, p, 0)
                        fx_norm(l, p, 1)
                    if p + 1 < PAIRS:
                        q_rest(l, p + 1)
                    split = sb_split if p < 4 else fx_split
                    split(l, p, 0)
                    split(l, p, 1)
                    if p + 1 < PAIRS:
                        k_rest(l, p + 1)
                    y_rest(l, p)
                for n in range(KD):
                    merge(l, n)
                for n in range(KD):
                    dve.wait_ge(unit_done.sem, unit_done.at(l, U_WO + n + 1))
                    x_add(l, 8 + n, bank[WO_BANK(n)][:, :], n)
                    square_lo(l, 1, n)
                h_tiles(l, 1, 2)
                ffn(l, 1)
            h_tiles(DEPTH, -1, 0, final=True)

        @block.tensor
        def _(pe):
            def mm3(o, wh, wl, xh, xl, start, stop):
                nc.tensor.matmul(o, wh, xh, start=start, stop=False, skip_group_check=True)
                nc.tensor.matmul(o, wh, xl, start=False, stop=False, skip_group_check=True)
                return nc.tensor.matmul(o, wl, xh, start=False, stop=stop, skip_group_check=True)

            def unit(l, u, bnk, hi, lo):
                s = u % RING
                pe.wait_ge(unit_lo.sem, unit_lo.at(l, u + 1))
                for k in range(KD):
                    i = mm3(bnk, w_hi[s][:, k, :], w_lo[s][:, k, :], hi[:, k, :], lo[:, k, :], k == 0, k == KD - 1)
                i.then_inc(unit_done.sem, 1)

            def pair(l, u, b0, b1, hi, lo, ready=None):
                pe.wait_ge(unit_lo.sem, unit_lo.at(l, u + 2))
                for k in range(KD):
                    if ready:
                        pe.wait_ge(ready[0].sem, ready[0].at(l, ready[1] + k + 1))
                    for j, b in ((0, b0), (1, b1)):
                        s = (u + j) % RING
                        i = mm3(bank[b][:, :], w_hi[s][:, k, :], w_lo[s][:, k, :], hi[:, k, :], lo[:, k, :], k == 0,
                                k == KD - 1)
                        if k == KD - 1:
                            i.then_inc(unit_done.sem, 1)

            def sum_squares(l, m, n):
                pe.wait_ge(sql_ready.sem, sql_ready.at(l, 8 * m + n + 1))
                nc.tensor.matmul(bank[BS][:, :], ones_r[:, :], sq_hi[n % 2][:, :], start=(n == 0), stop=False,
                                 skip_group_check=True)
                nc.tensor.matmul(bank[BS][:, :], ones_r[:, :], sq_lo[n % 2][:, :], start=False, stop=(n == KD - 1),
                                 skip_group_check=True).then_inc(sumsq.sem, 1)

            def ffn(l, s):
                u0 = U_FFN[s]
                for f in range(KF):
                    if f >= 2:
                        pe.wait_ge(g_ready.sem, g_ready.at(l, s * KF + f - 1))
                    pair(l, u0 + 2 * f, 2 * (f % 2), 2 * (f % 2) + 1, h_hi, h_lo,
                         (hl_ready, 16 * s) if f == 0 else None)
                for b in range(KD * KF):
                    n, k = divmod(b, KF)
                    u, j = divmod(b, UB)
                    if j == 0:
                        pe.wait_ge(unit_lo.sem, unit_lo.at(l, u0 + 2 * KF + u + 1))
                    if n == 0:
                        pe.wait_ge(gl_ready.sem, gl_ready.at(l, s * KF + k + 1))
                    if k == 0 and n >= 2:
                        pe.wait_ge(x_ready.sem, x_ready.at(l, 16 * s + n - 1))
                    sl = (2 * KF + u0 + u) % RING
                    i = mm3(bank[4 + n % 2][:, :], w_hi[sl][:, j, :], w_lo[sl][:, j, :], g_hi[:, k, :], g_lo[:, k, :],
                            k == 0, k == KF - 1)
                    if j == UB - 1:
                        i.then_inc(unit_done.sem, 1)
                    elif k == KF - 1:
                        i.then_inc(down_done.sem, 1)
                    if k == KF - 1:
                        if n:
                            sum_squares(l, 2 * s, n - 1)
                sum_squares(l, 2 * s, KD - 1)

            def gates(l, c):
                pe.wait_ge(xal.sem, xal.at(l, c + 1))
                pe.wait_ge(wabl.sem, wabl.at(l, c + 1))
                if c:
                    pe.wait_ge(i_ready.sem, i_ready.at(l, c))
                for j in range(2):
                    i = mm3(bank[4 + j][:, :], wab_hi[c % 2][:, j, :], wab_lo[c % 2][:, j, :], xa_hi[:, :],
                            xa_lo[:, :], True, True)
                i.then_inc(gates_done.sem, 1)

            def scores(l, p, e):
                r = slice(HD * e, HD * e + HD)
                n = 2 * p + e
                if p == 0:
                    pe.wait_ge(i_ready.sem, i_ready.at(l, KD))
                    pe.wait_ge(gelu_ready.sem, gelu_ready.at(l, KD))
                    pe.wait_ge(vt_ready.sem, vt_ready.at(l, 1))
                if e == 0:
                    pe.wait_ge(ql.sem, ql.at(l, p + 1))
                    pe.wait_ge(kl.sem, kl.at(l, p + 1))
                if p == 4 and e == 0:
                    pe.wait_ge(ncl.sem, ncl.at(l, 1))
                if p >= 1:
                    if p <= 4:
                        pe.wait_ge(w_ready.sem, w_ready.at(l, 3 * (n - 2) + 3))
                    else:
                        pe.wait_ge(pl.sem, pl.at(l, 3 * (n - 8 - 2) + 3))
                order = [0, 1, 3, 2] if p < 4 else [3, 2, 0, 1]
                for i in order:
                    b, o = (SB_AT if p < 4 else FX_AT)[i]
                    begins = o == 0
                    if p < 4:
                        w = T - P * i
                        dst = bank[ZB[e][b]][:, o:o + w]
                        mm3(dst, k_hi[r, P * i:P * i + P], k_lo[r, P * i:P * i + P], q_hi[r, P * i:T],
                            q_lo[r, P * i:T], begins, False)
                        last = nc.tensor.matmul(dst[:, 0:P], ident_r[:, :], mask_sb[:, :], start=False, stop=False,
                                                skip_group_check=True)
                    else:
                        w = P * (i + 1)
                        h = n - HEADS
                        dst = bank[ZB[e][b]][:, o:o + w]
                        mm3(dst, q_hi[r, P * i:P * i + P], q_lo[r, P * i:P * i + P], k_hi[r, 0:w], k_lo[r, 0:w],
                            begins, False)
                        pick = ident_r[0:HEADS, h:h + 1].to_broadcast([HEADS, P])
                        for d in (nc_hi, nc_lo):
                            nc.tensor.matmul(dst, pick, d[:, 0:w], start=False, stop=False, skip_group_check=True)
                        last = nc.tensor.matmul(dst[:, P * i:w], ident_r[:, :], mask_fx[:, :], start=False,
                                                stop=False, skip_group_check=True)
                    if (b == 0) or (b == 2) or o == 384:
                        last.then_inc(z_done.sem, 1)

            def suffix(l, p, e):
                pe.wait_ge(spl.sem, spl.at(l, 2 * p + e + 1))
                for i in (0, 1, 3, 2):
                    b, o = SB_AT[i]
                    for j in range(i, TT):
                        bj, oj = SB_AT[j]
                        w = T - P * j
                        dst = bank[ZB[e][b]][:, o + P * (j - i):o + P * (j - i) + w]
                        for src in (e_hi[e], e_lo[e]):
                            last = nc.tensor.matmul(dst, (ntri_r if i == j else nones_r)[:, :],
                                                    src[:, 512 * bj + oj:512 * bj + oj + w], start=False,
                                                    stop=False, skip_group_check=True)
                    if i != 1:
                        last.then_inc(suf_done.sem, 1)

            def turn(l, p, e):
                pe.wait_ge(pn_ready.sem, pn_ready.at(l, TT * (2 * (p - 4) + e) + TT))
                for j in (0, 1, 3, 2):
                    b, o = SB_AT[j]
                    for i in range(j, TT):
                        bi, oi = FX_AT[i]
                        src = 512 * bi + oi + P * j
                        last = nc.tensor.transpose(bank[ZB[e][b]][:, o + P * (i - j):o + P * (i - j) + P],
                                                   e_f[e][:, src:src + P], ident[:, :])
                    if j != 1:
                        last.then_inc(suf_done.sem, 1)

            def values(l, p, e):
                if e == 0:
                    pe.wait_ge(vl.sem, vl.at(l, p + 1))
                if p < 4:
                    pe.wait_ge(el.sem, el.at(l, 2 * p + e + 1))
                else:
                    pe.wait_ge(pl.sem, pl.at(l, 3 * (2 * (p - 4) + e) + 3))
                for j in range(TT):
                    b, o = SB_AT[j]
                    w = T - P * j
                    src = slice(512 * b + o, 512 * b + o + w)
                    i = mm3(bank[7][:, P * j:T], v_hi[:, j, e * P:e * P + P], v_lo[:, j, e * P:e * P + P],
                            e_hi[e][:, src], e_lo[e][:, src], e == 0 and j == 0, False)
                i.then_inc(pv_head.sem, 1)

            def turn_v(l, p):
                pe.wait_ge(vt_ready.sem, vt_ready.at(l, p + 1))
                if p:
                    pe.wait_ge(ybl.sem, ybl.at(l, p))
                if p == 0:
                    pe.wait_ge(fx_step.sem, fx_step.at(l, 1))
                for j in range(TT):
                    i = nc.tensor.transpose(bank[7][:, P * j:P * j + P], vt[:, P * j:P * j + P], ident[:, :])
                i.then_inc(vt_done.sem, 1)

            def qkv(l, p, j):
                if p == 0:
                    pe.wait_ge((xa0_ready, gelu_ready, xa0_ready)[j].sem, (xa0_ready, gelu_ready, xa0_ready)[j].at(l, KD - (j < 2)))
                else:
                    pe.wait_ge((vt_ready, ql, kl)[j].sem, (vt_ready, ql, kl)[j].at(l, p + (0 if j == 0 else 1)))
                unit(l, U_QKV + 3 * p + j, bank[QKV_BANK(p, j)][:, :], h_hi, h_lo)

            pe.wait_ge(consts_v.sem, 8)
            for n in range(KD):
                sum_squares(0, -1, n)
            with pe.Fori(0, DEPTH) as l:
                ffn(l, 0)
                pair(l, U_RG, 0, 1, h_hi, h_lo, (hl_ready, 8))
                for c in range(1, KD):
                    if c >= 2:
                        pe.wait_ge(xa0_ready.sem, xa0_ready.at(l, c - 1))
                    unit(l, U_RG + 2 * c, bank[2 * (c % 2)][:, :], h_hi, h_lo)
                    if c >= 2:
                        pe.wait_ge(gelu_ready.sem, gelu_ready.at(l, c - 1))
                    unit(l, U_RG + 2 * c + 1, bank[2 * (c % 2) + 1][:, :], h_hi, h_lo)
                    if c == 1:
                        pe.wait_ge(wfl.sem, wfl.at(l, 1))
                        for k in range(KD):
                            i = mm3(bank[7][0:HEADS, :], wf_hi[:, k, :], wf_lo[:, k, :], h_hi[:, k, :],
                                    h_lo[:, k, :], k == 0, k == KD - 1)
                        i.then_inc(foxf_done.sem, 1)
                    gates(l, c - 1)
                qkv(l, 0, 0)
                gates(l, KD - 1)
                qkv(l, 0, 1)
                qkv(l, 0, 2)
                for p in range(PAIRS):
                    nxt = p + 1 < PAIRS
                    middle = suffix if p < 4 else turn
                    scores(l, p, 0)
                    scores(l, p, 1)
                    turn_v(l, p)
                    if nxt:
                        qkv(l, p + 1, 0)
                    middle(l, p, 0)
                    middle(l, p, 1)
                    if nxt:
                        qkv(l, p + 1, 1)
                    values(l, p, 0)
                    values(l, p, 1)
                    if nxt:
                        qkv(l, p + 1, 2)
                pe.wait_ge(pl.sem, pl.at(l, 3 * HEADS))
                for n in range(KD):
                    u = U_MERGE + 5 * n
                    for g in range(3):
                        if n:
                            pe.wait_ge(sg_ready.sem, sg_ready.at(l, 3 * n - 2 + g))
                        unit(l, u + g, bank[g][:, :], h_hi, h_lo)
                    if n == 0:
                        pe.wait_ge(yal.sem, yal.at(l, KD))
                    if n:
                        pe.wait_ge(mx_step.sem, mx_step.at(l, 5 * n))
                    unit(l, u + 3, bank[3][:, :], ya_hi, ya_lo)
                    if n == 0:
                        pe.wait_ge(ybl.sem, ybl.at(l, PAIRS))
                    s = (u + 4) % RING
                    pe.wait_ge(unit_lo.sem, unit_lo.at(l, u + 5))
                    for j in range(KD):
                        i = mm3(bank[4 + j // 4][:, :], w_hi[s][:, j, :], w_lo[s][:, j, :], yb_hi[:, j, :],
                                yb_lo[:, j, :], j % 4 == 0, j % 4 == 3)
                    i.then_inc(unit_done.sem, 1)
                pe.wait_ge(sg_ready.sem, sg_ready.at(l, 3 * KD))
                for n in range(0, KD, 2):
                    if n == 2:
                        pe.wait_ge(mx_step.sem, mx_step.at(l, 5 * KD))
                    if n >= 4:
                        pe.wait_ge(x_ready.sem, x_ready.at(l, 8 + n - 2))
                    pair(l, U_WO + n, WO_BANK(n), WO_BANK(n + 1), mx_hi, mx_lo, (mxl, 0) if n == 0 else None)
                    if n:
                        sum_squares(l, 1, n - 2)
                        sum_squares(l, 1, n - 1)
                sum_squares(l, 1, KD - 2)
                sum_squares(l, 1, KD - 1)
                ffn(l, 1)


ZB = [(4, 5, 6), (1, 2, 3)]


def QKV_BANK(p, j):
    return j if p == 0 else 0


def WO_BANK(n):
    return n % 4


def _layout(inputs):
    import numpy as np
    g = {k: np.asarray(v, dtype=v.dtype) for k, v in inputs.items()}

    def cols(w):
        k, n = w.shape
        return w.reshape(k // P, P, n // P, P).transpose(2, 1, 0, 3)

    units = np.zeros((DEPTH * UNITS + RAW, P, UB, P), np.float32)
    for l in range(DEPTH):
        o = l * UNITS

        def ffn(u, w1, w3, w2):
            units[u:u + 2 * KF:2] = cols(w1)
            units[u + 1:u + 2 * KF:2] = cols(w3)
            d = cols(w2).transpose(0, 2, 1, 3).reshape(-1, UB, P, P)
            units[u + 2 * KF:u + FFN_UNITS] = d.transpose(0, 2, 1, 3)
        ffn(o + U_FFN[0], g["ffn1_w1"][l], g["ffn1_w3"][l], g["ffn1_w2"][l])
        ffn(o + U_FFN[1], g["ffn2_w1"][l], g["ffn2_w3"][l], g["ffn2_w2"][l])
        win = g["w_in"][l]
        a = cols(win[:, 0:2 * D])
        units[o + U_RG:o + U_QKV:2] = a[0:KD]
        units[o + U_RG + 1:o + U_QKV:2] = a[KD:2 * KD]
        for b in range(2):
            qkv = cols(win[:, 2 * D + 1536 * b:2 * D + 1536 * (b + 1)])
            for j in range(3):
                u = o + U_QKV + 12 * b + j
                units[u:u + 12:3] = qkv[4 * j:4 * j + 4]
        mg = cols(win[:, 2 * D + 3072 + HEADS:])
        for j in range(3):
            units[o + U_MERGE + j:o + U_WO:5] = mg[8 * j:8 * j + 8]
        units[o + U_MERGE + 3:o + U_WO:5] = cols(g["w_rg"][l])
        units[o + U_MERGE + 4:o + U_WO:5, :, 0:4] = cols(g["w_sb"][l])
        units[o + U_MERGE + 4:o + U_WO:5, :, 4:8] = cols(g["w_fox"][l])
        units[o + U_WO:o + U_FFN[1]] = cols(g["w_o"][l])

    def rows(w):
        return w.T.reshape(-1, P, w.shape[0])
    ada_w = np.concatenate([rows(g["ada_w"][l]) for l in range(DEPTH)] + [rows(g["final_ada_w"])])

    vecs = np.zeros((DEPTH + 1, P, NV), np.float32)

    def put(l, c, v):
        v = v.reshape(-1, P).T
        vecs[l, :, c:c + v.shape[1]] = v
    for l in range(DEPTH):
        for c, name in ((V_NORM1, "ffn1_norm"), (V_NORM2, "mix_norm"), (V_NORM3, "ffn2_norm"), (V_ADAB, "ada_b"),
                        (V_CONVW, "conv_w"), (V_CONVB, "conv_b"), (V_BA, "rg_ba"), (V_BX, "rg_bx"),
                        (V_LAM, "rg_lam"), (V_MERGEB, "merge_b")):
            put(l, c, g[name][l])
        vecs[l, 0:HEADS, V_FOXB] = g["fox_bf"][l]
    put(DEPTH, V_NORM1, g["final_norm"])
    put(DEPTH, V_ADAB, g["final_ada_b"])

    f0 = 2 * D + 3072
    wf = np.stack([g["w_in"][l][:, f0:f0 + HEADS].reshape(KD, P, HEADS).transpose(1, 0, 2) for l in range(DEPTH)])
    wab = np.zeros((DEPTH, P, KD, 2, P), np.float32)
    for j, name in enumerate(("rg_wa", "rg_wx")):
        w = g[name].reshape(DEPTH, KD, 2, HD, HD)
        for b in range(2):
            wab[:, b * HD:(b + 1) * HD, :, j, b * HD:(b + 1) * HD] = w[:, :, b].transpose(0, 2, 1, 3)
    return {
        "w_units": units, "ada_w": ada_w, "vecs": vecs, "wf": wf, "wab": wab,
        "c_rows": np.ascontiguousarray(np.broadcast_to(g["c"], (P, D))),
        "x_in": np.ascontiguousarray(g["x"][0].T).reshape(KD, P, T),
    }


def kernel(**inputs):
    import numpy as np
    import concourse.bacc as bacc
    from concourse.bass_utils import run_bass_kernel_spmd

    nc = bacc.Bacc("TRN2", target_bir_lowering=False, num_devices=1)
    arrays = {k: np.ascontiguousarray(v) for k, v in _layout(inputs).items()}
    args = {k: nc.dram_tensor(k, v.shape, mybir.dt.from_np(v.dtype), kind="ExternalInput").ap()
            for k, v in arrays.items()}
    y = nc.dram_tensor("y", (KD, P, T), F32, kind="ExternalOutput").ap()
    trunk(nc, out=y, **args)
    r = run_bass_kernel_spmd(nc, [arrays], core_ids=[0])
    return np.ascontiguousarray(r.results[0]["y"].reshape(D, T).T).reshape(1, T, D)
```

```python
from contextlib import ExitStack

import concourse.bass as bass
from concourse import mybir

F32 = mybir.dt.float32
F32R = mybir.dt.float32r
ALU = mybir.AluOpType
ACT = mybir.ActivationFunctionType
AX = mybir.AxisListType

P = 128
D = 1024
T = 512
DEPTH = 2
DFF = 2816
KD = D // P
KF = DFF // P
UB = 8
HEADS = 8
PAIRS = HEADS
HD = 64
TT = T // P
EPS = 1e-6
NEG = -(2.0 ** 100)

FFN_UNITS = 2 * KF + KF * KD // UB
U_FFN = (0, FFN_UNITS + 88)
U_RG = FFN_UNITS
U_QKV = U_RG + 2 * KD
U_MERGE = U_QKV + 3 * PAIRS
U_WO = U_MERGE + 5 * KD
UNITS = 2 * FFN_UNITS + 88
AHEAD = 3
RAW, RING = 2, 4
assert UNITS % RING == 0 and U_WO + KD == U_FFN[1]

V_NORM1, V_NORM2, V_NORM3 = 0, 8, 16
V_ADAB = 24
V_CONVW = 96
V_CONVB, V_BA, V_BX, V_LAM = 128, 136, 144, 152
V_MERGEB = 160
V_FOXB = 184
NV = 185

SB_AT = [(0, 0), (1, 0), (2, 0), (1, 384)]
FX_AT = [(1, 384), (2, 0), (1, 0), (0, 0)]
CHUNK = [(0, 512), (512, 512), (1024, 256)]
NS = 1280


INSIDE = [n for n in range(KD) if (n + 1) * KF % UB]
TILE_ENDS = len(INSIDE)
QUAD = 32
G0 = 2


class Signal:

    def __init__(self, sem, per_layer, before=0):
        self.sem, self.per_layer, self.before = sem, per_layer, before

    def at(self, l, k):
        assert k + self.before > 0
        return l * self.per_layer + k + self.before


def trunk(nc, w_units, ada_w, vecs, wf, wab, c_rows, x_in, out):
    with ExitStack() as ctx:
        def sb(name, shape, dt=F32):
            return ctx.enter_context(nc.sbuf_tensor(name, shape, dt))

        def sig(name, per_layer=0, before=0):
            return Signal(ctx.enter_context(nc.semaphore(name)), per_layer, before)

        x = sb("x", [P, KD, T])
        h_hi = sb("h_hi", [P, KD, T], F32R)
        h_lo = sb("h_lo", [P, KD, T], F32R)
        raw = [sb(f"raw{i}", [P, UB, P]) for i in range(RAW)]
        w_hi = [sb(f"w_hi{i}", [P, UB, P], F32R) for i in range(RING)]
        w_lo = [sb(f"w_lo{i}", [P, UB, P], F32R) for i in range(RING)]
        c_act = sb("c_act", [P, D])
        vec = sb("vec", [P, NV])
        mod = sb("mod", [P, 72])
        nscale = sb("nscale", [P, 3, KD])
        gatec = sb("gatec", [P, KD])
        spc = sb("spc", [P, 6, KD])
        neg_sp = sb("neg_sp", [P, KD])
        pos_sp = sb("pos_sp", [P, KD])
        negmax = sb("negmax", [P, 2, TT])
        psums = sb("psums", [P, 2, TT])
        rsums = sb("rsums", [P, 2, TT])
        eps_col = sb("eps_col", [P, 1])
        one_col = sb("one_col", [P, 1])
        ident = sb("ident", [P, P])
        ident_r = sb("ident_r", [P, P], F32R)
        pick = sb("pick", [P, HEADS], F32R)
        ones_r = sb("ones_r", [P, P], F32R)
        nones_r = sb("nones_r", [P, P], F32R)
        ntri_r = sb("ntri_r", [P, P], F32R)
        mask_sb = sb("mask_sb", [P, P], F32R)
        mask_fx = sb("mask_fx", [P, P], F32R)
        wf_raw = sb("wf_raw", [P, KD, HEADS])
        wf_hi = sb("wf_hi", [P, KD, HEADS], F32R)
        wf_lo = sb("wf_lo", [P, KD, HEADS], F32R)

        base = (nc.sbuf_base + 31) // 32 * 32
        ARENA = 110720
        sb("arena", [P, ARENA // 4])

        def at(name, offset, shape, dt=F32):
            size = 4
            for s in shape[1:]:
                size *= s
            assert offset + size <= ARENA, (name, offset + size)
            return nc.alloc_sbuf_tensor_at(name, shape, dt, offset=base + offset)

        g_hi = at("g_hi", 0, [P, KF, T], F32R)
        g_lo = at("g_lo", 45056, [P, KF, T], F32R)
        ada = [at(f"ada{i}", 90112 + 4096 * i, [P, D]) for i in range(2)]
        tmp = [at(f"tmp{i}", 98304 + 2048 * i, [P, T]) for i in range(4)]
        sqsum = at("sqsum", 102400, [P, T])
        rstd = at("rstd", 106496, [P, T])
        ada0 = [at(f"ada0_{i}", 4096 * G0 * i, [P, G0, D]) for i in range(16 // G0)]
        fin = [at(f"fin{i}", 4096 * i, [P, 2, T]) for i in range(KD // 2)]
        ya_hi = at("ya_hi", 0, [P, KD, T], F32R)
        ya_lo = at("ya_lo", 16384, [P, KD, T], F32R)
        yb_hi = at("yb_hi", 32768, [P, KD, T], F32R)
        yb_lo = at("yb_lo", 49152, [P, KD, T], F32R)
        xa = [at(f"xa{i}", 32768 + 2048 * i, [P, T]) for i in range(2)]
        gel = [at(f"gel{i}", 36864 + 2048 * i, [P, T]) for i in range(4)]
        gr = [at(f"gr{i}", 45056 + 2048 * i, [P, T]) for i in range(2)]
        gi = [at(f"gi{i}", 49152 + 2048 * i, [P, T]) for i in range(2)]
        gt = [at(f"gt{i}", 53248 + 2048 * i, [P, T]) for i in range(2)]
        wab_raw = at("wab_raw", 57344, [P, KD, 2, P])
        wab_hi = [at(f"wab_hi{i}", 65536 + 1024 * i, [P, 2, P], F32R) for i in range(2)]
        wab_lo = [at(f"wab_lo{i}", 67584 + 1024 * i, [P, 2, P], F32R) for i in range(2)]
        xa_hi = [at(f"xa_hi{i}", 69632 + 2048 * i, [P, T], F32R) for i in range(2)]
        xa_lo = [at(f"xa_lo{i}", 73728 + 2048 * i, [P, T], F32R) for i in range(2)]
        asq = [at(f"asq{i}", 77824 + 2048 * i, [P, T]) for i in range(2)]
        q_hi = at("q_hi", 65536, [P, T], F32R)
        q_lo = at("q_lo", 67584, [P, T], F32R)
        k_hi = at("k_hi", 69632, [P, T], F32R)
        k_lo = at("k_lo", 71680, [P, T], F32R)
        v_hi = at("v_hi", 73728, [P, TT, 2 * P], F32R)
        v_lo = at("v_lo", 77824, [P, TT, 2 * P], F32R)
        e_f = [at(f"e_f{i}", 81920 + 10240 * i, [P, NS]) for i in range(2)]
        e_lo = [at(f"e_lo{i}", 81920 + 10240 * i, [P, NS], F32R) for i in range(2)]
        e_hi = [at(f"e_hi{i}", 87040 + 10240 * i, [P, NS], F32R) for i in range(2)]
        decay = at("decay", 102400, [P, T], F32R)
        fx_a = at("fx_a", 98304, [HEADS, T])
        fx_b = at("fx_b", 100352, [HEADS, T])
        fx_c = at("fx_c", 106496, [HEADS, T])
        vt = at("vt", 108544, [P, T])
        mx_hi = at("mx_hi", 65536, [P, KD, T], F32R)
        mx_lo = at("mx_lo", 81920, [P, KD, T], F32R)
        sg = tmp[0:3]
        mx = tmp[3]

        bank = [ctx.enter_context(nc.psum_tensor(f"bank{i}", [P, T], F32)) for i in range(8)]
        BS = 6

        x_loaded = sig("x_loaded")
        c_loaded = sig("c_loaded")
        vec_loaded = sig("vec_loaded", 16, 16)
        wf_loaded = sig("wf_loaded", 16)
        wab_loaded = sig("wab_loaded", 16)
        raw_loaded = [sig(f"raw_loaded{i}", 16 * UNITS // RAW) for i in range(RAW)]
        ada0_loaded = [sig(f"ada0_loaded{i}") for i in range(16 // G0)]
        ada_loaded = [sig(f"ada_loaded{i}", 16 * 36) for i in range(2)]
        fin_ready = sig("fin_ready")
        out_stored = sig("out_stored")
        consts = sig("consts")
        consts_v = sig("consts_v")
        silu_c = sig("silu_c")
        unit_hi = sig("unit_hi", UNITS)
        unit_lo = sig("unit_lo", UNITS)
        unit_done = sig("unit_done", UNITS)
        ada_done = sig("ada_done", 72, 16)
        mod_set = sig("mod_set", 3, 1)
        nscale_set = sig("nscale_set", 3, 1)
        gate_set = sig("gate_set", 3)
        x_ready = sig("x_ready", 24, 0)
        sq_ready = sig("sq_ready", 24, 8)
        sqsum_ready = sig("sqsum_ready", 21, 7)
        sumsq = sig("sumsq", 3, 1)
        ln_ready = sig("ln_ready", 3, 1)
        rstd_ready = sig("rstd_ready", 3, 1)
        xr_ready = sig("xr_ready", 24, 0)
        hf_ready = sig("hf_ready", 24, 0)
        hh_ready = sig("hh_ready", 24, 0)
        hl_ready = sig("hl_ready", 24, 0)
        silu_ready = sig("silu_ready", 2 * KF)
        g_ready = sig("g_ready", 2 * KF)
        gh_ready = sig("gh_ready", 2 * KF)
        gl_ready = sig("gl_ready", 2 * KF)
        down_done = sig("down_done", 2 * TILE_ENDS)
        wfh = sig("wfh", 1)
        wfl = sig("wfl", 1)
        sp_step = sig("sp_step", 14)
        sp_exp = sig("sp_exp", 2)
        sp_set = sig("sp_set", 2)
        xa0_ready = sig("xa0_ready", KD)
        conv = sig("conv", 3 * KD)
        xah = sig("xah", KD)
        xal = sig("xal", KD)
        gelu_ready = sig("gelu_ready", KD)
        wabh = sig("wabh", KD)
        wabl = sig("wabl", KD)
        gates_done = sig("gates_done", KD)
        r_ready = sig("r_ready", KD)
        i_ready = sig("i_ready", KD)
        t_ready = sig("t_ready", KD)
        a_ready = sig("a_ready", KD)
        ix_ready = sig("ix_ready", KD)
        asq_ready = sig("asq_ready", KD)
        s_ready = sig("s_ready", KD)
        sqrt_ready = sig("sqrt_ready", KD)
        u_ready = sig("u_ready", KD)
        scan_ready = sig("scan_ready", KD)
        ya_ready = sig("ya_ready", KD)
        yah = sig("yah", KD)
        yal = sig("yal", KD)
        foxf_done = sig("foxf_done", 1)
        fx_step = sig("fx_step", 3)
        fx_act = sig("fx_act", 3)
        nch = sig("nch", 2)
        ncl = sig("ncl", 1)
        qh = sig("qh", PAIRS)
        ql = sig("ql", PAIRS)
        kh = sig("kh", PAIRS)
        kl = sig("kl", PAIRS)
        vt_ready = sig("vt_ready", PAIRS)
        vt_done = sig("vt_done", PAIRS)
        vh = sig("vh", PAIRS)
        vl = sig("vl", PAIRS)
        v_zero = sig("v_zero", 2)
        z_done = sig("z_done", 3 * 2 * PAIRS)
        abs_ready = sig("abs_ready", 3 * HEADS)
        exp_ready = sig("exp_ready", HEADS)
        lnp_ready = sig("lnp_ready", HEADS)
        sp_ready = sig("sp_ready", 3 * HEADS)
        sph = sig("sph", HEADS)
        spl = sig("spl", HEADS)
        suf_done = sig("suf_done", 3 * 2 * PAIRS)
        w_ready = sig("w_ready", 3 * HEADS)
        eh = sig("eh", HEADS)
        el = sig("el", HEADS)
        max_ready = sig("max_ready", TT * HEADS)
        p_ready = sig("p_ready", TT * HEADS)
        rs_ready = sig("rs_ready", HEADS)
        pn_ready = sig("pn_ready", TT * HEADS)
        ph = sig("ph", 3 * HEADS)
        pl = sig("pl", 3 * HEADS)
        pv_head = sig("pv_head", 2 * PAIRS)
        ybh = sig("ybh", PAIRS)
        ybl = sig("ybl", PAIRS)
        sg_ready = sig("sg_ready", 3 * KD)
        mx_step = sig("mx_step", 5 * KD)
        mxh = sig("mxh", KD)
        mxl = sig("mxl", KD)

        block = ctx.enter_context(nc.Block())

        @block.sync
        def _(sp):
            def load_unit(l, u, idx=None):
                sp.wait_ge(unit_lo.sem, unit_lo.at(l, u - RAW + 1))
                idx = l * UNITS + u if idx is None else idx
                sp.dma_start(raw[u % RAW][:, :, :], w_units[idx]).then_inc(raw_loaded[u % RAW].sem, 16)

            def load_ada(l, a):
                sp.wait_ge(ada_done.sem, ada_done.at(l, a - 1))
                sp.dma_start(ada[a % 2][:, :], ada_w[l * 72 + a + 16]).then_inc(ada_loaded[a % 2].sem, 16)

            sp.dma_start(c_act[:, :], c_rows).then_inc(c_loaded.sem, 16)
            sp.dma_start(vec[:, :], vecs[0]).then_inc(vec_loaded.sem, 16)
            for n in range(0, KD, 2):
                sp.dma_start(x[:, n:n + 2, :], x_in[n:n + 2].rearrange("n p t -> p n t")).then_inc(x_loaded.sem, 16)
            for g in range(16 // G0):
                sp.dma_start(ada0[g][:, :, :], ada_w[G0 * g:G0 * g + G0].rearrange("n p t -> p n t"))\
                    .then_inc(ada0_loaded[g].sem, 16)
                if 2 <= g < 2 + RAW:
                    sp.dma_start(raw[g - 2][:, :, :], w_units[g - 2]).then_inc(raw_loaded[g - 2].sem, 16)
            with sp.Fori(0, DEPTH) as l:
                for u in range(RAW, UNITS + RAW):
                    load_unit(l, u)
                    if u == 4:
                        sp.dma_start(wf_raw[:, :, :], wf[l]).then_inc(wf_loaded.sem, 16)
                    if 4 <= u < 48:
                        load_ada(l, u - 4)
                    for m in range(12):
                        if u == 49 + m * 4 // 3:
                            load_ada(l, 44 + m)
                    if u == U_RG + 4:
                        sp.wait_ge(unit_done.sem, unit_done.at(l, U_RG))
                        sp.dma_start(wab_raw[:, :, :, :], wab[l]).then_inc(wab_loaded.sem, 16)
                    if u == U_FFN[1] + 1:
                        sp.wait_ge(sg_ready.sem, sg_ready.at(l, 3 * KD))
                        sp.dma_start(vec[:, :], vecs[l + 1]).then_inc(vec_loaded.sem, 16)
                    if u == U_FFN[1] + 5:
                        sp.wait_ge(unit_done.sem, unit_done.at(l, U_WO + KD))
                    if U_FFN[1] + 10 <= u < U_FFN[1] + 26:
                        load_ada(l, 56 + u - U_FFN[1] - 10)
            for u in range(RAW, AHEAD):
                load_unit(DEPTH, u, u)
            for n in range(0, KD, 2):
                sp.wait_ge(fin_ready.sem, n + 2)
                sp.dma_start(out[n:n + 2].rearrange("n p t -> p n t"), fin[n // 2][:, :, :])\
                    .then_inc(out_stored.sem, 16)
            sp.wait_ge(out_stored.sem, 16 * KD // 2)

        @block.gpsimd
        def _(gp):
            def const(i, fn):
                if i:
                    gp.wait_ge(consts.sem, i)
                fn().then_inc(consts.sem, 1)
            f = tmp
            sel = lambda dst, src, op, fill, b, cm, st: nc.gpsimd.affine_select(
                out=dst, in_=src, compare_op=op, fill=fill, base=b, pattern=[[st, P]], channel_multiplier=cm)
            const(0, lambda: nc.gpsimd.memset(ident[:, :], 0.0))
            const(1, lambda: sel(ident[:, :], ident[:, :], ALU.not_equal, 1.0, 0, 1, -1))
            const(2, lambda: nc.gpsimd.memset(f[0][:, 0:128], -1.0))
            const(3, lambda: sel(f[0][:, 128:256], f[0][:, 0:128], ALU.is_ge, 0.0, 0, 1, -1))
            const(4, lambda: nc.gpsimd.memset(f[1][:, 0:128], 0.0))
            const(5, lambda: sel(f[1][:, 128:256], f[1][:, 0:128], ALU.is_gt, NEG, 0, -1, 1))
            const(6, lambda: sel(f[1][:, 256:384], f[1][:, 0:128], ALU.is_ge, NEG, 0, 1, -1))
            const(7, lambda: nc.gpsimd.memset(f[0][:, 256:384], 1.0))

            def lo(l, u):
                gp.wait_ge(unit_hi.sem, unit_hi.at(l, u + 1))
                s = u % RING
                nc.gpsimd.tensor_tensor(w_lo[s][:, :, :], raw[u % RAW][:, :, :], w_hi[s][:, :, :].bitcast(F32),
                                        ALU.subtract).then_inc(unit_lo.sem, 1)

            def wab_lo_part(l, c):
                gp.wait_ge(wabh.sem, wabh.at(l, c + 1))
                nc.gpsimd.tensor_tensor(wab_lo[c % 2][:, :, :], wab_raw[:, c, :, :],
                                        wab_hi[c % 2][:, :, :].bitcast(F32), ALU.subtract).then_inc(wabl.sem, 1)

            with gp.Fori(0, DEPTH) as l:
                for u in range(UNITS):
                    lo(l, u)
                    if U_RG + 3 <= u < U_RG + 3 + 2 * KD and (u - U_RG) % 2 == 1:
                        wab_lo_part(l, (u - U_RG - 3) // 2)
            for u in range(AHEAD):
                lo(DEPTH, u)

        @block.scalar
        def _(act):
            A = nc.scalar.activation

            def tick(l, u):
                n = u + AHEAD
                slot = n % RAW
                act.wait_ge(raw_loaded[slot].sem, raw_loaded[slot].at(l, 16 * (n // RAW + 1)))
                if n >= RING:
                    act.wait_ge(unit_done.sem, unit_done.at(l, n - RING + 1))
                A(w_hi[n % RING][:, :, :], raw[slot][:, :, :], ACT.Copy).then_inc(unit_hi.sem, 1)

            def square(l, m, n):
                if n >= 3:
                    act.wait_ge(sqsum_ready.sem, sqsum_ready.at(l, 7 * m + n - 2))
                A((tmp[n % 2] if n else sqsum)[:, :], x[:, n, :], ACT.Square).then_inc(sq_ready.sem, 1)

            def norm(l, m):
                nc.scalar.preload_act_table_set("natural_log_exp_and_others")
                act.wait_ge(sumsq.sem, sumsq.at(l, m + 1))
                A(rstd[:, :], bank[BS][:, :], ACT.Ln, bias=eps_col[:, 0:1], scale=1.0 / D).then_inc(ln_ready.sem, 1)
                act.wait_ge(ln_ready.sem, ln_ready.at(l, m + 1))
                A(rstd[:, :], rstd[:, :], ACT.Exp, scale=-0.5).then_inc(rstd_ready.sem, 1)

            def h_round(l, m, group):
                act.wait_ge(nscale_set.sem, nscale_set.at(l, m + 1))
                for k in range(KD):
                    j = 8 * (m + 1) + k
                    act.wait_ge(xr_ready.sem, xr_ready.at(l, j + 1))
                    if k >= 2:
                        act.wait_ge(hl_ready.sem, hl_ready.at(l, j - 1))
                    A(tmp[2 + k % 2][:, :], tmp[k % 2][:, :], ACT.Identity,
                      bias=mod[:, 24 * group + k:24 * group + k + 1],
                      scale=nscale[:, group, k:k + 1]).then_inc(hf_ready.sem, 1)
                    A(h_hi[:, k, :], tmp[k % 2][:, :], ACT.Identity, bias=mod[:, 24 * group + k:24 * group + k + 1],
                      scale=nscale[:, group, k:k + 1]).then_inc(hh_ready.sem, 1)

            def ffn(l, s):
                u0 = U_FFN[s]
                for f in range(KF):
                    tick(l, u0 + 2 * f)
                    tick(l, u0 + 2 * f + 1)
                    if f:
                        g_round(l, s, f - 1)
                    act.wait_ge(unit_done.sem, unit_done.at(l, u0 + 2 * f + 2))
                    if f >= 2:
                        act.wait_ge(g_ready.sem, g_ready.at(l, s * KF + f - 1))
                    A(tmp[f % 2][:, :], bank[2 * (f % 2)][:, :], ACT.Silu).then_inc(silu_ready.sem, 1)
                tick(l, u0 + 2 * KF)
                g_round(l, s, KF - 1)
                u = 2 * KF + 1
                for n in range(KD):
                    while u < 2 * KF + ((n + 1) * KF + UB - 1) // UB:
                        tick(l, u0 + u)
                        u += 1
                    act.wait_ge(x_ready.sem, x_ready.at(l, 16 * s + n + 1))
                    square(l, 2 * s, n)

            def g_round(l, s, f):
                act.wait_ge(g_ready.sem, g_ready.at(l, s * KF + f + 1))
                A(g_hi[:, f, :], tmp[2 + f % 2][:, :], ACT.Copy).then_inc(gh_ready.sem, 1)

            def rg_1(l, c):
                u = U_RG + 2 * c
                if c % 2 or c == 0:
                    tick(l, u)
                act.wait_ge(unit_done.sem, unit_done.at(l, u + 1))
                if c >= 2:
                    act.wait_ge(ix_ready.sem, ix_ready.at(l, c - 1))
                A(xa[c % 2][:, :], bank[2 * (c % 2)][:, :], ACT.Identity, bias=vec[:, V_CONVB + c:V_CONVB + c + 1],
                  scale=vec[:, V_CONVW + 24 + c:V_CONVW + 25 + c]).then_inc(xa0_ready.sem, 1)
                tick(l, u + 1)
                if c == 0:
                    act.wait_ge(wab_loaded.sem, wab_loaded.at(l, 16))
                if c >= 2:
                    act.wait_ge(gates_done.sem, gates_done.at(l, c - 1))
                A(wab_hi[c % 2][:, :, :], wab_raw[:, c, :, :], ACT.Copy).then_inc(wabh.sem, 1)
                act.wait_ge(unit_done.sem, unit_done.at(l, u + 2))
                if c >= 4:
                    act.wait_ge(yal.sem, yal.at(l, c - 3))
                A(gel[c % 4][:, :], bank[2 * (c % 2) + 1][:, :], ACT.Gelu_apprx_tanh).then_inc(gelu_ready.sem, 1)

            def rg_2(l, c0, nxt):
                both = (c0, c0 + 1)
                tick(l, U_RG + 2 * c0 + 4)
                nc.scalar.preload_act_table_set("sigmoid_and_others")
                for c in both:
                    s, b = c % 2, 4 + 2 * (c % 2)
                    act.wait_ge(gates_done.sem, gates_done.at(l, c + 1))
                    if c >= 2:
                        act.wait_ge(scan_ready.sem, scan_ready.at(l, c - 1))
                    A(gr[s][:, :], bank[b][:, :], ACT.Sigmoid, bias=vec[:, V_BA + c:V_BA + c + 1])\
                        .then_inc(r_ready.sem, 1)
                    A(gi[s][:, :], bank[b + 1][:, :], ACT.Sigmoid, bias=vec[:, V_BX + c:V_BX + c + 1])\
                        .then_inc(i_ready.sem, 1)
                for c in both:
                    if c == 0:
                        act.wait_ge(sp_set.sem, sp_set.at(l, 2))
                    act.wait_ge(r_ready.sem, r_ready.at(l, c + 1))
                    if c >= 2:
                        act.wait_ge(ya_ready.sem, ya_ready.at(l, c - 1))
                    A(gt[c % 2][:, :], gr[c % 2][:, :], ACT.Tanh, scale=pos_sp[:, c:c + 1]).then_inc(t_ready.sem, 1)
                nc.scalar.preload_act_table_set("natural_log_exp_and_others")
                for c in both:
                    act.wait_ge(t_ready.sem, t_ready.at(l, c + 1))
                    A(gr[c % 2][:, :], gr[c % 2][:, :], ACT.Exp, scale=neg_sp[:, c:c + 1]).then_inc(a_ready.sem, 1)
                if c0 == 0:
                    act.wait_ge(fx_step.sem, fx_step.at(l, 1))
                    A(fx_b[:, :], fx_a[:, :], ACT.Abs).then_inc(fx_act.sem, 1)
                    act.wait_ge(fx_act.sem, fx_act.at(l, 1))
                    A(fx_b[:, :], fx_b[:, :], ACT.Exp, scale=-1.0).then_inc(fx_act.sem, 1)
                    act.wait_ge(fx_act.sem, fx_act.at(l, 2))
                    A(fx_b[:, :], fx_b[:, :], ACT.Ln, bias=one_col[0:HEADS, 0:1]).then_inc(fx_act.sem, 1)
                nc.scalar.preload_act_table_set("sqrt_and_others")
                for c in both:
                    act.wait_ge(s_ready.sem, s_ready.at(l, c + 1))
                    A(gt[c % 2][:, :], gt[c % 2][:, :], ACT.Sqrt).then_inc(sqrt_ready.sem, 1)
                nc.scalar.preload_act_table_set(nxt)

            def q_round(l, p):
                u = U_QKV + 3 * p
                if p:
                    tick(l, u)
                act.wait_ge(unit_done.sem, unit_done.at(l, u + 1))
                if p:
                    act.wait_ge(z_done.sem, z_done.at(l, 6 * p))
                A(q_hi[:, :], bank[QKV_BANK(p, 0)][:, :], ACT.Copy, scale=HD ** -0.5).then_inc(qh.sem, 1)

            def k_round(l, p):
                u = U_QKV + 3 * p + 1
                tick(l, u)
                act.wait_ge(unit_done.sem, unit_done.at(l, u + 1))
                A(k_hi[:, :], bank[QKV_BANK(p, 1)][:, :], ACT.Copy).then_inc(kh.sem, 1)

            def v_copy(l, p):
                u = U_QKV + 3 * p + 2
                tick(l, u)
                act.wait_ge(unit_done.sem, unit_done.at(l, u + 1))
                if p:
                    act.wait_ge(vt_done.sem, vt_done.at(l, p))
                A(vt[:, :], bank[QKV_BANK(p, 2)][:, :], ACT.Copy).then_inc(vt_ready.sem, 1)

            def v_round(l, p):
                act.wait_ge(vt_done.sem, vt_done.at(l, p + 1))
                if p:
                    act.wait_ge(pv_head.sem, pv_head.at(l, 2 * p))
                if p == 0:
                    act.wait_ge(v_zero.sem, v_zero.at(l, 1))
                src = bank[7][:, :].rearrange("p (j e d) -> p j e d", j=TT, e=2)
                for e in range(2):
                    i = A(v_hi[:, :, e * (P + HD):e * (P + HD) + HD], src[:, :, e, :], ACT.Copy)
                i.then_inc(vh.sem, 1)

            def sb_1(l, p, e):
                n = 2 * p + e
                if n >= 2:
                    act.wait_ge(pv_head.sem, pv_head.at(l, n - 1))
                for c, (o, w) in enumerate(CHUNK):
                    act.wait_ge(z_done.sem, z_done.at(l, 3 * n + c + 1))
                    A(e_f[e][:, o:o + w], bank[ZB[e][c]][:, 0:w], ACT.Abs).then_inc(abs_ready.sem, 1)
                act.wait_ge(abs_ready.sem, abs_ready.at(l, 3 * n + 3))
                A(e_f[e][:, :], e_f[e][:, :], ACT.Exp, scale=-1.0).then_inc(exp_ready.sem, 1)
                act.wait_ge(exp_ready.sem, exp_ready.at(l, n + 1))
                A(e_f[e][:, :], e_f[e][:, :], ACT.Ln, bias=one_col[:, 0:1]).then_inc(lnp_ready.sem, 1)

            def sb_2(l, p, e):
                n = 2 * p + e
                for c, (o, w) in enumerate(CHUNK):
                    act.wait_ge(suf_done.sem, suf_done.at(l, 3 * n + 3))
                    A(e_f[e][:, o:o + w], bank[ZB[e][c]][:, 0:w], ACT.Exp).then_inc(w_ready.sem, 1)

            def fx_1(l, p, e):
                n = 2 * (p - 4) + e
                act.wait_ge(max_ready.sem, max_ready.at(l, TT * n + TT))
                for i in range(TT):
                    b, o = FX_AT[i]
                    A(e_f[e][:, 512 * b + o:512 * b + o + P * (i + 1)], bank[ZB[e][b]][:, o:o + P * (i + 1)], ACT.Exp,
                      bias=negmax[:, e, i:i + 1], accum_out=psums[:, e, i:i + 1]).then_inc(p_ready.sem, 1)

            def fx_2(l, p, e):
                n = 2 * (p - 4) + e
                act.wait_ge(suf_done.sem, suf_done.at(l, 6 * p + 3 * e + 3))
                for c, (o, w) in enumerate(CHUNK):
                    A(e_hi[e][:, o:o + w], bank[ZB[e][c]][:, 0:w], ACT.Copy).then_inc(ph.sem, 1)

            def y_round(l, p):
                act.wait_ge(pv_head.sem, pv_head.at(l, 2 * p + 2))
                if p == 0:
                    act.wait_ge(yal.sem, yal.at(l, KD))
                A(yb_hi[:, p, :], bank[7][:, :], ACT.Copy).then_inc(ybh.sem, 1)

            def merge(l, n):
                u = U_MERGE + 5 * n
                for g in range(3):
                    tick(l, u + g)
                    act.wait_ge(unit_done.sem, unit_done.at(l, u + g + 1))
                    if n:
                        act.wait_ge(mx_step.sem, mx_step.at(l, 5 * n))
                    A(sg[g][:, :], bank[g][:, :], ACT.Sigmoid,
                      bias=vec[:, V_MERGEB + 8 * g + n:V_MERGEB + 8 * g + n + 1]).then_inc(sg_ready.sem, 1)
                tick(l, u + 3)
                tick(l, u + 4)
                act.wait_ge(mx_step.sem, mx_step.at(l, 5 * n + 5))
                A(mx_hi[:, n, :], mx[:, :], ACT.Copy).then_inc(mxh.sem, 1)

            act.wait_ge(c_loaded.sem, 16)
            A(c_act[:, :], c_act[:, :], ACT.Silu).then_inc(silu_c.sem, 1)
            act.wait_ge(consts.sem, 8)
            for dst, src in ((ident_r, ident[:, :]), (ntri_r, tmp[0][:, 128:256]), (nones_r, tmp[0][:, 0:128]),
                             (ones_r, tmp[0][:, 256:384]), (mask_sb, tmp[1][:, 128:256]),
                             (mask_fx, tmp[1][:, 256:384])):
                A(dst[:, :], src, ACT.Copy).then_inc(consts_v.sem, 1)
            A(pick[:, :], ident[:, 0:HEADS], ACT.Copy).then_inc(consts_v.sem, 1)
            act.wait_ge(consts_v.sem, 9)
            A(pick[QUAD:2 * QUAD, :], ident[QUAD:2 * QUAD, QUAD:QUAD + HEADS], ACT.Copy).then_inc(consts_v.sem, 1)
            act.wait_ge(consts_v.sem, 10)
            for n in range(KD):
                act.wait_ge(x_loaded.sem, 16 * KD // 2)
                square(0, -1, n)
            for u in range(-AHEAD, 0):
                tick(0, u)
            norm(0, -1)
            with act.Fori(0, DEPTH) as l:
                h_round(l, -1, 0)
                nc.scalar.preload_act_table_set("silu_and_others")
                ffn(l, 0)
                norm(l, 0)
                h_round(l, 0, 1)
                act.wait_ge(wf_loaded.sem, wf_loaded.at(l, 16))
                A(wf_hi[:, :, :], wf_raw[:, :, :], ACT.Copy).then_inc(wfh.sem, 1)
                act.wait_ge(sp_step.sem, sp_step.at(l, 1))
                A(spc[:, 1, :], spc[:, 0, :], ACT.Exp).then_inc(sp_exp.sem, 1)
                nc.scalar.preload_act_table_set("gelu_apprx_tanh_and_others")
                for c in range(0, KD, 2):
                    rg_1(l, c)
                    rg_1(l, c + 1)
                    rg_2(l, c, "gelu_apprx_tanh_and_others" if c + 2 < KD else "natural_log_exp_and_others")
                q_round(l, 0)
                k_round(l, 0)
                v_copy(l, 0)
                for p in range(PAIRS):
                    first, second = (sb_1, sb_2) if p < 4 else (fx_1, fx_2)
                    first(l, p, 0)
                    v_round(l, p)
                    if p + 1 < PAIRS:
                        first(l, p, 1)
                        q_round(l, p + 1)
                        second(l, p, 0)
                        second(l, p, 1)
                        k_round(l, p + 1)
                        y_round(l, p)
                        v_copy(l, p + 1)
                    else:
                        first(l, p, 1)
                        second(l, p, 0)
                        second(l, p, 1)
                        y_round(l, p)
                nc.scalar.preload_act_table_set("sigmoid_and_others")
                for n in range(KD):
                    merge(l, n)
                for n in range(KD):
                    tick(l, U_WO + n)
                    if n % 2 == 1:
                        for i in (n - 1, n):
                            act.wait_ge(x_ready.sem, x_ready.at(l, 8 + i + 1))
                            square(l, 1, i)
                norm(l, 1)
                h_round(l, 1, 2)
                nc.scalar.preload_act_table_set("silu_and_others")
                ffn(l, 1)
                norm(l, 2)
            act.wait_ge(nscale_set.sem, nscale_set.at(DEPTH, 0))
            for k in range(KD):
                act.wait_ge(xr_ready.sem, xr_ready.at(DEPTH, k + 1))
                A(fin[k // 2][:, k % 2, :], fin[k // 2][:, k % 2, :], ACT.Identity, bias=mod[:, k:k + 1],
                  scale=nscale[:, 0, k:k + 1]).then_inc(fin_ready.sem, 1)

        @block.vector
        def _(dve):
            V = nc.vector

            def ada_tile(l, a):
                col = (a + 16) % 72
                dve.wait_ge(ada_loaded[a % 2].sem, ada_loaded[a % 2].at(l, 16 * (a // 2 + 1)))
                V.tensor_tensor_reduce(ada[a % 2][:, :], ada[a % 2][:, :], c_act[:, :], 1.0, 0.0, ALU.mult, ALU.add,
                                       mod[:, col:col + 1]).then_inc(ada_done.sem, 1)

            def mod_bias(l, a1, c0, c1):
                dve.wait_ge(ada_done.sem, ada_done.at(l, a1))
                V.tensor_tensor(mod[:, c0:c1], mod[:, c0:c1], vec[:, V_ADAB + c0:V_ADAB + c1],
                                ALU.add).then_inc(mod_set.sem, 1)

            def scale_col(l, k, vnorm, group):
                dve.wait_ge(mod_set.sem, mod_set.at(l, k))
                V.scalar_tensor_tensor(out=nscale[:, group, :], in0=mod[:, 24 * group + 8:24 * group + 16], scalar=1.0,
                                       in1=vec[:, vnorm:vnorm + 8], op0=ALU.add,
                                       op1=ALU.mult).then_inc(nscale_set.sem, 1)

            def gate_col(l, s, group, half):
                V.tensor_scalar(gatec[:, :], mod[:, 24 * group + 16:24 * group + 24], 1.0, half, ALU.add,
                                ALU.mult).then_inc(gate_set.sem, 1)
                dve.wait_ge(gate_set.sem, gate_set.at(l, s + 1))

            def square_add(l, m, n):
                if n == 0:
                    return
                dve.wait_ge(sq_ready.sem, sq_ready.at(l, 8 * m + n + 1))
                if n > 1:
                    dve.wait_ge(sqsum_ready.sem, sqsum_ready.at(l, 7 * m + n - 1))
                V.tensor_tensor(sqsum[:, :], sqsum[:, :], tmp[n % 2][:, :], ALU.add).then_inc(sqsum_ready.sem, 1)

            def h_tiles(l, m):
                dve.wait_ge(rstd_ready.sem, rstd_ready.at(l, m + 1))

                def rest(k):
                    j = 8 * (m + 1) + k
                    dve.wait_ge(hh_ready.sem, hh_ready.at(l, j + 1))
                    V.tensor_tensor(h_lo[:, k, :], tmp[2 + k % 2][:, :], h_hi[:, k, :].bitcast(F32),
                                    ALU.subtract).then_inc(hl_ready.sem, 1)

                for k in range(KD):
                    if k >= 2:
                        dve.wait_ge(hh_ready.sem, hh_ready.at(l, 8 * (m + 1) + k - 1))
                    V.tensor_tensor(tmp[k % 2][:, :], x[:, k, :], rstd[:, :], ALU.mult).then_inc(xr_ready.sem, 1)
                    if k:
                        rest(k - 1)
                rest(KD - 1)

            def x_add(l, j, bnk, n):
                V.scalar_tensor_tensor(out=x[:, n, :], in0=bnk, scalar=gatec[:, n:n + 1], in1=x[:, n, :],
                                       op0=ALU.mult, op1=ALU.add).then_inc(x_ready.sem, 1)

            def ffn(l, s):
                u0 = U_FFN[s]
                tiles = (lambda u: [u] if u < 56 else []) if s == 0 else (
                    lambda u: [56 + u - 6] if 6 <= u < 22 else [])

                def gl(f):
                    dve.wait_ge(gh_ready.sem, gh_ready.at(l, s * KF + f + 1))
                    V.tensor_tensor(g_lo[:, f, :], tmp[2 + f % 2][:, :], g_hi[:, f, :].bitcast(F32),
                                    ALU.subtract).then_inc(gl_ready.sem, 1)

                for f in range(KF):
                    for u in (2 * f, 2 * f + 1):
                        for a in tiles(u):
                            ada_tile(l, a)
                    dve.wait_ge(silu_ready.sem, silu_ready.at(l, s * KF + f + 1))
                    if f >= 2:
                        dve.wait_ge(gl_ready.sem, gl_ready.at(l, s * KF + f - 1))
                    V.tensor_tensor(tmp[2 + f % 2][:, :], tmp[f % 2][:, :], bank[2 * (f % 2) + 1][:, :],
                                    ALU.mult).then_inc(g_ready.sem, 1)
                    if f:
                        gl(f - 1)
                gl(KF - 1)
                if s == 0:
                    ada_tiles = list(range(44, 56))
                    mod_bias(l, 8, 16, 24)
                    dve.wait_ge(mod_set.sem, mod_set.at(l, 1))
                    gate_col(l, 0, 0, 0.5)
                else:
                    gate_col(l, 2, 2, 0.5)
                    dve.wait_ge(vec_loaded.sem, vec_loaded.at(l, 16))
                    mod_bias(l, 72, 0, 16)
                    scale_col(l, 3, V_NORM1, 0)
                for n in range(KD):
                    if n in INSIDE:
                        dve.wait_ge(down_done.sem, down_done.at(l, s * TILE_ENDS + INSIDE.index(n) + 1))
                    else:
                        dve.wait_ge(unit_done.sem, unit_done.at(l, u0 + 2 * KF + (n + 1) * KF // UB))
                    x_add(l, 16 * s + n, bank[4 + n % 2][:, :], n)
                    square_add(l, 2 * s, n)
                    if s == 0:
                        for a in ada_tiles[2 * n:2 * n + 2]:
                            ada_tile(l, a)
                if s == 0:
                    mod_bias(l, 56, 24, 72)
                    scale_col(l, 2, V_NORM2, 1)
                    scale_col(l, 2, V_NORM3, 2)

            def rg_1(l, c):
                s = c % 2
                dve.wait_ge(xa0_ready.sem, xa0_ready.at(l, c + 1))
                for j in range(3):
                    if j:
                        dve.wait_ge(conv.sem, conv.at(l, 3 * c + j))
                    V.scalar_tensor_tensor(out=xa[s][:, 3 - j:T], in0=bank[2 * s][:, 0:T - 3 + j],
                                           scalar=vec[:, V_CONVW + 8 * j + c:V_CONVW + 8 * j + c + 1],
                                           in1=xa[s][:, 3 - j:T], op0=ALU.mult, op1=ALU.add).then_inc(conv.sem, 1)
                dve.wait_ge(conv.sem, conv.at(l, 3 * c + 3))
                if c >= 2:
                    dve.wait_ge(gates_done.sem, gates_done.at(l, c - 1))
                V.tensor_copy(xa_hi[s][:, :], xa[s][:, :]).then_inc(xah.sem, 1)
                dve.wait_ge(xah.sem, xah.at(l, c + 1))
                V.tensor_tensor(xa_lo[s][:, :], xa[s][:, :], xa_hi[s][:, :].bitcast(F32),
                                ALU.subtract).then_inc(xal.sem, 1)

            def rg_2(l, c0):
                both = (c0, c0 + 1)
                for c in both:
                    dve.wait_ge(i_ready.sem, i_ready.at(l, c + 1))
                    V.tensor_tensor(gi[c % 2][:, :], gi[c % 2][:, :], xa[c % 2][:, :], ALU.mult)\
                        .then_inc(ix_ready.sem, 1)
                for c in both:
                    s = c % 2
                    dve.wait_ge(a_ready.sem, a_ready.at(l, c + 1))
                    V.tensor_tensor(asq[s][:, :], gr[s][:, :], gr[s][:, :], ALU.mult).then_inc(asq_ready.sem, 1)
                    dve.wait_ge(asq_ready.sem, asq_ready.at(l, c + 1))
                    V.scalar_tensor_tensor(out=gt[s][:, :], in0=asq[s][:, :], scalar=1.0, in1=gt[s][:, :], op0=ALU.add,
                                           op1=ALU.mult).then_inc(s_ready.sem, 1)
                for c in both:
                    s, g = c % 2, c % 4
                    dve.wait_ge(ix_ready.sem, ix_ready.at(l, c + 1))
                    dve.wait_ge(sqrt_ready.sem, sqrt_ready.at(l, c + 1))
                    V.tensor_tensor(gi[s][:, :], gt[s][:, :], gi[s][:, :], ALU.mult).then_inc(u_ready.sem, 1)
                    dve.wait_ge(u_ready.sem, u_ready.at(l, c + 1))
                    V.tensor_tensor_scan(gt[s][:, :], gr[s][:, :], gi[s][:, :], 0.0, ALU.mult, ALU.add)\
                        .then_inc(scan_ready.sem, 1)
                    dve.wait_ge(scan_ready.sem, scan_ready.at(l, c + 1))
                    dve.wait_ge(gelu_ready.sem, gelu_ready.at(l, c + 1))
                    V.tensor_tensor(gel[g][:, :], gel[g][:, :], gt[s][:, :], ALU.mult).then_inc(ya_ready.sem, 1)
                    dve.wait_ge(ya_ready.sem, ya_ready.at(l, c + 1))
                    V.tensor_copy(ya_hi[:, c, :], gel[g][:, :]).then_inc(yah.sem, 1)
                    dve.wait_ge(yah.sem, yah.at(l, c + 1))
                    V.tensor_tensor(ya_lo[:, c, :], gel[g][:, :], ya_hi[:, c, :].bitcast(F32),
                                    ALU.subtract).then_inc(yal.sem, 1)

            def softplus_lambda(l):
                n = [0]

                def step(i):
                    i.then_inc(sp_step.sem, 1)
                    n[0] += 1
                    dve.wait_ge(sp_step.sem, sp_step.at(l, n[0]))
                lam = vec[:, V_LAM:V_LAM + 8]
                step(V.scalar_tensor_tensor(out=spc[:, 0, :], in0=lam, scalar=-1.0, in1=lam, op0=ALU.mult,
                                            op1=ALU.min))
                dve.wait_ge(sp_exp.sem, sp_exp.at(l, 1))
                e = spc[:, 1, :]
                step(V.tensor_scalar(spc[:, 2, :], e, 2.0, None, ALU.add))
                step(V.reciprocal(spc[:, 2, :], spc[:, 2, :]))
                step(V.tensor_tensor(spc[:, 2, :], spc[:, 2, :], e, ALU.mult))
                step(V.tensor_tensor(spc[:, 3, :], spc[:, 2, :], spc[:, 2, :], ALU.mult))
                step(V.tensor_scalar(spc[:, 4, :], spc[:, 3, :], 1.0 / 15, None, ALU.mult))
                for d in (13, 11, 9, 7, 5, 3):
                    step(V.scalar_tensor_tensor(out=spc[:, 4, :], in0=spc[:, 4, :], scalar=1.0 / d,
                                                in1=spc[:, 3, :], op0=ALU.add, op1=ALU.mult))
                step(V.scalar_tensor_tensor(out=spc[:, 4, :], in0=spc[:, 4, :], scalar=1.0, in1=spc[:, 2, :],
                                            op0=ALU.add, op1=ALU.mult))
                step(V.tensor_scalar(spc[:, 5, :], lam, -1.0, 0.0, ALU.mult, ALU.max))
                V.scalar_tensor_tensor(out=spc[:, 0, :], in0=spc[:, 4, :], scalar=2.0, in1=spc[:, 5, :],
                                       op0=ALU.mult, op1=ALU.add).then_inc(sp_exp.sem, 1)
                dve.wait_ge(sp_exp.sem, sp_exp.at(l, 2))
                V.tensor_scalar(neg_sp[:, :], spc[:, 0, :], -8.0, None, ALU.mult).then_inc(sp_set.sem, 1)
                V.tensor_scalar(pos_sp[:, :], spc[:, 0, :], 8.0, None, ALU.mult).then_inc(sp_set.sem, 1)

            def forget_1(l):
                dve.wait_ge(foxf_done.sem, foxf_done.at(l, 1))
                b = vec[0:HEADS, V_FOXB:V_FOXB + 1]
                V.tensor_scalar(fx_a[:, :], bank[7][0:HEADS, :], b, None, ALU.add).then_inc(fx_step.sem, 1)

            def forget_2(l):
                dve.wait_ge(fx_act.sem, fx_act.at(l, 1))
                V.memset(decay[:, :].bitcast(F32), 0.0).then_inc(nch.sem, 1)
                V.tensor_scalar(fx_a[:, :], fx_a[:, :], -1.0, 0.0, ALU.mult, ALU.max).then_inc(fx_step.sem, 1)
                dve.wait_ge(fx_step.sem, fx_step.at(l, 2))
                dve.wait_ge(fx_act.sem, fx_act.at(l, 3))
                V.tensor_tensor_scan(fx_c[:, :], fx_a[:, :], fx_b[:, :], 0.0, ALU.add, ALU.add)\
                    .then_inc(fx_step.sem, 1)
                dve.wait_ge(fx_step.sem, fx_step.at(l, 3))
                dve.wait_ge(nch.sem, nch.at(l, 1))
                V.tensor_copy(decay[0:HEADS, :], fx_c[:, :]).then_inc(nch.sem, 1)
                dve.wait_ge(nch.sem, nch.at(l, 2))
                V.tensor_tensor(decay[QUAD:QUAD + HEADS, :], fx_c[:, :], decay[0:HEADS, :].bitcast(F32),
                                ALU.subtract).then_inc(ncl.sem, 1)

            def q_rest(l, p):
                dve.wait_ge(qh.sem, qh.at(l, p + 1))
                V.scalar_tensor_tensor(out=q_lo[:, :], in0=bank[QKV_BANK(p, 0)][:, :], scalar=HD ** -0.5,
                                       in1=q_hi[:, :].bitcast(F32), op0=ALU.mult,
                                       op1=ALU.subtract).then_inc(ql.sem, 1)

            def k_rest(l, p):
                dve.wait_ge(kh.sem, kh.at(l, p + 1))
                V.tensor_tensor(k_lo[:, :], bank[QKV_BANK(p, 1)][:, :], k_hi[:, :].bitcast(F32),
                                ALU.subtract).then_inc(kl.sem, 1)

            def v_rest(l, p):
                if p == 0:
                    dve.wait_ge(v_zero.sem, v_zero.at(l, 2))
                dve.wait_ge(vh.sem, vh.at(l, p + 1))
                src = bank[7][:, :].rearrange("p (j e d) -> p j e d", j=TT, e=2)
                for e in range(2):
                    o = e * (P + HD)
                    i = V.tensor_tensor(v_lo[:, :, o:o + HD], src[:, :, e, :], v_hi[:, :, o:o + HD].bitcast(F32),
                                        ALU.subtract)
                i.then_inc(vl.sem, 1)

            def sb_softplus(l, p, e):
                n = 2 * p + e
                dve.wait_ge(lnp_ready.sem, lnp_ready.at(l, n + 1))
                for c, (o, w) in enumerate(CHUNK):
                    V.scalar_tensor_tensor(out=e_f[e][:, o:o + w], in0=bank[ZB[e][c]][:, 0:w], scalar=0.0,
                                           in1=e_f[e][:, o:o + w], op0=ALU.max,
                                           op1=ALU.add).then_inc(sp_ready.sem, 1)
                dve.wait_ge(sp_ready.sem, sp_ready.at(l, 3 * n + 3))
                V.tensor_copy(e_hi[e][:, :], e_f[e][:, :]).then_inc(sph.sem, 1)
                dve.wait_ge(sph.sem, sph.at(l, n + 1))
                V.tensor_tensor(e_lo[e][:, :], e_f[e][:, :], e_hi[e][:, :].bitcast(F32),
                                ALU.subtract).then_inc(spl.sem, 1)

            def sb_split(l, p, e):
                n = 2 * p + e
                dve.wait_ge(w_ready.sem, w_ready.at(l, 3 * n + 3))
                V.tensor_copy(e_hi[e][:, :], e_f[e][:, :]).then_inc(eh.sem, 1)
                dve.wait_ge(eh.sem, eh.at(l, n + 1))
                V.tensor_tensor(e_lo[e][:, :], e_f[e][:, :], e_hi[e][:, :].bitcast(F32),
                                ALU.subtract).then_inc(el.sem, 1)

            def fx_max(l, p, e):
                n = 2 * (p - 4) + e
                dve.wait_ge(pv_head.sem, pv_head.at(l, 2 * p + e - 1))
                dve.wait_ge(z_done.sem, z_done.at(l, 6 * p + 3 * e + 3))
                for i in range(TT):
                    b, o = FX_AT[i]
                    V.tensor_reduce(negmax[:, e, i:i + 1], bank[ZB[e][b]][:, o:o + P * (i + 1)], AX.X, ALU.max,
                                    negate=True).then_inc(max_ready.sem, 1)

            def fx_norm(l, p, e):
                n = 2 * (p - 4) + e
                dve.wait_ge(p_ready.sem, p_ready.at(l, TT * n + TT))
                V.reciprocal(rsums[:, e, :], psums[:, e, :]).then_inc(rs_ready.sem, 1)
                dve.wait_ge(rs_ready.sem, rs_ready.at(l, n + 1))
                for i in range(TT):
                    b, o = FX_AT[i]
                    t = e_f[e][:, 512 * b + o:512 * b + o + P * (i + 1)]
                    V.tensor_scalar(t, t, rsums[:, e, i:i + 1], None, ALU.mult).then_inc(pn_ready.sem, 1)

            def fx_split(l, p, e):
                n = 2 * (p - 4) + e
                for c, (o, w) in enumerate(CHUNK):
                    dve.wait_ge(ph.sem, ph.at(l, 3 * n + c + 1))
                    V.tensor_tensor(e_lo[e][:, o:o + w], bank[ZB[e][c]][:, 0:w], e_hi[e][:, o:o + w].bitcast(F32),
                                    ALU.subtract).then_inc(pl.sem, 1)

            def y_rest(l, p):
                dve.wait_ge(ybh.sem, ybh.at(l, p + 1))
                V.tensor_tensor(yb_lo[:, p, :], bank[7][:, :], yb_hi[:, p, :].bitcast(F32),
                                ALU.subtract).then_inc(ybl.sem, 1)

            def merge(l, n):
                u = U_MERGE + 5 * n
                m0 = 5 * n
                if n:
                    dve.wait_ge(mxl.sem, mxl.at(l, n))
                dve.wait_ge(sg_ready.sem, sg_ready.at(l, 3 * n + 3))
                dve.wait_ge(unit_done.sem, unit_done.at(l, u + 4))
                V.tensor_tensor(mx[:, :], sg[0][:, :], bank[3][:, :], ALU.mult).then_inc(mx_step.sem, 1)
                dve.wait_ge(unit_done.sem, unit_done.at(l, u + 5))
                for g in (1, 2):
                    V.tensor_tensor(sg[g][:, :], sg[g][:, :], bank[3 + g][:, :], ALU.mult).then_inc(mx_step.sem, 1)
                dve.wait_ge(mx_step.sem, mx_step.at(l, m0 + 2))
                V.tensor_tensor(mx[:, :], mx[:, :], sg[1][:, :], ALU.add).then_inc(mx_step.sem, 1)
                dve.wait_ge(mx_step.sem, mx_step.at(l, m0 + 4))
                V.tensor_tensor(mx[:, :], mx[:, :], sg[2][:, :], ALU.add).then_inc(mx_step.sem, 1)
                dve.wait_ge(mxh.sem, mxh.at(l, n + 1))
                V.tensor_tensor(mx_lo[:, n, :], mx[:, :], mx_hi[:, n, :].bitcast(F32),
                                ALU.subtract).then_inc(mxl.sem, 1)

            V.memset(eps_col[:, :], EPS).then_inc(consts_v.sem, 1)
            V.memset(one_col[:, :], 1.0).then_inc(consts_v.sem, 1)
            dve.wait_ge(silu_c.sem, 1)
            dve.wait_ge(vec_loaded.sem, 16)
            def ada_tile_0(a):
                g, i = divmod(a, G0)
                dve.wait_ge(ada0_loaded[g].sem, 16)
                V.tensor_tensor_reduce(ada0[g][:, i, :], ada0[g][:, i, :], c_act[:, :], 1.0, 0.0, ALU.mult, ALU.add,
                                       mod[:, a:a + 1]).then_inc(ada_done.sem, 1)
            for n in range(KD):
                square_add(0, -1, n)
                ada_tile_0(n)
            for a in range(KD, 16):
                ada_tile_0(a)
            mod_bias(0, 0, 0, 16)
            scale_col(0, 0, V_NORM1, 0)
            with dve.Fori(0, DEPTH) as l:
                h_tiles(l, -1)
                ffn(l, 0)
                h_tiles(l, 0)
                gate_col(l, 1, 1, 1.0)
                dve.wait_ge(wfh.sem, wfh.at(l, 1))
                V.tensor_tensor(wf_lo[:, :, :], wf_raw[:, :, :], wf_hi[:, :, :].bitcast(F32),
                                ALU.subtract).then_inc(wfl.sem, 1)
                softplus_lambda(l)
                for c in range(0, KD, 2):
                    rg_1(l, c)
                    if c == 0:
                        forget_1(l)
                    rg_1(l, c + 1)
                    rg_2(l, c)
                    if c == 0:
                        forget_2(l)
                q_rest(l, 0)
                k_rest(l, 0)
                V.memset(v_hi[:, :, :].bitcast(F32), 0.0).then_inc(v_zero.sem, 1)
                V.memset(v_lo[:, :, :].bitcast(F32), 0.0).then_inc(v_zero.sem, 1)
                for p in range(PAIRS):
                    if p < 4:
                        v_rest(l, p)
                        sb_softplus(l, p, 0)
                        sb_softplus(l, p, 1)
                    else:
                        fx_max(l, p, 0)
                        fx_max(l, p, 1)
                        v_rest(l, p)
                        fx_norm(l, p, 0)
                        fx_norm(l, p, 1)
                    if p + 1 < PAIRS:
                        q_rest(l, p + 1)
                    split = sb_split if p < 4 else fx_split
                    split(l, p, 0)
                    split(l, p, 1)
                    if p + 1 < PAIRS:
                        k_rest(l, p + 1)
                    y_rest(l, p)
                for n in range(KD):
                    merge(l, n)
                for n in range(KD):
                    dve.wait_ge(unit_done.sem, unit_done.at(l, U_WO + n + 1))
                    x_add(l, 8 + n, bank[WO_BANK(n)][:, :], n)
                    square_add(l, 1, n)
                h_tiles(l, 1)
                ffn(l, 1)
            dve.wait_ge(rstd_ready.sem, rstd_ready.at(DEPTH, 0))
            for k in range(KD):
                V.tensor_tensor(fin[k // 2][:, k % 2, :], x[:, k, :], rstd[:, :], ALU.mult).then_inc(xr_ready.sem, 1)

        @block.tensor
        def _(pe):
            def mm3(o, wh, wl, xh, xl, start, stop):
                nc.tensor.matmul(o, wh, xh, start=start, stop=False, skip_group_check=True)
                nc.tensor.matmul(o, wh, xl, start=False, stop=False, skip_group_check=True)
                return nc.tensor.matmul(o, wl, xh, start=False, stop=stop, skip_group_check=True)

            def unit(l, u, bnk, hi, lo):
                s = u % RING
                pe.wait_ge(unit_lo.sem, unit_lo.at(l, u + 1))
                for k in range(KD):
                    i = mm3(bnk, w_hi[s][:, k, :], w_lo[s][:, k, :], hi[:, k, :], lo[:, k, :], k == 0, k == KD - 1)
                i.then_inc(unit_done.sem, 1)

            def pair(l, u, b0, b1, hi, lo, ready=None, first=0):
                pe.wait_ge(unit_lo.sem, unit_lo.at(l, u + 2))
                for k in range(KD):
                    if ready:
                        pe.wait_ge(ready.sem, ready.at(l, first + k + 1))
                    for j, b in ((0, b0), (1, b1)):
                        s = (u + j) % RING
                        i = mm3(bank[b][:, :], w_hi[s][:, k, :], w_lo[s][:, k, :], hi[:, k, :], lo[:, k, :], k == 0,
                                k == KD - 1)
                        if k == KD - 1:
                            i.then_inc(unit_done.sem, 1)

            def sum_squares(l, m):
                pe.wait_ge(sqsum_ready.sem, sqsum_ready.at(l, 7 * m + 7))
                nc.tensor.matmul(bank[BS][:, :], ones_r[:, :].bitcast(F32), sqsum[:, :], start=True,
                                 stop=True).then_inc(sumsq.sem, 1)

            def ffn(l, s):
                u0 = U_FFN[s]
                for f in range(KF):
                    if f >= 2:
                        pe.wait_ge(g_ready.sem, g_ready.at(l, s * KF + f - 1))
                    pair(l, u0 + 2 * f, 2 * (f % 2), 2 * (f % 2) + 1, h_hi, h_lo,
                         hl_ready if f == 0 else None, 16 * s)
                for b in range(KD * KF):
                    n, k = divmod(b, KF)
                    u, j = divmod(b, UB)
                    if j == 0:
                        pe.wait_ge(unit_lo.sem, unit_lo.at(l, u0 + 2 * KF + u + 1))
                    if n == 0:
                        pe.wait_ge(gl_ready.sem, gl_ready.at(l, s * KF + k + 1))
                    if k == 0 and n >= 2:
                        pe.wait_ge(x_ready.sem, x_ready.at(l, 16 * s + n - 1))
                    sl = (2 * KF + u0 + u) % RING
                    i = mm3(bank[4 + n % 2][:, :], w_hi[sl][:, j, :], w_lo[sl][:, j, :], g_hi[:, k, :], g_lo[:, k, :],
                            k == 0, k == KF - 1)
                    if j == UB - 1:
                        i.then_inc(unit_done.sem, 1)
                    elif k == KF - 1:
                        i.then_inc(down_done.sem, 1)
                sum_squares(l, 2 * s)

            def gates(l, c):
                pe.wait_ge(xal.sem, xal.at(l, c + 1))
                pe.wait_ge(wabl.sem, wabl.at(l, c + 1))
                if c == 1:
                    pe.wait_ge(fx_step.sem, fx_step.at(l, 1))
                if c >= 2:
                    pe.wait_ge(i_ready.sem, i_ready.at(l, c - 1))
                for j in range(2):
                    i = mm3(bank[4 + 2 * (c % 2) + j][:, :], wab_hi[c % 2][:, j, :], wab_lo[c % 2][:, j, :],
                            xa_hi[c % 2][:, :], xa_lo[c % 2][:, :], True, True)
                i.then_inc(gates_done.sem, 1)

            def scores(l, p, e):
                r = slice(HD * e, HD * e + HD)
                n = 2 * p + e
                if p == 0:
                    if e == 0:
                        pe.wait_ge(i_ready.sem, i_ready.at(l, KD))
                    else:
                        pe.wait_ge(gelu_ready.sem, gelu_ready.at(l, KD))
                        pe.wait_ge(vt_ready.sem, vt_ready.at(l, 1))
                if e == 0:
                    pe.wait_ge(ql.sem, ql.at(l, p + 1))
                    pe.wait_ge(kl.sem, kl.at(l, p + 1))
                if p == 4 and e == 0:
                    pe.wait_ge(ncl.sem, ncl.at(l, 1))
                if p >= 1:
                    if p <= 4:
                        pe.wait_ge(w_ready.sem, w_ready.at(l, 3 * (n - 2) + 3))
                    else:
                        pe.wait_ge(pl.sem, pl.at(l, 3 * (n - 8 - 2) + 3))
                order = [0, 1, 3, 2] if p < 4 else [3, 2, 0, 1]
                for i in order:
                    b, o = (SB_AT if p < 4 else FX_AT)[i]
                    begins = o == 0
                    if p < 4:
                        w = T - P * i
                        dst = bank[ZB[e][b]][:, o:o + w]
                        mm3(dst, k_hi[r, P * i:P * i + P], k_lo[r, P * i:P * i + P], q_hi[r, P * i:T],
                            q_lo[r, P * i:T], begins, False)
                        last = nc.tensor.matmul(dst[:, 0:P], ident_r[:, :], mask_sb[:, :], start=False, stop=False,
                                                skip_group_check=True)
                    else:
                        w = P * (i + 1)
                        h = n - HEADS
                        dst = bank[ZB[e][b]][:, o:o + w]
                        mm3(dst, q_hi[r, P * i:P * i + P], q_lo[r, P * i:P * i + P], k_hi[r, 0:w], k_lo[r, 0:w],
                            begins, False)
                        nc.tensor.matmul(dst, pick[:, h:h + 1].to_broadcast([P, P]), decay[:, 0:w], start=False,
                                         stop=False, skip_group_check=True)
                        last = nc.tensor.matmul(dst[:, P * i:w], ident_r[:, :], mask_fx[:, :], start=False,
                                                stop=False, skip_group_check=True)
                    if (b == 0) or (b == 2) or o == 384:
                        last.then_inc(z_done.sem, 1)

            def suffix(l, p, e):
                pe.wait_ge(spl.sem, spl.at(l, 2 * p + e + 1))
                for i in (0, 1, 3, 2):
                    b, o = SB_AT[i]
                    for j in range(i, TT):
                        bj, oj = SB_AT[j]
                        w = T - P * j
                        dst = bank[ZB[e][b]][:, o + P * (j - i):o + P * (j - i) + w]
                        for src in (e_hi[e], e_lo[e]):
                            last = nc.tensor.matmul(dst, (ntri_r if i == j else nones_r)[:, :],
                                                    src[:, 512 * bj + oj:512 * bj + oj + w], start=False,
                                                    stop=False, skip_group_check=True)
                    if i != 1:
                        last.then_inc(suf_done.sem, 1)

            def turn(l, p, e):
                pe.wait_ge(pn_ready.sem, pn_ready.at(l, TT * (2 * (p - 4) + e) + TT))
                for j in (0, 1, 3, 2):
                    b, o = SB_AT[j]
                    for i in range(j, TT):
                        bi, oi = FX_AT[i]
                        src = 512 * bi + oi + P * j
                        last = nc.tensor.transpose(bank[ZB[e][b]][:, o + P * (i - j):o + P * (i - j) + P],
                                                   e_f[e][:, src:src + P], ident[:, :])
                    if j != 1:
                        last.then_inc(suf_done.sem, 1)

            def values(l, p, e):
                if e == 0:
                    pe.wait_ge(vl.sem, vl.at(l, p + 1))
                if p < 4:
                    pe.wait_ge(el.sem, el.at(l, 2 * p + e + 1))
                else:
                    pe.wait_ge(pl.sem, pl.at(l, 3 * (2 * (p - 4) + e) + 3))
                for j in range(TT):
                    b, o = SB_AT[j]
                    w = T - P * j
                    src = slice(512 * b + o, 512 * b + o + w)
                    i = mm3(bank[7][:, P * j:T], v_hi[:, j, e * P:e * P + P], v_lo[:, j, e * P:e * P + P],
                            e_hi[e][:, src], e_lo[e][:, src], e == 0 and j == 0, False)
                i.then_inc(pv_head.sem, 1)

            def turn_v(l, p):
                pe.wait_ge(vt_ready.sem, vt_ready.at(l, p + 1))
                if p:
                    pe.wait_ge(ybl.sem, ybl.at(l, p))
                for j in range(TT):
                    i = nc.tensor.transpose(bank[7][:, P * j:P * j + P], vt[:, P * j:P * j + P], ident[:, :])
                i.then_inc(vt_done.sem, 1)

            def qkv(l, p, j):
                if p == 0:
                    if j == 1:
                        pe.wait_ge(gelu_ready.sem, gelu_ready.at(l, KD - 1))
                    else:
                        pe.wait_ge(conv.sem, conv.at(l, 3 * (KD - 1 + j // 2)))
                else:
                    pe.wait_ge((vt_ready, ql, kl)[j].sem, (vt_ready, ql, kl)[j].at(l, p + (0 if j == 0 else 1)))
                unit(l, U_QKV + 3 * p + j, bank[QKV_BANK(p, j)][:, :], h_hi, h_lo)

            pe.wait_ge(consts_v.sem, 10)
            sum_squares(0, -1)
            with pe.Fori(0, DEPTH) as l:
                ffn(l, 0)
                pair(l, U_RG, 0, 1, h_hi, h_lo, hl_ready, 8)
                pe.wait_ge(wfl.sem, wfl.at(l, 1))
                for k in range(KD):
                    i = mm3(bank[7][0:HEADS, :], wf_hi[:, k, :], wf_lo[:, k, :], h_hi[:, k, :], h_lo[:, k, :], k == 0,
                            k == KD - 1)
                i.then_inc(foxf_done.sem, 1)
                for c in range(1, KD):
                    if c >= 2:
                        pe.wait_ge(conv.sem, conv.at(l, 3 * (c - 1)))
                    unit(l, U_RG + 2 * c, bank[2 * (c % 2)][:, :], h_hi, h_lo)
                    if c >= 2:
                        pe.wait_ge(gelu_ready.sem, gelu_ready.at(l, c - 1))
                    unit(l, U_RG + 2 * c + 1, bank[2 * (c % 2) + 1][:, :], h_hi, h_lo)
                    if c % 2:
                        gates(l, c - 1)
                        gates(l, c)
                qkv(l, 0, 0)
                qkv(l, 0, 1)
                qkv(l, 0, 2)
                for p in range(PAIRS):
                    nxt = p + 1 < PAIRS
                    middle = suffix if p < 4 else turn
                    scores(l, p, 0)
                    scores(l, p, 1)
                    turn_v(l, p)
                    if nxt:
                        qkv(l, p + 1, 0)
                    middle(l, p, 0)
                    middle(l, p, 1)
                    if nxt:
                        qkv(l, p + 1, 1)
                    values(l, p, 0)
                    values(l, p, 1)
                    if nxt:
                        qkv(l, p + 1, 2)
                pe.wait_ge(pl.sem, pl.at(l, 3 * HEADS))
                for n in range(KD):
                    u = U_MERGE + 5 * n
                    for g in range(3):
                        if n:
                            pe.wait_ge(sg_ready.sem, sg_ready.at(l, 3 * n - 2 + g))
                        unit(l, u + g, bank[g][:, :], h_hi, h_lo)
                    if n == 0:
                        pe.wait_ge(yal.sem, yal.at(l, KD))
                    if n:
                        pe.wait_ge(mx_step.sem, mx_step.at(l, 5 * n))
                    unit(l, u + 3, bank[3][:, :], ya_hi, ya_lo)
                    if n == 0:
                        pe.wait_ge(ybl.sem, ybl.at(l, PAIRS))
                    s = (u + 4) % RING
                    pe.wait_ge(unit_lo.sem, unit_lo.at(l, u + 5))
                    for j in range(KD):
                        i = mm3(bank[4 + j // 4][:, :], w_hi[s][:, j, :], w_lo[s][:, j, :], yb_hi[:, j, :],
                                yb_lo[:, j, :], j % 4 == 0, j % 4 == 3)
                    i.then_inc(unit_done.sem, 1)
                pe.wait_ge(sg_ready.sem, sg_ready.at(l, 3 * KD))
                for n in range(0, KD, 2):
                    if n == 2:
                        pe.wait_ge(mx_step.sem, mx_step.at(l, 5 * KD))
                    if n >= 4:
                        pe.wait_ge(x_ready.sem, x_ready.at(l, 8 + n - 2))
                    pair(l, U_WO + n, WO_BANK(n), WO_BANK(n + 1), mx_hi, mx_lo, mxl if n == 0 else None)
                sum_squares(l, 1)
                ffn(l, 1)


ZB = [(4, 5, 6), (1, 2, 3)]


def QKV_BANK(p, j):
    return j if p == 0 else 0


def WO_BANK(n):
    return n % 4


def _layout(inputs):
    import numpy as np
    g = {k: np.asarray(v, dtype=v.dtype) for k, v in inputs.items()}

    def cols(w):
        k, n = w.shape
        return w.reshape(k // P, P, n // P, P).transpose(2, 1, 0, 3)

    units = np.zeros((DEPTH * UNITS + RAW, P, UB, P), np.float32)
    for l in range(DEPTH):
        o = l * UNITS

        def ffn(u, w1, w3, w2):
            units[u:u + 2 * KF:2] = cols(w1)
            units[u + 1:u + 2 * KF:2] = cols(w3)
            d = cols(w2).transpose(0, 2, 1, 3).reshape(-1, UB, P, P)
            units[u + 2 * KF:u + FFN_UNITS] = d.transpose(0, 2, 1, 3)
        ffn(o + U_FFN[0], g["ffn1_w1"][l], g["ffn1_w3"][l], g["ffn1_w2"][l])
        ffn(o + U_FFN[1], g["ffn2_w1"][l], g["ffn2_w3"][l], g["ffn2_w2"][l])
        win = g["w_in"][l]
        a = cols(win[:, 0:2 * D])
        units[o + U_RG:o + U_QKV:2] = a[0:KD]
        units[o + U_RG + 1:o + U_QKV:2] = a[KD:2 * KD]
        for b in range(2):
            qkv = cols(win[:, 2 * D + 1536 * b:2 * D + 1536 * (b + 1)])
            for j in range(3):
                u = o + U_QKV + 12 * b + j
                units[u:u + 12:3] = qkv[4 * j:4 * j + 4]
        mg = cols(win[:, 2 * D + 3072 + HEADS:])
        for j in range(3):
            units[o + U_MERGE + j:o + U_WO:5] = mg[8 * j:8 * j + 8]
        units[o + U_MERGE + 3:o + U_WO:5] = cols(g["w_rg"][l])
        units[o + U_MERGE + 4:o + U_WO:5, :, 0:4] = cols(g["w_sb"][l])
        units[o + U_MERGE + 4:o + U_WO:5, :, 4:8] = cols(g["w_fox"][l])
        units[o + U_WO:o + U_FFN[1]] = cols(g["w_o"][l])

    def rows(w):
        return w.T.reshape(-1, P, w.shape[0])
    ada_w = np.concatenate([rows(g["ada_w"][l]) for l in range(DEPTH)] + [rows(g["final_ada_w"])])

    vecs = np.zeros((DEPTH + 1, P, NV), np.float32)

    def put(l, c, v):
        v = v.reshape(-1, P).T
        vecs[l, :, c:c + v.shape[1]] = v
    for l in range(DEPTH):
        for c, name in ((V_NORM1, "ffn1_norm"), (V_NORM2, "mix_norm"), (V_NORM3, "ffn2_norm"), (V_ADAB, "ada_b"),
                        (V_CONVW, "conv_w"), (V_CONVB, "conv_b"), (V_BA, "rg_ba"), (V_BX, "rg_bx"),
                        (V_LAM, "rg_lam"), (V_MERGEB, "merge_b")):
            put(l, c, g[name][l])
        vecs[l, 0:HEADS, V_FOXB] = g["fox_bf"][l]
    put(DEPTH, V_NORM1, g["final_norm"])
    put(DEPTH, V_ADAB, g["final_ada_b"])

    f0 = 2 * D + 3072
    wf = np.stack([g["w_in"][l][:, f0:f0 + HEADS].reshape(KD, P, HEADS).transpose(1, 0, 2) for l in range(DEPTH)])
    wab = np.zeros((DEPTH, P, KD, 2, P), np.float32)
    for j, name in enumerate(("rg_wa", "rg_wx")):
        w = g[name].reshape(DEPTH, KD, 2, HD, HD)
        for b in range(2):
            wab[:, b * HD:(b + 1) * HD, :, j, b * HD:(b + 1) * HD] = w[:, :, b].transpose(0, 2, 1, 3)
    return {
        "w_units": units, "ada_w": ada_w, "vecs": vecs, "wf": wf, "wab": wab,
        "c_rows": np.ascontiguousarray(np.broadcast_to(g["c"], (P, D))),
        "x_in": np.ascontiguousarray(g["x"][0].T).reshape(KD, P, T),
    }


def kernel(**inputs):
    import numpy as np
    import concourse.bacc as bacc
    from concourse.bass_utils import run_bass_kernel_spmd

    nc = bacc.Bacc("TRN2", target_bir_lowering=False, num_devices=1)
    arrays = {k: np.ascontiguousarray(v) for k, v in _layout(inputs).items()}
    args = {k: nc.dram_tensor(k, v.shape, mybir.dt.from_np(v.dtype), kind="ExternalInput").ap()
            for k, v in arrays.items()}
    y = nc.dram_tensor("y", (KD, P, T), F32, kind="ExternalOutput").ap()
    trunk(nc, out=y, **args)
    r = run_bass_kernel_spmd(nc, [arrays], core_ids=[0])
    return np.ascontiguousarray(r.results[0]["y"].reshape(D, T).T).reshape(1, T, D)
```

```python
from contextlib import ExitStack

import concourse.bass as bass
from concourse import mybir

F32 = mybir.dt.float32
F32R = mybir.dt.float32r
ALU = mybir.AluOpType
ACT = mybir.ActivationFunctionType
AX = mybir.AxisListType

P = 128
D = 1024
T = 512
DEPTH = 2
DFF = 2816
KD = D // P
KF = DFF // P
UB = 8
HEADS = 8
PAIRS = HEADS
HD = 64
TT = T // P
EPS = 1e-6
HALF = (slice(0, T // 2), slice(T // 2, T))
NEG = -(2.0 ** 100)

FFN_UNITS = 2 * KF + KF * KD // UB
U_FFN = (0, FFN_UNITS + 88)
U_RG = FFN_UNITS
U_QKV = U_RG + 2 * KD
U_MERGE = U_QKV + 3 * PAIRS
U_WO = U_MERGE + 5 * KD
UNITS = 2 * FFN_UNITS + 88
AHEAD = 3
RAW, RING = 2, 4
assert UNITS % RING == 0 and U_WO + KD == U_FFN[1]

V_NORM1, V_NORM2, V_NORM3 = 0, 8, 16
V_ADAB = 24
V_CONVW = 96
V_CONVB, V_BA, V_BX, V_LAM = 128, 136, 144, 152
V_MERGEB = 160
V_FOXB = 184
NV = 185

SB_AT = [(0, 0), (1, 0), (2, 0), (1, 384)]
FX_AT = [(1, 384), (2, 0), (1, 0), (0, 0)]
CHUNK = [(0, 512), (512, 512), (1024, 256)]
NS = 1280
SB_ORDER = (1, 2, 0)
PART = [slice(512, NS), slice(0, 512)]


INSIDE = [n for n in range(KD) if (n + 1) * KF % UB]
TILE_ENDS = len(INSIDE)
QUAD = 32
G0 = 2


class Signal:

    def __init__(self, sem, per_layer, before=0):
        self.sem, self.per_layer, self.before = sem, per_layer, before

    def at(self, l, k):
        assert k + self.before > 0
        return l * self.per_layer + (k + self.before)


def trunk(nc, w_units, ada_w, vecs, wf, wab, c_rows, x_in, out):
    with ExitStack() as ctx:
        def sb(name, shape, dt=F32):
            return ctx.enter_context(nc.sbuf_tensor(name, shape, dt))

        def sig(name, per_layer=0, before=0):
            return Signal(ctx.enter_context(nc.semaphore(name)), per_layer, before)

        x = sb("x", [P, KD, T])
        h_hi = sb("h_hi", [P, KD, T], F32R)
        h_lo = sb("h_lo", [P, KD, T], F32R)
        raw = [sb(f"raw{i}", [P, UB, P]) for i in range(RAW)]
        w_hi = [sb(f"w_hi{i}", [P, UB, P], F32R) for i in range(RING)]
        w_lo = [sb(f"w_lo{i}", [P, UB, P], F32R) for i in range(RING)]
        c_act = sb("c_act", [P, D])
        vec = sb("vec", [P, NV])
        mod = sb("mod", [P, 72])
        nscale = sb("nscale", [P, 3, KD])
        gatec = sb("gatec", [P, KD])
        spc = sb("spc", [P, 6, KD])
        neg_sp = sb("neg_sp", [P, KD])
        pos_sp = sb("pos_sp", [P, KD])
        negmax = sb("negmax", [P, 2, TT])
        psums = sb("psums", [P, 2, TT])
        rsums = sb("rsums", [P, 2, TT])
        eps_col = sb("eps_col", [P, 1])
        one_col = sb("one_col", [P, 1])
        ident = sb("ident", [P, P])
        ident_r = sb("ident_r", [P, P], F32R)
        pick = sb("pick", [P, HEADS], F32R)
        ones_r = sb("ones_r", [P, P], F32R)
        nones_r = sb("nones_r", [P, P], F32R)
        ntri_r = sb("ntri_r", [P, P], F32R)
        mask_sb = sb("mask_sb", [P, P], F32R)
        mask_fx = sb("mask_fx", [P, P], F32R)
        wf_raw = sb("wf_raw", [P, KD, HEADS])
        wf_hi = sb("wf_hi", [P, KD, HEADS], F32R)
        wf_lo = sb("wf_lo", [P, KD, HEADS], F32R)

        base = (nc.sbuf_base + 31) // 32 * 32
        ARENA = 110720
        sb("arena", [P, ARENA // 4])

        def at(name, offset, shape, dt=F32):
            size = 4
            for s in shape[1:]:
                size *= s
            assert offset + size <= ARENA, (name, offset + size)
            return nc.alloc_sbuf_tensor_at(name, shape, dt, offset=base + offset)

        g_hi = at("g_hi", 0, [P, KF, T], F32R)
        g_lo = at("g_lo", 45056, [P, KF, T], F32R)
        ada = [at(f"ada{i}", 90112 + 4096 * i, [P, D]) for i in range(2)]
        tmp = [at(f"tmp{i}", 98304 + 2048 * i, [P, T]) for i in range(4)]
        sqsum = at("sqsum", 102400, [P, T])
        rstd = at("rstd", 106496, [P, T])
        ada0 = [at(f"ada0_{i}", 4096 * G0 * i, [P, G0, D]) for i in range(16 // G0)]
        fin = [at(f"fin{i}", 4096 * i, [P, 2, T]) for i in range(KD // 2)]
        ya_hi = at("ya_hi", 0, [P, KD, T], F32R)
        ya_lo = at("ya_lo", 16384, [P, KD, T], F32R)
        yb_hi = at("yb_hi", 32768, [P, KD, T], F32R)
        yb_lo = at("yb_lo", 49152, [P, KD, T], F32R)
        xa = [at(f"xa{i}", 32768 + 2048 * i, [P, T]) for i in range(2)]
        gel = [at(f"gel{i}", 36864 + 2048 * i, [P, T]) for i in range(4)]
        gr = [at(f"gr{i}", 45056 + 2048 * i, [P, T]) for i in range(2)]
        gi = [at(f"gi{i}", 49152 + 2048 * i, [P, T]) for i in range(2)]
        gt = [at(f"gt{i}", 53248 + 2048 * i, [P, T]) for i in range(2)]
        wab_raw = at("wab_raw", 57344, [P, KD, 2, P])
        wab_hi = [at(f"wab_hi{i}", 65536 + 1024 * i, [P, 2, P], F32R) for i in range(2)]
        wab_lo = [at(f"wab_lo{i}", 67584 + 1024 * i, [P, 2, P], F32R) for i in range(2)]
        xa_hi = [at(f"xa_hi{i}", 69632 + 2048 * i, [P, T], F32R) for i in range(2)]
        xa_lo = [at(f"xa_lo{i}", 73728 + 2048 * i, [P, T], F32R) for i in range(2)]
        asq = [at(f"asq{i}", 77824 + 2048 * i, [P, T]) for i in range(2)]
        q_hi = at("q_hi", 65536, [P, T], F32R)
        q_lo = at("q_lo", 67584, [P, T], F32R)
        k_hi = at("k_hi", 69632, [P, T], F32R)
        k_lo = at("k_lo", 71680, [P, T], F32R)
        v_hi = at("v_hi", 73728, [P, TT, 2 * P], F32R)
        v_lo = at("v_lo", 77824, [P, TT, 2 * P], F32R)
        e_f = [at(f"e_f{i}", 81920 + 10240 * i, [P, NS]) for i in range(2)]
        e_lo = [at(f"e_lo{i}", 81920 + 10240 * i, [P, NS], F32R) for i in range(2)]
        e_hi = [at(f"e_hi{i}", 87040 + 10240 * i, [P, NS], F32R) for i in range(2)]
        decay = at("decay", 102400, [P, T], F32R)
        fx_a = at("fx_a", 98304, [HEADS, T])
        fx_b = at("fx_b", 100352, [HEADS, T])
        fx_c = at("fx_c", 106496, [HEADS, T])
        vt = at("vt", 108544, [P, T])
        mx_hi = at("mx_hi", 65536, [P, KD, T], F32R)
        mx_lo = at("mx_lo", 81920, [P, KD, T], F32R)
        sg = tmp[0:3]
        mx = tmp[3]

        bank = [ctx.enter_context(nc.psum_tensor(f"bank{i}", [P, T], F32)) for i in range(8)]
        BS = 6

        x_loaded = sig("x_loaded")
        c_loaded = sig("c_loaded")
        vec_loaded = sig("vec_loaded", 16, 16)
        wf_loaded = sig("wf_loaded", 16)
        wab_loaded = sig("wab_loaded", 16)
        raw_loaded = [sig(f"raw_loaded{i}", 16 * UNITS // RAW) for i in range(RAW)]
        ada0_loaded = [sig(f"ada0_loaded{i}") for i in range(16 // G0)]
        ada_loaded = [sig(f"ada_loaded{i}", 16 * 36) for i in range(2)]
        fin_ready = sig("fin_ready")
        out_stored = sig("out_stored")
        consts = sig("consts")
        consts_v = sig("consts_v")
        silu_c = sig("silu_c")
        unit_hi = sig("unit_hi", UNITS)
        unit_lo = sig("unit_lo", UNITS)
        unit_done = sig("unit_done", UNITS)
        ada_done = sig("ada_done", 72, 16)
        mod_set = sig("mod_set", 3, 1)
        nscale_set = sig("nscale_set", 3, 1)
        gate_set = sig("gate_set", 3)
        x_ready = sig("x_ready", 27)
        sq_ready = sig("sq_ready", 27, 9)
        sqsum_ready = sig("sqsum_ready", 24, 8)
        half_done = sig("half_done", 3)
        sumsq = sig("sumsq", 6, 2)
        ln_ready = sig("ln_ready", 6, 2)
        rstd_ready = sig("rstd_ready", 6, 2)
        xr_ready = sig("xr_ready", 48)
        hf_ready = sig("hf_ready", 48)
        hh_ready = sig("hh_ready", 48)
        hl_ready = sig("hl_ready", 48)
        silu_ready = sig("silu_ready", 2 * KF)
        g_ready = sig("g_ready", 2 * KF)
        gh_ready = sig("gh_ready", 2 * KF)
        gl_ready = sig("gl_ready", 2 * KF)
        down_done = sig("down_done", 2 * TILE_ENDS)
        wfh = sig("wfh", 1)
        wfl = sig("wfl", 1)
        sp_step = sig("sp_step", 14)
        sp_exp = sig("sp_exp", 2)
        sp_set = sig("sp_set", 2)
        xa0_ready = sig("xa0_ready", KD)
        conv = sig("conv", 3 * KD)
        xah = sig("xah", KD)
        xal = sig("xal", KD)
        gelu_ready = sig("gelu_ready", KD)
        wabh = sig("wabh", KD)
        wabl = sig("wabl", KD)
        gates_done = sig("gates_done", KD)
        r_ready = sig("r_ready", KD)
        i_ready = sig("i_ready", KD)
        t_ready = sig("t_ready", KD)
        a_ready = sig("a_ready", KD)
        ix_ready = sig("ix_ready", KD)
        asq_ready = sig("asq_ready", KD)
        s_ready = sig("s_ready", KD)
        sqrt_ready = sig("sqrt_ready", KD)
        u_ready = sig("u_ready", KD)
        scan_ready = sig("scan_ready", KD)
        ya_ready = sig("ya_ready", KD)
        yah = sig("yah", KD)
        yal = sig("yal", KD)
        foxf_done = sig("foxf_done", 1)
        fx_step = sig("fx_step", 3)
        fx_act = sig("fx_act", 3)
        nch = sig("nch", 2)
        ncl = sig("ncl", 1)
        qh = sig("qh", PAIRS)
        ql = sig("ql", PAIRS)
        kh = sig("kh", PAIRS)
        kl = sig("kl", PAIRS)
        vt_ready = sig("vt_ready", PAIRS)
        vt_done = sig("vt_done", PAIRS)
        vh = sig("vh", PAIRS)
        vl = sig("vl", PAIRS)
        v_zero = sig("v_zero", 2)
        z_done = sig("z_done", 3 * 2 * PAIRS)
        abs_ready = sig("abs_ready", 3 * HEADS)
        exp_ready = sig("exp_ready", HEADS)
        lnp_ready = sig("lnp_ready", 2 * HEADS)
        softplus = sig("softplus", 7 * HEADS)
        suf_done = sig("suf_done", 3 * 2 * PAIRS)
        w_ready = sig("w_ready", 3 * HEADS)
        eh = sig("eh", HEADS)
        el = sig("el", HEADS)
        max_ready = sig("max_ready", TT * HEADS)
        p_ready = sig("p_ready", TT * HEADS)
        rs_ready = sig("rs_ready", HEADS)
        pn_ready = sig("pn_ready", TT * HEADS)
        ph = sig("ph", 3 * HEADS)
        pl = sig("pl", 3 * HEADS)
        pv_head = sig("pv_head", 2 * PAIRS)
        ybh = sig("ybh", PAIRS)
        ybl = sig("ybl", PAIRS)
        sg_ready = sig("sg_ready", 3 * KD)
        mx_step = sig("mx_step", 5 * KD)
        mxh = sig("mxh", KD)
        mxl = sig("mxl", KD)

        block = ctx.enter_context(nc.Block())

        @block.sync
        def _(sp):
            def load_unit(l, u, index=None):
                sp.wait_ge(unit_lo.sem, unit_lo.at(l, u - RAW + 1))
                index = l * UNITS + u if index is None else index
                sp.dma_start(raw[u % RAW][:, :, :], w_units[index]).then_inc(raw_loaded[u % RAW].sem, 16)

            def load_ada(l, a):
                sp.wait_ge(ada_done.sem, ada_done.at(l, a - 1))
                sp.dma_start(ada[a % 2][:, :], ada_w[l * 72 + a + 16]).then_inc(ada_loaded[a % 2].sem, 16)

            sp.dma_start(c_act[:, :], c_rows).then_inc(c_loaded.sem, 16)
            sp.dma_start(vec[:, :], vecs[0]).then_inc(vec_loaded.sem, 16)
            for n in range(0, KD, 2):
                sp.dma_start(x[:, n:n + 2, :], x_in[n:n + 2].rearrange("n p t -> p n t")).then_inc(x_loaded.sem, 16)
            for g in range(16 // G0):
                sp.dma_start(ada0[g][:, :, :], ada_w[G0 * g:G0 * g + G0].rearrange("n p t -> p n t"))\
                    .then_inc(ada0_loaded[g].sem, 16)
                if 2 <= g < 2 + RAW:
                    sp.dma_start(raw[g - 2][:, :, :], w_units[g - 2]).then_inc(raw_loaded[g - 2].sem, 16)
            with sp.Fori(0, DEPTH) as l:
                for u in range(RAW, UNITS + RAW):
                    load_unit(l, u)
                    if u == 4:
                        sp.dma_start(wf_raw[:, :, :], wf[l]).then_inc(wf_loaded.sem, 16)
                    if 4 <= u < 48:
                        load_ada(l, u - 4)
                    for m in range(12):
                        if u == 49 + m * 4 // 3:
                            load_ada(l, 44 + m)
                    if u == U_RG + 4:
                        sp.wait_ge(unit_done.sem, unit_done.at(l, U_RG))
                        sp.dma_start(wab_raw[:, :, :, :], wab[l]).then_inc(wab_loaded.sem, 16)
                    if u == U_FFN[1] + 1:
                        sp.wait_ge(sg_ready.sem, sg_ready.at(l, 3 * KD))
                        sp.dma_start(vec[:, :], vecs[l + 1]).then_inc(vec_loaded.sem, 16)
                    if u == U_FFN[1] + 5:
                        sp.wait_ge(unit_done.sem, unit_done.at(l, U_WO + KD))
                    if U_FFN[1] + 10 <= u < U_FFN[1] + 26:
                        load_ada(l, 56 + u - U_FFN[1] - 10)
            for u in range(RAW, AHEAD):
                load_unit(DEPTH, u, u)
            for h in range(2):
                for n in range(0, KD, 2):
                    sp.wait_ge(fin_ready.sem, KD * h + n + 2)
                    sp.dma_start(out[n:n + 2, :, HALF[h]].rearrange("n p t -> p n t"), fin[n // 2][:, :, HALF[h]])\
                        .then_inc(out_stored.sem, 16)
            sp.wait_ge(out_stored.sem, 16 * KD)

        @block.gpsimd
        def _(gp):
            def const(i, fn):
                if i:
                    gp.wait_ge(consts.sem, i)
                fn().then_inc(consts.sem, 1)
            f = tmp
            sel = lambda dst, src, op, fill, b, cm, st: nc.gpsimd.affine_select(
                out=dst, in_=src, compare_op=op, fill=fill, base=b, pattern=[[st, P]], channel_multiplier=cm)
            const(0, lambda: nc.gpsimd.memset(ident[:, :], 0.0))
            const(1, lambda: sel(ident[:, :], ident[:, :], ALU.not_equal, 1.0, 0, 1, -1))
            const(2, lambda: nc.gpsimd.memset(f[0][:, 0:128], -1.0))
            const(3, lambda: sel(f[0][:, 128:256], f[0][:, 0:128], ALU.is_ge, 0.0, 0, 1, -1))
            const(4, lambda: nc.gpsimd.memset(f[1][:, 0:128], 0.0))
            const(5, lambda: sel(f[1][:, 128:256], f[1][:, 0:128], ALU.is_gt, NEG, 0, -1, 1))
            const(6, lambda: sel(f[1][:, 256:384], f[1][:, 0:128], ALU.is_ge, NEG, 0, 1, -1))
            const(7, lambda: nc.gpsimd.memset(f[0][:, 256:384], 1.0))

            def lo(l, u):
                gp.wait_ge(unit_hi.sem, unit_hi.at(l, u + 1))
                s = u % RING
                nc.gpsimd.tensor_tensor(w_lo[s][:, :, :], raw[u % RAW][:, :, :], w_hi[s][:, :, :].bitcast(F32),
                                        ALU.subtract).then_inc(unit_lo.sem, 1)

            def wab_lo_part(l, c):
                gp.wait_ge(wabh.sem, wabh.at(l, c + 1))
                nc.gpsimd.tensor_tensor(wab_lo[c % 2][:, :, :], wab_raw[:, c, :, :],
                                        wab_hi[c % 2][:, :, :].bitcast(F32), ALU.subtract).then_inc(wabl.sem, 1)

            with gp.Fori(0, DEPTH) as l:
                for u in range(UNITS):
                    lo(l, u)
                    if U_RG + 3 <= u < U_RG + 3 + 2 * KD and (u - U_RG) % 2 == 1:
                        wab_lo_part(l, (u - U_RG - 3) // 2)
            for u in range(AHEAD):
                lo(DEPTH, u)

        @block.scalar
        def _(act):
            A = nc.scalar.activation

            def tick(l, u):
                n = u + AHEAD
                slot = n % RAW
                act.wait_ge(raw_loaded[slot].sem, raw_loaded[slot].at(l, 16 * (n // RAW + 1)))
                if n >= RING:
                    act.wait_ge(unit_done.sem, unit_done.at(l, n - RING + 1))
                A(w_hi[n % RING][:, :, :], raw[slot][:, :, :], ACT.Copy).then_inc(unit_hi.sem, 1)

            def square(l, m, n, cols=slice(0, T)):
                if n >= 3:
                    act.wait_ge(sqsum_ready.sem, sqsum_ready.at(l, 8 * m + n - 2))
                A((tmp[n % 2] if n else sqsum)[:, cols], x[:, n, cols], ACT.Square).then_inc(sq_ready.sem, 1)

            def norm(l, m, h):
                act.wait_ge(sumsq.sem, sumsq.at(l, 2 * m + h + 1))
                A(rstd[:, HALF[h]], bank[BS][:, HALF[h]], ACT.Ln, bias=eps_col[:, 0:1], scale=1.0 / D)\
                    .then_inc(ln_ready.sem, 1)
                act.wait_ge(ln_ready.sem, ln_ready.at(l, 2 * m + h + 1))
                A(rstd[:, HALF[h]], rstd[:, HALF[h]], ACT.Exp, scale=-0.5).then_inc(rstd_ready.sem, 1)

            def h_round(l, m, group, h, ticks=()):
                act.wait_ge(nscale_set.sem, nscale_set.at(l, m + 1))
                for k in range(KD):
                    j = 16 * (m + 1) + 8 * h + k
                    act.wait_ge(xr_ready.sem, xr_ready.at(l, j + 1))
                    shift, scale = mod[:, 24 * group + k:24 * group + k + 1], nscale[:, group, k:k + 1]
                    A(h_hi[:, k, HALF[h]], tmp[k % 2][:, HALF[h]], ACT.Identity, bias=shift,
                      scale=scale).then_inc(hh_ready.sem, 1)
                    if k >= 2:
                        act.wait_ge(hl_ready.sem, hl_ready.at(l, j - 1))
                    A(tmp[2 + k % 2][:, HALF[h]], tmp[k % 2][:, HALF[h]], ACT.Identity, bias=shift,
                      scale=scale).then_inc(hf_ready.sem, 1)
                    for after, u in ticks:
                        if k == after:
                            tick(l, u)

            def ffn(l, s):
                u0 = U_FFN[s]
                for f in range(KF):
                    if f:
                        tick(l, u0 + 2 * f)
                    tick(l, u0 + 2 * f + 1)
                    if f:
                        g_round(l, s, f - 1)
                    act.wait_ge(unit_done.sem, unit_done.at(l, u0 + 2 * f + 2))
                    if f >= 2:
                        act.wait_ge(g_ready.sem, g_ready.at(l, s * KF + f - 1))
                    A(tmp[f % 2][:, :], bank[2 * (f % 2)][:, :], ACT.Silu).then_inc(silu_ready.sem, 1)
                tick(l, u0 + 2 * KF)
                g_round(l, s, KF - 1)
                u = 2 * KF + 1
                for n in range(KD - 1):
                    while u < 2 * KF + ((n + 1) * KF + UB - 1) // UB:
                        tick(l, u0 + u)
                        u += 1
                    act.wait_ge(x_ready.sem, x_ready.at(l, 18 * s + n + 1))
                    square(l, 2 * s, n)
                nc.scalar.preload_act_table_set("natural_log_exp_and_others")
                act.wait_ge(x_ready.sem, x_ready.at(l, 18 * s + 8))
                square(l, 2 * s, KD - 1, HALF[0])
                tick(l, u0 + FFN_UNITS - 2)
                norm(l, 2 * s, 0)
                if s == 0:
                    h_round(l, 0, 1, 0, ((1, u0 + FFN_UNITS - 1), (5, u0 + FFN_UNITS)))
                else:
                    tick(l, u0 + FFN_UNITS - 1)
                act.wait_ge(x_ready.sem, x_ready.at(l, 18 * s + 9))
                square(l, 2 * s, KD - 1, HALF[1])

            def g_round(l, s, f):
                act.wait_ge(g_ready.sem, g_ready.at(l, s * KF + f + 1))
                A(g_hi[:, f, :], tmp[2 + f % 2][:, :], ACT.Copy).then_inc(gh_ready.sem, 1)

            def rg_1(l, c):
                u = U_RG + 2 * c
                if c % 2:
                    tick(l, u)
                act.wait_ge(unit_done.sem, unit_done.at(l, u + 1))
                if c >= 2:
                    act.wait_ge(ix_ready.sem, ix_ready.at(l, c - 1))
                A(xa[c % 2][:, :], bank[2 * (c % 2)][:, :], ACT.Identity, bias=vec[:, V_CONVB + c:V_CONVB + c + 1],
                  scale=vec[:, V_CONVW + 24 + c:V_CONVW + 25 + c]).then_inc(xa0_ready.sem, 1)
                if c == 0:
                    act.wait_ge(wab_loaded.sem, wab_loaded.at(l, 16))
                if c >= 2:
                    act.wait_ge(gates_done.sem, gates_done.at(l, c - 1))
                A(wab_hi[c % 2][:, :, :], wab_raw[:, c, :, :], ACT.Copy).then_inc(wabh.sem, 1)
                tick(l, u + 1)
                act.wait_ge(unit_done.sem, unit_done.at(l, u + 2))
                if c >= 4:
                    act.wait_ge(yal.sem, yal.at(l, c - 3))
                A(gel[c % 4][:, :], bank[2 * (c % 2) + 1][:, :], ACT.Gelu_apprx_tanh).then_inc(gelu_ready.sem, 1)

            def rg_2(l, c0, nxt):
                both = (c0, c0 + 1)
                tick(l, U_RG + 2 * c0 + 4)
                nc.scalar.preload_act_table_set("sigmoid_and_others")
                for c in both:
                    s, b = c % 2, 4 + 2 * (c % 2)
                    act.wait_ge(gates_done.sem, gates_done.at(l, c + 1))
                    if c >= 2:
                        act.wait_ge(scan_ready.sem, scan_ready.at(l, c - 1))
                    A(gr[s][:, :], bank[b][:, :], ACT.Sigmoid, bias=vec[:, V_BA + c:V_BA + c + 1])\
                        .then_inc(r_ready.sem, 1)
                    A(gi[s][:, :], bank[b + 1][:, :], ACT.Sigmoid, bias=vec[:, V_BX + c:V_BX + c + 1])\
                        .then_inc(i_ready.sem, 1)
                for c in both:
                    if c == 0:
                        act.wait_ge(sp_set.sem, sp_set.at(l, 2))
                    act.wait_ge(r_ready.sem, r_ready.at(l, c + 1))
                    if c >= 2:
                        act.wait_ge(ya_ready.sem, ya_ready.at(l, c - 1))
                    A(gt[c % 2][:, :], gr[c % 2][:, :], ACT.Tanh, scale=pos_sp[:, c:c + 1]).then_inc(t_ready.sem, 1)
                nc.scalar.preload_act_table_set("natural_log_exp_and_others")
                for c in both:
                    act.wait_ge(t_ready.sem, t_ready.at(l, c + 1))
                    A(gr[c % 2][:, :], gr[c % 2][:, :], ACT.Exp, scale=neg_sp[:, c:c + 1]).then_inc(a_ready.sem, 1)
                if c0 == 0:
                    act.wait_ge(fx_step.sem, fx_step.at(l, 1))
                    A(fx_b[:, :], fx_a[:, :], ACT.Abs).then_inc(fx_act.sem, 1)
                    act.wait_ge(fx_act.sem, fx_act.at(l, 1))
                    A(fx_b[:, :], fx_b[:, :], ACT.Exp, scale=-1.0).then_inc(fx_act.sem, 1)
                    act.wait_ge(fx_act.sem, fx_act.at(l, 2))
                    A(fx_b[:, :], fx_b[:, :], ACT.Ln, bias=one_col[0:HEADS, 0:1]).then_inc(fx_act.sem, 1)
                nc.scalar.preload_act_table_set("sqrt_and_others")
                for c in both:
                    act.wait_ge(s_ready.sem, s_ready.at(l, c + 1))
                    A(gt[c % 2][:, :], gt[c % 2][:, :], ACT.Sqrt).then_inc(sqrt_ready.sem, 1)
                nc.scalar.preload_act_table_set(nxt)

            def q_round(l, p):
                u = U_QKV + 3 * p
                if p:
                    tick(l, u)
                act.wait_ge(unit_done.sem, unit_done.at(l, u + 1))
                if p:
                    act.wait_ge(z_done.sem, z_done.at(l, 6 * p))
                A(q_hi[:, :], bank[QKV_BANK(p, 0)][:, :], ACT.Copy, scale=HD ** -0.5).then_inc(qh.sem, 1)

            def k_round(l, p):
                u = U_QKV + 3 * p + 1
                tick(l, u)
                act.wait_ge(unit_done.sem, unit_done.at(l, u + 1))
                A(k_hi[:, :], bank[QKV_BANK(p, 1)][:, :], ACT.Copy).then_inc(kh.sem, 1)

            def v_copy(l, p):
                u = U_QKV + 3 * p + 2
                tick(l, u)
                act.wait_ge(unit_done.sem, unit_done.at(l, u + 1))
                if p:
                    act.wait_ge(vt_done.sem, vt_done.at(l, p))
                A(vt[:, :], bank[QKV_BANK(p, 2)][:, :], ACT.Copy).then_inc(vt_ready.sem, 1)

            def v_round(l, p):
                act.wait_ge(vt_done.sem, vt_done.at(l, p + 1))
                if p:
                    act.wait_ge(pv_head.sem, pv_head.at(l, 2 * p))
                if p == 0:
                    act.wait_ge(v_zero.sem, v_zero.at(l, 1))
                src = bank[7][:, :].rearrange("p (j e d) -> p j e d", j=TT, e=2)
                for e in range(2):
                    i = A(v_hi[:, :, e * (P + HD):e * (P + HD) + HD], src[:, :, e, :], ACT.Copy)
                i.then_inc(vh.sem, 1)

            def sb_1(l, p, e):
                n = 2 * p + e
                if n >= 2:
                    act.wait_ge(pv_head.sem, pv_head.at(l, n - 1))
                for i, c in enumerate(SB_ORDER):
                    o, w = CHUNK[c]
                    act.wait_ge(z_done.sem, z_done.at(l, 3 * n + i + 1))
                    A(e_f[e][:, o:o + w], bank[ZB[e][c]][:, 0:w], ACT.Abs).then_inc(abs_ready.sem, 1)
                act.wait_ge(abs_ready.sem, abs_ready.at(l, 3 * n + 3))
                A(e_f[e][:, :], e_f[e][:, :], ACT.Exp, scale=-1.0).then_inc(exp_ready.sem, 1)
                act.wait_ge(exp_ready.sem, exp_ready.at(l, n + 1))
                for part in PART:
                    A(e_f[e][:, part], e_f[e][:, part], ACT.Ln, bias=one_col[:, 0:1]).then_inc(lnp_ready.sem, 1)

            def sb_2(l, p, e):
                n = 2 * p + e
                act.wait_ge(suf_done.sem, suf_done.at(l, 3 * n + 3))
                for c, (o, w) in enumerate(CHUNK):
                    A(e_f[e][:, o:o + w], bank[ZB[e][c]][:, 0:w], ACT.Exp).then_inc(w_ready.sem, 1)

            def fx_1(l, p, e):
                n = 2 * (p - 4) + e
                act.wait_ge(max_ready.sem, max_ready.at(l, TT * n + TT))
                for i in range(TT):
                    b, o = FX_AT[i]
                    A(e_f[e][:, 512 * b + o:512 * b + o + P * (i + 1)], bank[ZB[e][b]][:, o:o + P * (i + 1)], ACT.Exp,
                      bias=negmax[:, e, i:i + 1], accum_out=psums[:, e, i:i + 1]).then_inc(p_ready.sem, 1)

            def fx_2(l, p, e):
                n = 2 * (p - 4) + e
                act.wait_ge(suf_done.sem, suf_done.at(l, 6 * p + 3 * e + 3))
                for c, (o, w) in enumerate(CHUNK):
                    A(e_hi[e][:, o:o + w], bank[ZB[e][c]][:, 0:w], ACT.Copy).then_inc(ph.sem, 1)

            def y_round(l, p):
                act.wait_ge(pv_head.sem, pv_head.at(l, 2 * p + 2))
                if p == 0:
                    act.wait_ge(yal.sem, yal.at(l, KD))
                A(yb_hi[:, p, :], bank[7][:, :], ACT.Copy).then_inc(ybh.sem, 1)

            def merge(l, n):
                u = U_MERGE + 5 * n
                for g in range(3):
                    tick(l, u + g)
                    act.wait_ge(unit_done.sem, unit_done.at(l, u + g + 1))
                    if n:
                        act.wait_ge(mx_step.sem, mx_step.at(l, 5 * n))
                    A(sg[g][:, :], bank[g][:, :], ACT.Sigmoid,
                      bias=vec[:, V_MERGEB + 8 * g + n:V_MERGEB + 8 * g + n + 1]).then_inc(sg_ready.sem, 1)
                tick(l, u + 3)
                tick(l, u + 4)
                act.wait_ge(mx_step.sem, mx_step.at(l, 5 * n + 5))
                A(mx_hi[:, n, :], mx[:, :], ACT.Copy).then_inc(mxh.sem, 1)

            act.wait_ge(c_loaded.sem, 16)
            A(c_act[:, :], c_act[:, :], ACT.Silu).then_inc(silu_c.sem, 1)
            act.wait_ge(consts.sem, 8)
            for dst, src in ((ident_r, ident[:, :]), (ntri_r, tmp[0][:, 128:256]), (nones_r, tmp[0][:, 0:128]),
                             (ones_r, tmp[0][:, 256:384]), (mask_sb, tmp[1][:, 128:256]),
                             (mask_fx, tmp[1][:, 256:384])):
                A(dst[:, :], src, ACT.Copy).then_inc(consts_v.sem, 1)
            A(pick[:, :], ident[:, 0:HEADS], ACT.Copy).then_inc(consts_v.sem, 1)
            act.wait_ge(consts_v.sem, 9)
            A(pick[QUAD:2 * QUAD, :], ident[QUAD:2 * QUAD, QUAD:QUAD + HEADS], ACT.Copy).then_inc(consts_v.sem, 1)
            act.wait_ge(consts_v.sem, 10)
            nc.scalar.preload_act_table_set("natural_log_exp_and_others")
            act.wait_ge(x_loaded.sem, 16 * KD // 2)
            for n in range(KD - 1):
                square(0, -1, n)
            square(0, -1, KD - 1, HALF[0])
            square(0, -1, KD - 1, HALF[1])
            norm(0, -1, 0)
            for u in range(-AHEAD, 0):
                tick(0, u)
            with act.Fori(0, DEPTH) as l:
                h_round(l, -1, 0, 0, ((2, 0),))
                norm(l, -1, 1)
                h_round(l, -1, 0, 1)
                nc.scalar.preload_act_table_set("silu_and_others")
                ffn(l, 0)
                norm(l, 0, 1)
                h_round(l, 0, 1, 1)
                act.wait_ge(wf_loaded.sem, wf_loaded.at(l, 16))
                A(wf_hi[:, :, :], wf_raw[:, :, :], ACT.Copy).then_inc(wfh.sem, 1)
                act.wait_ge(sp_step.sem, sp_step.at(l, 1))
                A(spc[:, 1, :], spc[:, 0, :], ACT.Exp).then_inc(sp_exp.sem, 1)
                nc.scalar.preload_act_table_set("gelu_apprx_tanh_and_others")
                for c in range(0, KD, 2):
                    rg_1(l, c)
                    rg_1(l, c + 1)
                    rg_2(l, c, "gelu_apprx_tanh_and_others" if c + 2 < KD else "natural_log_exp_and_others")
                q_round(l, 0)
                k_round(l, 0)
                v_copy(l, 0)
                for p in range(PAIRS):
                    first, second = (sb_1, sb_2) if p < 4 else (fx_1, fx_2)
                    first(l, p, 0)
                    if p < 4:
                        first(l, p, 1)
                        v_round(l, p)
                    else:
                        v_round(l, p)
                        first(l, p, 1)
                    if p + 1 < PAIRS:
                        q_round(l, p + 1)
                        second(l, p, 0)
                        second(l, p, 1)
                        k_round(l, p + 1)
                        y_round(l, p)
                        v_copy(l, p + 1)
                    else:
                        second(l, p, 0)
                        second(l, p, 1)
                        y_round(l, p)
                nc.scalar.preload_act_table_set("sigmoid_and_others")
                for n in range(KD):
                    merge(l, n)
                for n in range(KD):
                    tick(l, U_WO + n)
                    if n % 2 == 1 and n < KD - 1:
                        for i in (n - 1, n):
                            act.wait_ge(x_ready.sem, x_ready.at(l, 9 + i + 1))
                            square(l, 1, i)
                act.wait_ge(x_ready.sem, x_ready.at(l, 9 + 7))
                square(l, 1, KD - 2)
                nc.scalar.preload_act_table_set("natural_log_exp_and_others")
                act.wait_ge(x_ready.sem, x_ready.at(l, 9 + 8))
                square(l, 1, KD - 1, HALF[0])
                norm(l, 1, 0)
                h_round(l, 1, 2, 0, ((2, U_FFN[1]),))
                act.wait_ge(x_ready.sem, x_ready.at(l, 9 + 9))
                square(l, 1, KD - 1, HALF[1])
                norm(l, 1, 1)
                h_round(l, 1, 2, 1)
                nc.scalar.preload_act_table_set("silu_and_others")
                ffn(l, 1)
            act.wait_ge(nscale_set.sem, nscale_set.at(DEPTH, 0))
            for h in range(2):
                if h:
                    norm(DEPTH, -1, 1)
                for k in range(KD):
                    act.wait_ge(xr_ready.sem, xr_ready.at(DEPTH, 8 * h + k + 1))
                    t = fin[k // 2][:, k % 2, HALF[h]]
                    A(t, t, ACT.Identity, bias=mod[:, k:k + 1], scale=nscale[:, 0, k:k + 1]).then_inc(fin_ready.sem, 1)

        @block.vector
        def _(dve):
            V = nc.vector

            def ada_tile(l, a):
                col = (a + 16) % 72
                dve.wait_ge(ada_loaded[a % 2].sem, ada_loaded[a % 2].at(l, 16 * (a // 2 + 1)))
                V.tensor_tensor_reduce(ada[a % 2][:, :], ada[a % 2][:, :], c_act[:, :], 1.0, 0.0, ALU.mult, ALU.add,
                                       mod[:, col:col + 1]).then_inc(ada_done.sem, 1)

            def mod_bias(l, a1, c0, c1):
                dve.wait_ge(ada_done.sem, ada_done.at(l, a1))
                V.tensor_tensor(mod[:, c0:c1], mod[:, c0:c1], vec[:, V_ADAB + c0:V_ADAB + c1],
                                ALU.add).then_inc(mod_set.sem, 1)

            def scale_col(l, k, vnorm, group):
                dve.wait_ge(mod_set.sem, mod_set.at(l, k))
                V.scalar_tensor_tensor(out=nscale[:, group, :], in0=mod[:, 24 * group + 8:24 * group + 16], scalar=1.0,
                                       in1=vec[:, vnorm:vnorm + 8], op0=ALU.add,
                                       op1=ALU.mult).then_inc(nscale_set.sem, 1)

            def gate_col(l, s, group, half):
                V.tensor_scalar(gatec[:, :], mod[:, 24 * group + 16:24 * group + 24], 1.0, half, ALU.add,
                                ALU.mult).then_inc(gate_set.sem, 1)
                dve.wait_ge(gate_set.sem, gate_set.at(l, s + 1))

            def square_add(l, m, n, cols=slice(0, T), h=0):
                if n == 0:
                    return
                dve.wait_ge(sq_ready.sem, sq_ready.at(l, 9 * m + n + h + 1))
                if n > 1:
                    dve.wait_ge(sqsum_ready.sem, sqsum_ready.at(l, 8 * m + n + h - 1))
                V.tensor_tensor(sqsum[:, cols], sqsum[:, cols], tmp[n % 2][:, cols],
                                ALU.add).then_inc(sqsum_ready.sem, 1)

            def h_tiles(l, m, h):
                dve.wait_ge(rstd_ready.sem, rstd_ready.at(l, 2 * m + h + 1))
                j0 = 16 * (m + 1) + 8 * h

                def rest(k):
                    dve.wait_ge(hf_ready.sem, hf_ready.at(l, j0 + k + 1))
                    V.tensor_tensor(h_lo[:, k, HALF[h]], tmp[2 + k % 2][:, HALF[h]],
                                    h_hi[:, k, HALF[h]].bitcast(F32), ALU.subtract).then_inc(hl_ready.sem, 1)

                for k in range(KD):
                    if k >= 2:
                        dve.wait_ge(hf_ready.sem, hf_ready.at(l, j0 + k - 1))
                    V.tensor_tensor(tmp[k % 2][:, HALF[h]], x[:, k, HALF[h]], rstd[:, HALF[h]],
                                    ALU.mult).then_inc(xr_ready.sem, 1)
                    if k:
                        rest(k - 1)
                rest(KD - 1)

            def x_add(bnk, n, cols=slice(0, T)):
                V.scalar_tensor_tensor(out=x[:, n, cols], in0=bnk[:, cols], scalar=gatec[:, n:n + 1], in1=x[:, n, cols],
                                       op0=ALU.mult, op1=ALU.add).then_inc(x_ready.sem, 1)

            def ffn(l, s):
                u0 = U_FFN[s]
                tiles = (lambda u: [u] if u < 56 else []) if s == 0 else (
                    lambda u: [56 + u - 6] if 6 <= u < 22 else [])

                def gl(f):
                    dve.wait_ge(gh_ready.sem, gh_ready.at(l, s * KF + f + 1))
                    V.tensor_tensor(g_lo[:, f, :], tmp[2 + f % 2][:, :], g_hi[:, f, :].bitcast(F32),
                                    ALU.subtract).then_inc(gl_ready.sem, 1)

                for f in range(KF):
                    for u in (2 * f, 2 * f + 1):
                        for a in tiles(u):
                            ada_tile(l, a)
                    dve.wait_ge(silu_ready.sem, silu_ready.at(l, s * KF + f + 1))
                    if f >= 2:
                        dve.wait_ge(gl_ready.sem, gl_ready.at(l, s * KF + f - 1))
                    V.tensor_tensor(tmp[2 + f % 2][:, :], tmp[f % 2][:, :], bank[2 * (f % 2) + 1][:, :],
                                    ALU.mult).then_inc(g_ready.sem, 1)
                    if f:
                        gl(f - 1)
                gl(KF - 1)
                if s == 0:
                    ada_tiles = list(range(44, 56))
                    mod_bias(l, 8, 16, 24)
                    dve.wait_ge(mod_set.sem, mod_set.at(l, 1))
                    gate_col(l, 0, 0, 0.5)
                else:
                    gate_col(l, 2, 2, 0.5)
                    dve.wait_ge(vec_loaded.sem, vec_loaded.at(l, 16))
                    mod_bias(l, 72, 0, 16)
                    scale_col(l, 3, V_NORM1, 0)
                for n in range(KD - 1):
                    if n in INSIDE:
                        dve.wait_ge(down_done.sem, down_done.at(l, s * TILE_ENDS + INSIDE.index(n) + 1))
                    else:
                        dve.wait_ge(unit_done.sem, unit_done.at(l, u0 + 2 * KF + (n + 1) * KF // UB))
                    x_add(bank[4 + n % 2], n)
                    square_add(l, 2 * s, n)
                    if s == 0:
                        for a in ada_tiles[2 * n:2 * n + 2]:
                            ada_tile(l, a)
                if s == 0:
                    mod_bias(l, 56, 24, 72)
                    scale_col(l, 2, V_NORM2, 1)
                    scale_col(l, 2, V_NORM3, 2)
                dve.wait_ge(half_done.sem, half_done.at(l, 2 * s + 1))
                x_add(bank[5], KD - 1, HALF[0])
                square_add(l, 2 * s, KD - 1, HALF[0], 0)
                if s == 0:
                    h_tiles(l, 0, 0)
                dve.wait_ge(unit_done.sem, unit_done.at(l, u0 + FFN_UNITS))
                x_add(bank[7], KD - 1, HALF[1])
                square_add(l, 2 * s, KD - 1, HALF[1], 1)

            def rg_1(l, c):
                s = c % 2
                dve.wait_ge(xa0_ready.sem, xa0_ready.at(l, c + 1))
                for j in range(3):
                    if j:
                        dve.wait_ge(conv.sem, conv.at(l, 3 * c + j))
                    V.scalar_tensor_tensor(out=xa[s][:, 3 - j:T], in0=bank[2 * s][:, 0:T - 3 + j],
                                           scalar=vec[:, V_CONVW + 8 * j + c:V_CONVW + 8 * j + c + 1],
                                           in1=xa[s][:, 3 - j:T], op0=ALU.mult, op1=ALU.add).then_inc(conv.sem, 1)
                dve.wait_ge(conv.sem, conv.at(l, 3 * c + 3))
                if c >= 2:
                    dve.wait_ge(gates_done.sem, gates_done.at(l, c - 1))
                V.tensor_copy(xa_hi[s][:, :], xa[s][:, :]).then_inc(xah.sem, 1)
                dve.wait_ge(xah.sem, xah.at(l, c + 1))
                V.tensor_tensor(xa_lo[s][:, :], xa[s][:, :], xa_hi[s][:, :].bitcast(F32),
                                ALU.subtract).then_inc(xal.sem, 1)

            def rg_2(l, c0):
                both = (c0, c0 + 1)
                for c in both:
                    dve.wait_ge(i_ready.sem, i_ready.at(l, c + 1))
                    V.tensor_tensor(gi[c % 2][:, :], gi[c % 2][:, :], xa[c % 2][:, :], ALU.mult)\
                        .then_inc(ix_ready.sem, 1)
                for c in both:
                    s = c % 2
                    dve.wait_ge(a_ready.sem, a_ready.at(l, c + 1))
                    V.tensor_tensor(asq[s][:, :], gr[s][:, :], gr[s][:, :], ALU.mult).then_inc(asq_ready.sem, 1)
                    dve.wait_ge(asq_ready.sem, asq_ready.at(l, c + 1))
                    V.scalar_tensor_tensor(out=gt[s][:, :], in0=asq[s][:, :], scalar=1.0, in1=gt[s][:, :], op0=ALU.add,
                                           op1=ALU.mult).then_inc(s_ready.sem, 1)
                for c in both:
                    s, g = c % 2, c % 4
                    dve.wait_ge(ix_ready.sem, ix_ready.at(l, c + 1))
                    dve.wait_ge(sqrt_ready.sem, sqrt_ready.at(l, c + 1))
                    V.tensor_tensor(gi[s][:, :], gt[s][:, :], gi[s][:, :], ALU.mult).then_inc(u_ready.sem, 1)
                    dve.wait_ge(u_ready.sem, u_ready.at(l, c + 1))
                    V.tensor_tensor_scan(gt[s][:, :], gr[s][:, :], gi[s][:, :], 0.0, ALU.mult, ALU.add)\
                        .then_inc(scan_ready.sem, 1)
                    dve.wait_ge(scan_ready.sem, scan_ready.at(l, c + 1))
                    dve.wait_ge(gelu_ready.sem, gelu_ready.at(l, c + 1))
                    V.tensor_tensor(gel[g][:, :], gel[g][:, :], gt[s][:, :], ALU.mult).then_inc(ya_ready.sem, 1)
                    dve.wait_ge(ya_ready.sem, ya_ready.at(l, c + 1))
                    V.tensor_copy(ya_hi[:, c, :], gel[g][:, :]).then_inc(yah.sem, 1)
                    dve.wait_ge(yah.sem, yah.at(l, c + 1))
                    V.tensor_tensor(ya_lo[:, c, :], gel[g][:, :], ya_hi[:, c, :].bitcast(F32),
                                    ALU.subtract).then_inc(yal.sem, 1)

            def softplus_lambda(l):
                n = [0]

                def step(i):
                    i.then_inc(sp_step.sem, 1)
                    n[0] += 1
                    dve.wait_ge(sp_step.sem, sp_step.at(l, n[0]))
                lam = vec[:, V_LAM:V_LAM + 8]
                step(V.scalar_tensor_tensor(out=spc[:, 0, :], in0=lam, scalar=-1.0, in1=lam, op0=ALU.mult,
                                            op1=ALU.min))
                dve.wait_ge(sp_exp.sem, sp_exp.at(l, 1))
                e = spc[:, 1, :]
                step(V.tensor_scalar(spc[:, 2, :], e, 2.0, None, ALU.add))
                step(V.reciprocal(spc[:, 2, :], spc[:, 2, :]))
                step(V.tensor_tensor(spc[:, 2, :], spc[:, 2, :], e, ALU.mult))
                step(V.tensor_tensor(spc[:, 3, :], spc[:, 2, :], spc[:, 2, :], ALU.mult))
                step(V.tensor_scalar(spc[:, 4, :], spc[:, 3, :], 1.0 / 15, None, ALU.mult))
                for d in (13, 11, 9, 7, 5, 3):
                    step(V.scalar_tensor_tensor(out=spc[:, 4, :], in0=spc[:, 4, :], scalar=1.0 / d,
                                                in1=spc[:, 3, :], op0=ALU.add, op1=ALU.mult))
                step(V.scalar_tensor_tensor(out=spc[:, 4, :], in0=spc[:, 4, :], scalar=1.0, in1=spc[:, 2, :],
                                            op0=ALU.add, op1=ALU.mult))
                step(V.tensor_scalar(spc[:, 5, :], lam, -1.0, 0.0, ALU.mult, ALU.max))
                V.scalar_tensor_tensor(out=spc[:, 0, :], in0=spc[:, 4, :], scalar=2.0, in1=spc[:, 5, :],
                                       op0=ALU.mult, op1=ALU.add).then_inc(sp_exp.sem, 1)
                dve.wait_ge(sp_exp.sem, sp_exp.at(l, 2))
                V.tensor_scalar(neg_sp[:, :], spc[:, 0, :], -8.0, None, ALU.mult).then_inc(sp_set.sem, 1)
                V.tensor_scalar(pos_sp[:, :], spc[:, 0, :], 8.0, None, ALU.mult).then_inc(sp_set.sem, 1)

            def forget_1(l):
                dve.wait_ge(foxf_done.sem, foxf_done.at(l, 1))
                b = vec[0:HEADS, V_FOXB:V_FOXB + 1]
                V.tensor_scalar(fx_a[:, :], bank[7][0:HEADS, :], b, None, ALU.add).then_inc(fx_step.sem, 1)

            def forget_2(l):
                dve.wait_ge(fx_act.sem, fx_act.at(l, 1))
                V.memset(decay[:, :].bitcast(F32), 0.0).then_inc(nch.sem, 1)
                V.tensor_scalar(fx_a[:, :], fx_a[:, :], -1.0, 0.0, ALU.mult, ALU.max).then_inc(fx_step.sem, 1)
                dve.wait_ge(fx_step.sem, fx_step.at(l, 2))
                dve.wait_ge(fx_act.sem, fx_act.at(l, 3))
                V.tensor_tensor_scan(fx_c[:, :], fx_a[:, :], fx_b[:, :], 0.0, ALU.add, ALU.add)\
                    .then_inc(fx_step.sem, 1)
                dve.wait_ge(fx_step.sem, fx_step.at(l, 3))
                dve.wait_ge(nch.sem, nch.at(l, 1))
                V.tensor_copy(decay[0:HEADS, :], fx_c[:, :]).then_inc(nch.sem, 1)
                dve.wait_ge(nch.sem, nch.at(l, 2))
                V.tensor_tensor(decay[QUAD:QUAD + HEADS, :], fx_c[:, :], decay[0:HEADS, :].bitcast(F32),
                                ALU.subtract).then_inc(ncl.sem, 1)

            def q_rest(l, p):
                dve.wait_ge(qh.sem, qh.at(l, p + 1))
                V.scalar_tensor_tensor(out=q_lo[:, :], in0=bank[QKV_BANK(p, 0)][:, :], scalar=HD ** -0.5,
                                       in1=q_hi[:, :].bitcast(F32), op0=ALU.mult,
                                       op1=ALU.subtract).then_inc(ql.sem, 1)

            def k_rest(l, p):
                dve.wait_ge(kh.sem, kh.at(l, p + 1))
                V.tensor_tensor(k_lo[:, :], bank[QKV_BANK(p, 1)][:, :], k_hi[:, :].bitcast(F32),
                                ALU.subtract).then_inc(kl.sem, 1)

            def v_rest(l, p):
                if p == 0:
                    dve.wait_ge(v_zero.sem, v_zero.at(l, 2))
                dve.wait_ge(vh.sem, vh.at(l, p + 1))
                src = bank[7][:, :].rearrange("p (j e d) -> p j e d", j=TT, e=2)
                for e in range(2):
                    o = e * (P + HD)
                    i = V.tensor_tensor(v_lo[:, :, o:o + HD], src[:, :, e, :], v_hi[:, :, o:o + HD].bitcast(F32),
                                        ALU.subtract)
                i.then_inc(vl.sem, 1)

            def sb_softplus(l, p, e):
                n = 2 * p + e
                for h, part in enumerate(PART):
                    dve.wait_ge(lnp_ready.sem, lnp_ready.at(l, 2 * n + h + 1))
                    for c in ((1, 2), (0,))[h]:
                        o, w = CHUNK[c]
                        V.scalar_tensor_tensor(out=e_f[e][:, o:o + w], in0=bank[ZB[e][c]][:, 0:w], scalar=0.0,
                                               in1=e_f[e][:, o:o + w], op0=ALU.max,
                                               op1=ALU.add).then_inc(softplus.sem, 1)
                    done = 7 * n + (2, 5)[h]
                    dve.wait_ge(softplus.sem, softplus.at(l, done))
                    V.tensor_copy(e_hi[e][:, part], e_f[e][:, part]).then_inc(softplus.sem, 1)
                    dve.wait_ge(softplus.sem, softplus.at(l, done + 1))
                    V.tensor_tensor(e_lo[e][:, part], e_f[e][:, part], e_hi[e][:, part].bitcast(F32),
                                    ALU.subtract).then_inc(softplus.sem, 1)

            def sb_split(l, p, e):
                n = 2 * p + e
                dve.wait_ge(w_ready.sem, w_ready.at(l, 3 * n + 3))
                V.tensor_copy(e_hi[e][:, :], e_f[e][:, :]).then_inc(eh.sem, 1)
                dve.wait_ge(eh.sem, eh.at(l, n + 1))
                V.tensor_tensor(e_lo[e][:, :], e_f[e][:, :], e_hi[e][:, :].bitcast(F32),
                                ALU.subtract).then_inc(el.sem, 1)

            def fx_max(l, p, e):
                n = 2 * (p - 4) + e
                dve.wait_ge(pv_head.sem, pv_head.at(l, 2 * p + e - 1))
                dve.wait_ge(z_done.sem, z_done.at(l, 6 * p + 3 * e + 3))
                for i in range(TT):
                    b, o = FX_AT[i]
                    V.tensor_reduce(negmax[:, e, i:i + 1], bank[ZB[e][b]][:, o:o + P * (i + 1)], AX.X, ALU.max,
                                    negate=True).then_inc(max_ready.sem, 1)

            def fx_norm(l, p, e):
                n = 2 * (p - 4) + e
                dve.wait_ge(p_ready.sem, p_ready.at(l, TT * n + TT))
                V.reciprocal(rsums[:, e, :], psums[:, e, :]).then_inc(rs_ready.sem, 1)
                dve.wait_ge(rs_ready.sem, rs_ready.at(l, n + 1))
                for i in range(TT):
                    b, o = FX_AT[i]
                    t = e_f[e][:, 512 * b + o:512 * b + o + P * (i + 1)]
                    V.tensor_scalar(t, t, rsums[:, e, i:i + 1], None, ALU.mult).then_inc(pn_ready.sem, 1)

            def fx_split(l, p, e):
                n = 2 * (p - 4) + e
                dve.wait_ge(ph.sem, ph.at(l, 3 * n + 3))
                for c, (o, w) in enumerate(CHUNK):
                    V.tensor_tensor(e_lo[e][:, o:o + w], bank[ZB[e][c]][:, 0:w], e_hi[e][:, o:o + w].bitcast(F32),
                                    ALU.subtract).then_inc(pl.sem, 1)

            def y_rest(l, p):
                dve.wait_ge(ybh.sem, ybh.at(l, p + 1))
                V.tensor_tensor(yb_lo[:, p, :], bank[7][:, :], yb_hi[:, p, :].bitcast(F32),
                                ALU.subtract).then_inc(ybl.sem, 1)

            def merge(l, n):
                u = U_MERGE + 5 * n
                m0 = 5 * n
                if n:
                    dve.wait_ge(mxl.sem, mxl.at(l, n))
                dve.wait_ge(sg_ready.sem, sg_ready.at(l, 3 * n + 3))
                dve.wait_ge(unit_done.sem, unit_done.at(l, u + 4))
                V.tensor_tensor(mx[:, :], sg[0][:, :], bank[3][:, :], ALU.mult).then_inc(mx_step.sem, 1)
                dve.wait_ge(unit_done.sem, unit_done.at(l, u + 5))
                for g in (1, 2):
                    V.tensor_tensor(sg[g][:, :], sg[g][:, :], bank[3 + g][:, :], ALU.mult).then_inc(mx_step.sem, 1)
                dve.wait_ge(mx_step.sem, mx_step.at(l, m0 + 2))
                V.tensor_tensor(mx[:, :], mx[:, :], sg[1][:, :], ALU.add).then_inc(mx_step.sem, 1)
                dve.wait_ge(mx_step.sem, mx_step.at(l, m0 + 4))
                V.tensor_tensor(mx[:, :], mx[:, :], sg[2][:, :], ALU.add).then_inc(mx_step.sem, 1)
                dve.wait_ge(mxh.sem, mxh.at(l, n + 1))
                V.tensor_tensor(mx_lo[:, n, :], mx[:, :], mx_hi[:, n, :].bitcast(F32),
                                ALU.subtract).then_inc(mxl.sem, 1)

            V.memset(eps_col[:, :], EPS).then_inc(consts_v.sem, 1)
            V.memset(one_col[:, :], 1.0).then_inc(consts_v.sem, 1)
            dve.wait_ge(silu_c.sem, 1)
            dve.wait_ge(vec_loaded.sem, 16)
            def ada_tile_0(a):
                g, i = divmod(a, G0)
                dve.wait_ge(ada0_loaded[g].sem, 16)
                V.tensor_tensor_reduce(ada0[g][:, i, :], ada0[g][:, i, :], c_act[:, :], 1.0, 0.0, ALU.mult, ALU.add,
                                       mod[:, a:a + 1]).then_inc(ada_done.sem, 1)
            for n in range(KD - 1):
                square_add(0, -1, n)
                ada_tile_0(n)
            for h in range(2):
                square_add(0, -1, KD - 1, HALF[h], h)
            ada_tile_0(KD - 1)
            for a in range(KD, 16):
                ada_tile_0(a)
            mod_bias(0, 0, 0, 16)
            scale_col(0, 0, V_NORM1, 0)
            with dve.Fori(0, DEPTH) as l:
                h_tiles(l, -1, 0)
                h_tiles(l, -1, 1)
                ffn(l, 0)
                h_tiles(l, 0, 1)
                gate_col(l, 1, 1, 1.0)
                dve.wait_ge(wfh.sem, wfh.at(l, 1))
                V.tensor_tensor(wf_lo[:, :, :], wf_raw[:, :, :], wf_hi[:, :, :].bitcast(F32),
                                ALU.subtract).then_inc(wfl.sem, 1)
                softplus_lambda(l)
                for c in range(0, KD, 2):
                    rg_1(l, c)
                    rg_1(l, c + 1)
                    if c == 0:
                        forget_1(l)
                    if c == 2:
                        forget_2(l)
                    rg_2(l, c)
                q_rest(l, 0)
                k_rest(l, 0)
                V.memset(v_hi[:, :, :].bitcast(F32), 0.0).then_inc(v_zero.sem, 1)
                V.memset(v_lo[:, :, :].bitcast(F32), 0.0).then_inc(v_zero.sem, 1)
                for p in range(PAIRS):
                    if p < 4:
                        sb_softplus(l, p, 0)
                        sb_softplus(l, p, 1)
                        v_rest(l, p)
                    else:
                        fx_max(l, p, 0)
                        fx_max(l, p, 1)
                        v_rest(l, p)
                        fx_norm(l, p, 0)
                        fx_norm(l, p, 1)
                    if p + 1 < PAIRS:
                        q_rest(l, p + 1)
                    split = sb_split if p < 4 else fx_split
                    split(l, p, 0)
                    split(l, p, 1)
                    if p + 1 < PAIRS:
                        k_rest(l, p + 1)
                    y_rest(l, p)
                for n in range(KD):
                    merge(l, n)
                for n in range(KD - 1):
                    dve.wait_ge(unit_done.sem, unit_done.at(l, U_WO + n + 1))
                    x_add(bank[WO_BANK(n)], n)
                    square_add(l, 1, n)
                dve.wait_ge(half_done.sem, half_done.at(l, 2))
                x_add(bank[WO_BANK(KD - 1)], KD - 1, HALF[0])
                square_add(l, 1, KD - 1, HALF[0], 0)
                h_tiles(l, 1, 0)
                dve.wait_ge(unit_done.sem, unit_done.at(l, U_WO + KD))
                x_add(bank[4], KD - 1, HALF[1])
                square_add(l, 1, KD - 1, HALF[1], 1)
                h_tiles(l, 1, 1)
                ffn(l, 1)
            for h in range(2):
                dve.wait_ge(rstd_ready.sem, rstd_ready.at(DEPTH, -2 + h + 1))
                for k in range(KD):
                    V.tensor_tensor(fin[k // 2][:, k % 2, HALF[h]], x[:, k, HALF[h]], rstd[:, HALF[h]],
                                    ALU.mult).then_inc(xr_ready.sem, 1)

        @block.tensor
        def _(pe):
            def mm3(o, wh, wl, xh, xl, start, stop):
                nc.tensor.matmul(o, wh, xh, start=start, stop=False, skip_group_check=True)
                nc.tensor.matmul(o, wh, xl, start=False, stop=False, skip_group_check=True)
                return nc.tensor.matmul(o, wl, xh, start=False, stop=stop, skip_group_check=True)

            def unit(l, u, bnk, hi, lo):
                s = u % RING
                pe.wait_ge(unit_lo.sem, unit_lo.at(l, u + 1))
                for k in range(KD):
                    i = mm3(bnk, w_hi[s][:, k, :], w_lo[s][:, k, :], hi[:, k, :], lo[:, k, :], k == 0, k == KD - 1)
                i.then_inc(unit_done.sem, 1)

            def pair(l, u, b0, b1, hi, lo, ready=None):
                pe.wait_ge(unit_lo.sem, unit_lo.at(l, u + 2))
                for k in range(KD):
                    if ready:
                        pe.wait_ge(ready.sem, ready.at(l, k + 1))
                    for j, b in ((0, b0), (1, b1)):
                        s = (u + j) % RING
                        i = mm3(bank[b][:, :], w_hi[s][:, k, :], w_lo[s][:, k, :], hi[:, k, :], lo[:, k, :], k == 0,
                                k == KD - 1)
                        if k == KD - 1:
                            i.then_inc(unit_done.sem, 1)

            def after_norm(l, u, m):
                for h in range(2):
                    for f in range(2):
                        if h == 0:
                            pe.wait_ge(unit_lo.sem, unit_lo.at(l, u + 2 * f + 2))
                        for k in range(KD):
                            if h == 0 and f == 1 and k == 0:
                                sum_squares(l, m, 1)
                            e = 16 * (m + 1) + 8 * h + k + 1
                            if f == 0:
                                pe.wait_ge(hh_ready.sem, hh_ready.at(l, e))
                            for j in (2 * f, 2 * f + 1):
                                for w in (w_hi, w_lo):
                                    nc.tensor.matmul(bank[j][:, HALF[h]], w[(u + j) % RING][:, k, :],
                                                     h_hi[:, k, HALF[h]], start=h == 0 and k == 0 and w is w_hi,
                                                     stop=False, skip_group_check=True)
                            if f == 0:
                                pe.wait_ge(hl_ready.sem, hl_ready.at(l, e))
                            for j in (2 * f, 2 * f + 1):
                                i = nc.tensor.matmul(bank[j][:, HALF[h]], w_hi[(u + j) % RING][:, k, :],
                                                     h_lo[:, k, HALF[h]], start=False, stop=k == KD - 1,
                                                     skip_group_check=True)
                                if h == 1 and k == KD - 1:
                                    i.then_inc(unit_done.sem, 1)

            def sum_squares(l, m, h):
                pe.wait_ge(sqsum_ready.sem, sqsum_ready.at(l, 8 * m + 7 + h))
                if h:
                    pe.wait_ge(ln_ready.sem, ln_ready.at(l, 2 * m + 1))
                nc.tensor.matmul(bank[BS][:, HALF[h]], ones_r[:, :].bitcast(F32), sqsum[:, HALF[h]], start=h == 0,
                                 stop=True, skip_group_check=True).then_inc(sumsq.sem, 1)

            def ffn(l, s):
                u0 = U_FFN[s]
                after_norm(l, u0, 2 * s - 1)
                for f in range(2, KF):
                    pe.wait_ge(g_ready.sem, g_ready.at(l, s * KF + f - 1))
                    pair(l, u0 + 2 * f, 2 * (f % 2), 2 * (f % 2) + 1, h_hi, h_lo)
                for b in range((KD - 1) * KF):
                    n, k = divmod(b, KF)
                    u, j = divmod(b, UB)
                    if j == 0:
                        pe.wait_ge(unit_lo.sem, unit_lo.at(l, u0 + 2 * KF + u + 1))
                    if n == 0:
                        pe.wait_ge(gl_ready.sem, gl_ready.at(l, s * KF + k + 1))
                    if k == 0 and n >= 2:
                        pe.wait_ge(x_ready.sem, x_ready.at(l, 18 * s + n - 1))
                    sl = (2 * KF + u0 + u) % RING
                    i = mm3(bank[4 + n % 2][:, :], w_hi[sl][:, j, :], w_lo[sl][:, j, :], g_hi[:, k, :], g_lo[:, k, :],
                            k == 0, k == KF - 1)
                    if j == UB - 1:
                        i.then_inc(unit_done.sem, 1)
                    elif k == KF - 1:
                        i.then_inc(down_done.sem, 1)
                pe.wait_ge(x_ready.sem, x_ready.at(l, 18 * s + KD - 2))
                for h in range(2):
                    for k in range(KF):
                        u, j = divmod((KD - 1) * KF + k, UB)
                        if j == 0 and h == 0:
                            pe.wait_ge(unit_lo.sem, unit_lo.at(l, u0 + 2 * KF + u + 1))
                        if h == 1 and k == 10:
                            sum_squares(l, 2 * s, 0)
                        sl = (2 * KF + u0 + u) % RING
                        i = mm3(bank[5 + 2 * h][:, HALF[h]], w_hi[sl][:, j, :], w_lo[sl][:, j, :],
                                g_hi[:, k, HALF[h]], g_lo[:, k, HALF[h]], k == 0, k == KF - 1)
                        if h == 1 and j == UB - 1:
                            i.then_inc(unit_done.sem, 1)
                        if h == 0 and k == KF - 1:
                            i.then_inc(half_done.sem, 1)

            def gates(l, c):
                pe.wait_ge(xal.sem, xal.at(l, c + 1))
                pe.wait_ge(wabl.sem, wabl.at(l, c + 1))
                if c == 1:
                    pe.wait_ge(fx_step.sem, fx_step.at(l, 1))
                if c >= 2:
                    pe.wait_ge(i_ready.sem, i_ready.at(l, c - 1))
                for j in range(2):
                    i = mm3(bank[4 + 2 * (c % 2) + j][:, :], wab_hi[c % 2][:, j, :], wab_lo[c % 2][:, j, :],
                            xa_hi[c % 2][:, :], xa_lo[c % 2][:, :], True, True)
                i.then_inc(gates_done.sem, 1)

            def scores(l, p, e):
                r = slice(HD * e, HD * e + HD)
                n = 2 * p + e
                if p == 0:
                    if e == 0:
                        pe.wait_ge(i_ready.sem, i_ready.at(l, KD))
                    else:
                        pe.wait_ge(gelu_ready.sem, gelu_ready.at(l, KD))
                        pe.wait_ge(vt_ready.sem, vt_ready.at(l, 1))
                if e == 0:
                    pe.wait_ge(ql.sem, ql.at(l, p + 1))
                    pe.wait_ge(kl.sem, kl.at(l, p + 1))
                if p == 4 and e == 0:
                    pe.wait_ge(ncl.sem, ncl.at(l, 1))
                if p >= 1:
                    if p <= 4:
                        pe.wait_ge(w_ready.sem, w_ready.at(l, 3 * (n - 2) + 3))
                    else:
                        pe.wait_ge(pl.sem, pl.at(l, 3 * (n - 8 - 2) + 3))
                order = [1, 3, 2, 0] if p < 4 else [3, 2, 0, 1]
                for i in order:
                    b, o = (SB_AT if p < 4 else FX_AT)[i]
                    begins = o == 0
                    if p < 4:
                        w = T - P * i
                        dst = bank[ZB[e][b]][:, o:o + w]
                        mm3(dst, k_hi[r, P * i:P * i + P], k_lo[r, P * i:P * i + P], q_hi[r, P * i:T],
                            q_lo[r, P * i:T], begins, False)
                        last = nc.tensor.matmul(dst[:, 0:P], ident_r[:, :], mask_sb[:, :], start=False, stop=False,
                                                skip_group_check=True)
                    else:
                        w = P * (i + 1)
                        h = n - HEADS
                        dst = bank[ZB[e][b]][:, o:o + w]
                        mm3(dst, q_hi[r, P * i:P * i + P], q_lo[r, P * i:P * i + P], k_hi[r, 0:w], k_lo[r, 0:w],
                            begins, False)
                        nc.tensor.matmul(dst, pick[:, h:h + 1].to_broadcast([P, P]), decay[:, 0:w], start=False,
                                         stop=False, skip_group_check=True)
                        last = nc.tensor.matmul(dst[:, P * i:w], ident_r[:, :], mask_fx[:, :], start=False,
                                                stop=False, skip_group_check=True)
                    if (b == 0) or (b == 2) or o == 384:
                        last.then_inc(z_done.sem, 1)

            def suffix(l, p, e):
                for i in (3, 2, 1, 0):
                    b, o = SB_AT[i]
                    if i == 3:
                        pe.wait_ge(softplus.sem, softplus.at(l, 7 * (2 * p + e) + 4))
                    if i == 0:
                        pe.wait_ge(softplus.sem, softplus.at(l, 7 * (2 * p + e) + 7))
                    for j in range(i, TT):
                        bj, oj = SB_AT[j]
                        w = T - P * j
                        dst = bank[ZB[e][b]][:, o + P * (j - i):o + P * (j - i) + w]
                        for src in (e_hi[e], e_lo[e]):
                            last = nc.tensor.matmul(dst, (ntri_r if i == j else nones_r)[:, :],
                                                    src[:, 512 * bj + oj:512 * bj + oj + w], start=False,
                                                    stop=False, skip_group_check=True)
                    if i != 3:
                        last.then_inc(suf_done.sem, 1)

            def turn(l, p, e):
                pe.wait_ge(pn_ready.sem, pn_ready.at(l, TT * (2 * (p - 4) + e) + TT))
                for j in (0, 1, 3, 2):
                    b, o = SB_AT[j]
                    for i in range(j, TT):
                        bi, oi = FX_AT[i]
                        src = 512 * bi + oi + P * j
                        last = nc.tensor.transpose(bank[ZB[e][b]][:, o + P * (i - j):o + P * (i - j) + P],
                                                   e_f[e][:, src:src + P], ident[:, :])
                    if j != 1:
                        last.then_inc(suf_done.sem, 1)

            def values(l, p, e):
                if e == 0:
                    pe.wait_ge(vl.sem, vl.at(l, p + 1))
                if p < 4:
                    pe.wait_ge(el.sem, el.at(l, 2 * p + e + 1))
                else:
                    pe.wait_ge(pl.sem, pl.at(l, 3 * (2 * (p - 4) + e) + 3))
                for j in range(TT):
                    b, o = SB_AT[j]
                    w = T - P * j
                    src = slice(512 * b + o, 512 * b + o + w)
                    i = mm3(bank[7][:, P * j:T], v_hi[:, j, e * P:e * P + P], v_lo[:, j, e * P:e * P + P],
                            e_hi[e][:, src], e_lo[e][:, src], e == 0 and j == 0, False)
                i.then_inc(pv_head.sem, 1)

            def turn_v(l, p):
                pe.wait_ge(vt_ready.sem, vt_ready.at(l, p + 1))
                if p:
                    pe.wait_ge(ybl.sem, ybl.at(l, p))
                for j in range(TT):
                    i = nc.tensor.transpose(bank[7][:, P * j:P * j + P], vt[:, P * j:P * j + P], ident[:, :])
                i.then_inc(vt_done.sem, 1)

            def qkv(l, p, j):
                if p == 0:
                    if j == 1:
                        pe.wait_ge(gelu_ready.sem, gelu_ready.at(l, KD - 1))
                    else:
                        pe.wait_ge(conv.sem, conv.at(l, 3 * (KD - 1 + j // 2)))
                else:
                    pe.wait_ge((vt_ready, ql, kl)[j].sem, (vt_ready, ql, kl)[j].at(l, p + (0 if j == 0 else 1)))
                unit(l, U_QKV + 3 * p + j, bank[QKV_BANK(p, j)][:, :], h_hi, h_lo)

            pe.wait_ge(consts_v.sem, 10)
            sum_squares(0, -1, 0)
            with pe.Fori(0, DEPTH) as l:
                ffn(l, 0)
                after_norm(l, U_RG, 0)
                pe.wait_ge(wfl.sem, wfl.at(l, 1))
                for k in range(KD):
                    i = mm3(bank[7][0:HEADS, :], wf_hi[:, k, :], wf_lo[:, k, :], h_hi[:, k, :], h_lo[:, k, :], k == 0,
                            k == KD - 1)
                i.then_inc(foxf_done.sem, 1)
                gates(l, 0)
                gates(l, 1)
                for c in range(2, KD):
                    pe.wait_ge(conv.sem, conv.at(l, 3 * (c - 1)))
                    unit(l, U_RG + 2 * c, bank[2 * (c % 2)][:, :], h_hi, h_lo)
                    pe.wait_ge(gelu_ready.sem, gelu_ready.at(l, c - 1))
                    unit(l, U_RG + 2 * c + 1, bank[2 * (c % 2) + 1][:, :], h_hi, h_lo)
                    if c % 2:
                        gates(l, c - 1)
                        gates(l, c)
                qkv(l, 0, 0)
                qkv(l, 0, 1)
                qkv(l, 0, 2)
                for p in range(PAIRS):
                    nxt = p + 1 < PAIRS
                    middle = suffix if p < 4 else turn
                    scores(l, p, 0)
                    scores(l, p, 1)
                    turn_v(l, p)
                    if nxt:
                        qkv(l, p + 1, 0)
                    else:
                        unit(l, U_MERGE, bank[0][:, :], h_hi, h_lo)
                    middle(l, p, 0)
                    middle(l, p, 1)
                    if nxt:
                        qkv(l, p + 1, 1)
                    values(l, p, 0)
                    values(l, p, 1)
                    if nxt:
                        qkv(l, p + 1, 2)
                pe.wait_ge(pl.sem, pl.at(l, 3 * HEADS))
                for n in range(KD):
                    u = U_MERGE + 5 * n
                    for g in range(3):
                        if n:
                            pe.wait_ge(sg_ready.sem, sg_ready.at(l, 3 * n - 2 + g))
                        if n or g:
                            unit(l, u + g, bank[g][:, :], h_hi, h_lo)
                    if n == 0:
                        pe.wait_ge(yal.sem, yal.at(l, KD))
                    if n:
                        pe.wait_ge(mx_step.sem, mx_step.at(l, 5 * n))
                    unit(l, u + 3, bank[3][:, :], ya_hi, ya_lo)
                    if n == 0:
                        pe.wait_ge(ybl.sem, ybl.at(l, PAIRS))
                    s = (u + 4) % RING
                    pe.wait_ge(unit_lo.sem, unit_lo.at(l, u + 5))
                    for j in range(KD):
                        i = mm3(bank[4 + j // 4][:, :], w_hi[s][:, j, :], w_lo[s][:, j, :], yb_hi[:, j, :],
                                yb_lo[:, j, :], j % 4 == 0, j % 4 == 3)
                    i.then_inc(unit_done.sem, 1)
                pe.wait_ge(sg_ready.sem, sg_ready.at(l, 3 * KD))
                pair(l, U_WO, WO_BANK(0), WO_BANK(1), mx_hi, mx_lo, mxl)
                pe.wait_ge(mx_step.sem, mx_step.at(l, 5 * KD))
                for n in range(2, KD - 1):
                    if n >= 4:
                        pe.wait_ge(x_ready.sem, x_ready.at(l, 9 + n - 3))
                    unit(l, U_WO + n, bank[WO_BANK(n)][:, :], mx_hi, mx_lo)
                pe.wait_ge(x_ready.sem, x_ready.at(l, 9 + KD - 4))
                pe.wait_ge(unit_lo.sem, unit_lo.at(l, U_WO + KD))
                for h, b in ((0, WO_BANK(KD - 1)), (1, 4)):
                    sl = (U_WO + KD - 1) % RING
                    for k in range(KD):
                        i = mm3(bank[b][:, HALF[h]], w_hi[sl][:, k, :], w_lo[sl][:, k, :], mx_hi[:, k, HALF[h]],
                                mx_lo[:, k, HALF[h]], k == 0, k == KD - 1)
                    i.then_inc((half_done, unit_done)[h].sem, 1)
                sum_squares(l, 1, 0)
                ffn(l, 1)
            sum_squares(DEPTH, -1, 1)


ZB = [(4, 5, 6), (1, 2, 3)]


def QKV_BANK(p, j):
    return j if p == 0 else 0


def WO_BANK(n):
    return n % 4


def _layout(inputs):
    import numpy as np
    g = {k: np.asarray(v, dtype=v.dtype) for k, v in inputs.items()}

    def cols(w):
        k, n = w.shape
        return w.reshape(k // P, P, n // P, P).transpose(2, 1, 0, 3)

    units = np.zeros((DEPTH * UNITS + RAW, P, UB, P), np.float32)
    for l in range(DEPTH):
        o = l * UNITS

        def ffn(u, w1, w3, w2):
            units[u:u + 2 * KF:2] = cols(w1)
            units[u + 1:u + 2 * KF:2] = cols(w3)
            d = cols(w2).transpose(0, 2, 1, 3).reshape(-1, UB, P, P)
            units[u + 2 * KF:u + FFN_UNITS] = d.transpose(0, 2, 1, 3)
        ffn(o + U_FFN[0], g["ffn1_w1"][l], g["ffn1_w3"][l], g["ffn1_w2"][l])
        ffn(o + U_FFN[1], g["ffn2_w1"][l], g["ffn2_w3"][l], g["ffn2_w2"][l])
        win = g["w_in"][l]
        a = cols(win[:, 0:2 * D])
        units[o + U_RG:o + U_QKV:2] = a[0:KD]
        units[o + U_RG + 1:o + U_QKV:2] = a[KD:2 * KD]
        for b in range(2):
            qkv = cols(win[:, 2 * D + 1536 * b:2 * D + 1536 * (b + 1)])
            for j in range(3):
                u = o + U_QKV + 12 * b + j
                units[u:u + 12:3] = qkv[4 * j:4 * j + 4]
        mg = cols(win[:, 2 * D + 3072 + HEADS:])
        for j in range(3):
            units[o + U_MERGE + j:o + U_WO:5] = mg[8 * j:8 * j + 8]
        units[o + U_MERGE + 3:o + U_WO:5] = cols(g["w_rg"][l])
        units[o + U_MERGE + 4:o + U_WO:5, :, 0:4] = cols(g["w_sb"][l])
        units[o + U_MERGE + 4:o + U_WO:5, :, 4:8] = cols(g["w_fox"][l])
        units[o + U_WO:o + U_FFN[1]] = cols(g["w_o"][l])

    def rows(w):
        return w.T.reshape(-1, P, w.shape[0])
    ada_w = np.concatenate([rows(g["ada_w"][l]) for l in range(DEPTH)] + [rows(g["final_ada_w"])])

    vecs = np.zeros((DEPTH + 1, P, NV), np.float32)

    def put(l, c, v):
        v = v.reshape(-1, P).T
        vecs[l, :, c:c + v.shape[1]] = v
    for l in range(DEPTH):
        for c, name in ((V_NORM1, "ffn1_norm"), (V_NORM2, "mix_norm"), (V_NORM3, "ffn2_norm"), (V_ADAB, "ada_b"),
                        (V_CONVW, "conv_w"), (V_CONVB, "conv_b"), (V_BA, "rg_ba"), (V_BX, "rg_bx"),
                        (V_LAM, "rg_lam"), (V_MERGEB, "merge_b")):
            put(l, c, g[name][l])
        vecs[l, 0:HEADS, V_FOXB] = g["fox_bf"][l]
    put(DEPTH, V_NORM1, g["final_norm"])
    put(DEPTH, V_ADAB, g["final_ada_b"])

    f0 = 2 * D + 3072
    wf = np.stack([g["w_in"][l][:, f0:f0 + HEADS].reshape(KD, P, HEADS).transpose(1, 0, 2) for l in range(DEPTH)])
    wab = np.zeros((DEPTH, P, KD, 2, P), np.float32)
    for j, name in enumerate(("rg_wa", "rg_wx")):
        w = g[name].reshape(DEPTH, KD, 2, HD, HD)
        for b in range(2):
            wab[:, b * HD:(b + 1) * HD, :, j, b * HD:(b + 1) * HD] = w[:, :, b].transpose(0, 2, 1, 3)
    return {
        "w_units": units, "ada_w": ada_w, "vecs": vecs, "wf": wf, "wab": wab,
        "c_rows": np.ascontiguousarray(np.broadcast_to(g["c"], (P, D))),
        "x_in": np.ascontiguousarray(g["x"][0].T).reshape(KD, P, T),
    }


def kernel(**inputs):
    import numpy as np
    import concourse.bacc as bacc
    from concourse.bass_utils import run_bass_kernel_spmd

    nc = bacc.Bacc("TRN2", target_bir_lowering=False, num_devices=1)
    arrays = {k: np.ascontiguousarray(v) for k, v in _layout(inputs).items()}
    args = {k: nc.dram_tensor(k, v.shape, mybir.dt.from_np(v.dtype), kind="ExternalInput").ap()
            for k, v in arrays.items()}
    y = nc.dram_tensor("y", (KD, P, T), F32, kind="ExternalOutput").ap()
    trunk(nc, out=y, **args)
    r = run_bass_kernel_spmd(nc, [arrays], core_ids=[0])
    return np.ascontiguousarray(r.results[0]["y"].reshape(D, T).T).reshape(1, T, D)
```
